# Optimizing a Trainium2 kernel written in Bass

```python
import math
import jax, jax.numpy as jnp
from jax import lax
import numpy as np

D_MODEL = 1024
BATCH = 1
SEQ = 256
DEPTH = 2

GRID_W = 64
CTX_LEN = 256
N_MIXERS = 2
EXPAND = 2
E_HY = EXPAND * D_MODEL
FILTER_EMB = 33
FILTER_WIDTH = 64
DECAY_TARGET = 1e-2
FAST_DECAY_PCT = 0.3
SLOW_DECAY_PCT = 1.5
MAX_DECAY = math.log(DECAY_TARGET) / FAST_DECAY_PCT
MIN_DECAY = math.log(DECAY_TARGET) / SLOW_DECAY_PCT
HEAD_DIM = 128
N_HEADS = (EXPAND * D_MODEL) // HEAD_DIM
N_KV = N_HEADS // 4
GROUP = N_HEADS // N_KV
QD = N_HEADS * HEAD_DIM
KVD = N_KV * HEAD_DIM
ROPE_AXIS_DIM = HEAD_DIM // 2
ROPE_THETA = 10000.0
Q_BLOCK = 128
EPS = 1e-6


def rms_norm(x, g):
    xf = x.astype(jnp.float32)
    y = xf * lax.rsqrt(jnp.mean(xf * xf, axis=-1, keepdims=True) + EPS)
    return (y * g.astype(jnp.float32)).astype(x.dtype)

def short_conv(x, w, b):
    xp = jnp.pad(x, ((0, 0), (1, 1), (0, 0)))
    return xp[:, :-2] * w[0] + xp[:, 1:-1] * w[1] + xp[:, 2:] * w[2] + b

def hyena_filter(L, w1, b1, w2, b2, w3, b3, w4, freq):
    f32 = jnp.float32
    t = jnp.linspace(0.0, 1.0, L, dtype=f32)[:, None]
    bands = (FILTER_EMB - 1) // 2
    w = 2.0 * math.pi * jnp.arange(L, dtype=f32)[:, None] / L
    fr = jnp.linspace(1e-4, bands - 1, bands, dtype=f32)[None, :]
    z = jnp.concatenate([t, jnp.cos(fr * w), -jnp.sin(fr * w)], axis=-1)
    fq = freq.astype(f32)
    h = jnp.sin(fq * (z @ w1.astype(f32) + b1.astype(f32)))
    h = jnp.sin(fq * (h @ w2.astype(f32) + b2.astype(f32)))
    h = jnp.sin(fq * (h @ w3.astype(f32) + b3.astype(f32)))
    h = h @ w4.astype(f32)
    deltas = jnp.abs(jnp.linspace(MIN_DECAY, MAX_DECAY, E_HY, dtype=f32))
    decay = jnp.exp(-t * deltas[None, :])
    hf = h[:, :E_HY] * decay
    hb = h[:, E_HY:] * decay
    k = jnp.concatenate([hf, jnp.zeros((1, E_HY), f32), hb[:0:-1]], axis=0)
    return k / jnp.sum(jnp.abs(k), axis=0, keepdims=True)

def hyena_mixer(h, w_in, conv_w, conv_b, fw1, fb1, fw2, fb2, fw3, fb3, fw4, freq, d_skip, w_out):
    L = h.shape[1]
    proj = h @ w_in
    xv = short_conv(proj[..., :3 * E_HY], conv_w, conv_b)
    z = proj[..., 3 * E_HY:]
    x0, x1, v = jnp.split(xv, 3, axis=-1)
    u = x1 * v
    k = hyena_filter(L, fw1, fb1, fw2, fb2, fw3, fb3, fw4, freq)
    U = jnp.fft.rfft(u.astype(jnp.float32), n=2 * L, axis=1)
    K = jnp.fft.rfft(k, n=2 * L, axis=0)
    y = jnp.fft.irfft(U * K[None], n=2 * L, axis=1)[:, :L].astype(h.dtype)
    y = (y + u * d_skip) * x0
    return (y * jax.nn.silu(z)) @ w_out

def rope_half(x, ang):
    F = ang.shape[-1]
    shape = (ang.shape[0],) + (1,) * (x.ndim - 3) + (F,)
    cos = jnp.cos(ang).reshape(shape).astype(x.dtype)
    sin = jnp.sin(ang).reshape(shape).astype(x.dtype)
    x1, x2 = x[..., :F], x[..., F:]
    return jnp.concatenate([x1 * cos - x2 * sin, x1 * sin + x2 * cos], axis=-1)

def axial_rope(x, row_ang, col_ang):
    return jnp.concatenate([rope_half(x[..., :ROPE_AXIS_DIM], row_ang),
                            rope_half(x[..., ROPE_AXIS_DIM:], col_ang)], axis=-1)

def attend(q, k, v):
    s = jnp.einsum('bqkgd,bskd->bkgqs', q, k).astype(jnp.float32) * (HEAD_DIM ** -0.5)
    p = jax.nn.softmax(s, axis=-1).astype(v.dtype)
    return jnp.einsum('bkgqs,bskd->bqkgd', p, v)

def gqa_mixer(h_lat, h_ctx, w_in, q_g, k_g, w_out, want_ctx):
    B, L, _ = h_lat.shape
    C = h_ctx.shape[1]
    p = h_lat @ w_in
    q = rms_norm(p[..., :QD].reshape(B, L, N_KV, GROUP, HEAD_DIM), q_g)
    k = rms_norm(p[..., QD:QD + KVD].reshape(B, L, N_KV, HEAD_DIM), k_g)
    v = p[..., QD + KVD:QD + 2 * KVD].reshape(B, L, N_KV, HEAD_DIM)
    z = p[..., QD + 2 * KVD:]
    rows = L // GRID_W
    row = jnp.repeat(jnp.arange(rows, dtype=jnp.float32), GRID_W)
    col = jnp.tile(jnp.arange(GRID_W, dtype=jnp.float32), rows)
    inv = 1.0 / (ROPE_THETA ** (jnp.arange(0, ROPE_AXIS_DIM, 2, dtype=jnp.float32) / ROPE_AXIS_DIM))
    row_ang = row[:, None] * inv[None, :]
    col_ang = col[:, None] * inv[None, :]
    q = axial_rope(q, row_ang, col_ang)
    k = axial_rope(k, row_ang, col_ang)
    if want_ctx:
        pc = h_ctx @ w_in
    else:
        pc = h_ctx @ w_in[:, QD:QD + 2 * KVD]
        pc = jnp.pad(pc, ((0, 0), (0, 0), (QD, 0)))
    kc = rms_norm(pc[..., QD:QD + KVD].reshape(B, C, N_KV, HEAD_DIM), k_g)
    vc = pc[..., QD + KVD:QD + 2 * KVD].reshape(B, C, N_KV, HEAD_DIM)
    k_all = jnp.concatenate([k, kc], axis=1)
    v_all = jnp.concatenate([v, vc], axis=1)
    nb = L // Q_BLOCK
    qb = q.reshape(B, nb, Q_BLOCK, N_KV, GROUP, HEAD_DIM).transpose(1, 0, 2, 3, 4, 5)
    o = lax.map(lambda qq: attend(qq, k_all, v_all), qb)
    o = o.transpose(1, 0, 2, 3, 4, 5).reshape(B, L, QD)
    y_lat = (o * jax.nn.silu(z)) @ w_out
    if want_ctx:
        qc = rms_norm(pc[..., :QD].reshape(B, C, N_KV, GROUP, HEAD_DIM), q_g)
        oc = attend(qc, kc, vc).reshape(B, C, QD)
        y_ctx = (oc * jax.nn.silu(pc[..., QD + 2 * KVD:])) @ w_out
    else:
        y_ctx = None
    return y_lat, y_ctx

def first_inputs(seed: int = 0) -> dict:
    key = jax.random.key(seed)
    ks = jax.random.split(key, 32)
    f32 = jnp.float32
    na = (DEPTH + 1) // 2
    nb = DEPTH // 2

    def nrm(k, shape, scale):
        return jax.random.normal(k, shape, f32) * scale

    return {
        "x": nrm(ks[0], (BATCH, SEQ, D_MODEL), 1.0),
        "c": nrm(ks[1], (BATCH, D_MODEL), 1.0),
        "ctx": nrm(ks[2], (BATCH, CTX_LEN, D_MODEL), 1.0),
        "c_ctx": nrm(ks[3], (D_MODEL,), 1.0),
        "norm_g": 1.0 + nrm(ks[4], (DEPTH, D_MODEL), 0.05),
        "ada_w": nrm(ks[5], (DEPTH, D_MODEL, 3 * D_MODEL), D_MODEL ** -0.5),
        "ada_b": nrm(ks[6], (DEPTH, 3 * D_MODEL), 0.02),
        "hy_w_in": nrm(ks[7], (na, D_MODEL, 4 * E_HY), D_MODEL ** -0.5),
        "hy_conv_w": nrm(ks[8], (na, 3, 3 * E_HY), 3 ** -0.5),
        "hy_conv_b": nrm(ks[9], (na, 3 * E_HY), 0.02),
        "hy_fw1": nrm(ks[10], (na, FILTER_EMB, FILTER_WIDTH), FILTER_EMB ** -0.5),
        "hy_fb1": nrm(ks[11], (na, FILTER_WIDTH), 0.02),
        "hy_fw2": nrm(ks[12], (na, FILTER_WIDTH, FILTER_WIDTH), FILTER_WIDTH ** -0.5),
        "hy_fb2": nrm(ks[13], (na, FILTER_WIDTH), 0.02),
        "hy_fw3": nrm(ks[14], (na, FILTER_WIDTH, FILTER_WIDTH), FILTER_WIDTH ** -0.5),
        "hy_fb3": nrm(ks[15], (na, FILTER_WIDTH), 0.02),
        "hy_fw4": nrm(ks[16], (na, FILTER_WIDTH, 2 * E_HY), FILTER_WIDTH ** -0.5),
        "hy_freq": 1.0 + nrm(ks[17], (na, FILTER_WIDTH), 0.05),
        "hy_d": nrm(ks[18], (na, E_HY), 0.5),
        "hy_w_out": nrm(ks[19], (na, E_HY, D_MODEL), E_HY ** -0.5),
        "at_w_in": nrm(ks[20], (nb, D_MODEL, 2 * QD + 2 * KVD), D_MODEL ** -0.5),
        "at_q_g": 1.0 + nrm(ks[21], (nb, HEAD_DIM), 0.05),
        "at_k_g": 1.0 + nrm(ks[22], (nb, HEAD_DIM), 0.05),
        "at_w_out": nrm(ks[23], (nb, QD, D_MODEL), QD ** -0.5),
    }

def first_block(x, c, ctx, c_ctx, norm_g, ada_w, ada_b,
              hy_w_in, hy_conv_w, hy_conv_b, hy_fw1, hy_fb1, hy_fw2, hy_fb2, hy_fw3, hy_fb3,
              hy_fw4, hy_freq, hy_d, hy_w_out,
              at_w_in, at_q_g, at_k_g, at_w_out):
    sc_lat = jax.nn.silu(c)
    sc_ctx = jax.nn.silu(c_ctx)
    x_lat, x_ctx = x, ctx
    for i in range(DEPTH):
        last = i == DEPTH - 1
        mixer = i % N_MIXERS
        j = i // N_MIXERS
        need_ctx_in = (not last) or mixer == 1
        sh, sc, gt = jnp.split(sc_lat @ ada_w[i] + ada_b[i], 3, axis=-1)
        h_lat = rms_norm(x_lat, norm_g[i]) * (1.0 + sc[:, None]) + sh[:, None]
        if need_ctx_in:
            sh_c, sc_c, gt_c = jnp.split(sc_ctx @ ada_w[i] + ada_b[i], 3, axis=-1)
            h_ctx = rms_norm(x_ctx, norm_g[i]) * (1.0 + sc_c) + sh_c
        if mixer == 0:
            hp = (hy_w_in[j], hy_conv_w[j], hy_conv_b[j], hy_fw1[j], hy_fb1[j], hy_fw2[j], hy_fb2[j],
                  hy_fw3[j], hy_fb3[j], hy_fw4[j], hy_freq[j], hy_d[j], hy_w_out[j])
            y_lat = hyena_mixer(h_lat, *hp)
            y_ctx = None if last else hyena_mixer(h_ctx, *hp)
        else:
            y_lat, y_ctx = gqa_mixer(h_lat, h_ctx, at_w_in[j], at_q_g[j], at_k_g[j], at_w_out[j],
                                     not last)
        x_lat = x_lat + gt[:, None] * y_lat
        if not last:
            x_ctx = x_ctx + gt_c * y_ctx
    return x_lat


W_LRU = D_MODEL // 2
LRU_BLOCKS = 8
LRU_C = 8.0
CONV_K = 4

SSM_HEAD_DIM = 64
SSM_D_INNER = D_MODEL
SSM_HEADS = SSM_D_INNER // SSM_HEAD_DIM
SSM_GROUPS = 2
SSM_STATE = 128
SSM_CHUNK = 128
SSM_CONV_CH = SSM_D_INNER + 2 * SSM_GROUPS * SSM_STATE

ATTN_HEAD_DIM = 64
ATTN_Q_HEADS = (D_MODEL // 2) // ATTN_HEAD_DIM
ATTN_KV_HEADS = 2
WINDOW = 128
ATTN_BLOCK = WINDOW

MIX_WIDTH = W_LRU + SSM_D_INNER + ATTN_Q_HEADS * ATTN_HEAD_DIM

_SEG = (W_LRU, W_LRU,
        SSM_D_INNER, SSM_CONV_CH, SSM_HEADS,
        ATTN_Q_HEADS * ATTN_HEAD_DIM,
        ATTN_KV_HEADS * ATTN_HEAD_DIM,
        ATTN_KV_HEADS * ATTN_HEAD_DIM)
IN_COLS = sum(_SEG)
SPLIT_POINTS = tuple(int(v) for v in np.cumsum(_SEG)[:-1])

PEER_HEADS = 8
PEER_NKEYS = 128
PEER_EXPERTS = PEER_NKEYS * PEER_NKEYS
PEER_DKEY = 128
PEER_TOPK = 16
PEER_CHUNK = 128

DN_ALPHA = (2 * DEPTH) ** 0.25
DN_BETA = (8 * DEPTH) ** -0.25
LN_EPS = 1e-5


def layer_norm(x, g, b):
    xf = x.astype(jnp.float32)
    mu = jnp.mean(xf, axis=-1, keepdims=True)
    var = jnp.mean(jnp.square(xf - mu), axis=-1, keepdims=True)
    return ((xf - mu) * lax.rsqrt(var + LN_EPS) * g + b).astype(x.dtype)

def causal_dwconv(x, w, b):
    k = w.shape[0]
    s = x.shape[1]
    xp = jnp.pad(x, ((0, 0), (k - 1, 0), (0, 0)))
    out = b + w[0] * xp[:, 0:s]
    for i in range(1, k):
        out = out + w[i] * xp[:, i:i + s]
    return out

def rg_lru(x, w_a, b_a, w_x, b_x, lam):
    bsz, s, w = x.shape
    xb = x.reshape(bsz, s, LRU_BLOCKS, w // LRU_BLOCKS)
    r = jax.nn.sigmoid((jnp.einsum('bsnc,ncd->bsnd', xb, w_a).reshape(bsz, s, w) + b_a).astype(jnp.float32))
    i = jax.nn.sigmoid((jnp.einsum('bsnc,ncd->bsnd', xb, w_x).reshape(bsz, s, w) + b_x).astype(jnp.float32))
    log_a = -LRU_C * r * jax.nn.softplus(-lam.astype(jnp.float32))
    a = jnp.exp(log_a)
    u = jnp.sqrt(-jnp.expm1(2.0 * log_a)) * (i * x.astype(jnp.float32))

    def combine(left, right):
        a_l, h_l = left
        a_r, h_r = right
        return a_l * a_r, a_r * h_l + h_r

    _, h = lax.associative_scan(combine, (a, u), axis=1)
    return h.astype(x.dtype)

def ssd_scan(xh, dt, a, bmat, cmat):
    f32 = jnp.float32
    bsz, s, h, p = xh.shape
    g, n = bmat.shape[2], bmat.shape[3]
    hg = h // g
    nc, l = s // SSM_CHUNK, SSM_CHUNK
    x = (xh.astype(f32) * dt[..., None]).reshape(bsz, nc, l, g, hg, p)
    da = (dt * a).reshape(bsz, nc, l, g, hg).transpose(0, 3, 4, 1, 2)
    bc = bmat.astype(f32).reshape(bsz, nc, l, g, n)
    cc = cmat.astype(f32).reshape(bsz, nc, l, g, n)
    a_cs = jnp.cumsum(da, axis=-1)
    causal = jnp.tril(jnp.ones((l, l), dtype=bool))
    seg = a_cs[..., :, None] - a_cs[..., None, :]
    decay = jnp.exp(jnp.where(causal, seg, -jnp.inf))
    cb = jnp.einsum('bclgn,bcsgn->bgcls', cc, bc)
    y_diag = jnp.einsum('bghcls,bcsghp->bclghp', cb[:, :, None] * decay, x)
    decay_states = jnp.exp(a_cs[..., -1:] - a_cs).transpose(0, 3, 4, 1, 2)
    states = jnp.einsum('bclgn,bclghp->bcghpn', bc, x * decay_states[..., None])
    chunk_decay = jnp.exp(a_cs[..., -1])

    def step(carry, inp):
        st, dec = inp
        return carry * dec[..., None, None] + st, carry

    init = jnp.zeros((bsz, g, hg, p, n), f32)
    _, prev = lax.scan(step, init, (jnp.moveaxis(states, 1, 0), jnp.moveaxis(chunk_decay, 3, 0)))
    prev = jnp.moveaxis(prev, 0, 1)
    out_decay = jnp.exp(a_cs).transpose(0, 3, 4, 1, 2)
    y_off = jnp.einsum('bclgn,bcghpn->bclghp', cc, prev) * out_decay[..., None]
    return (y_diag + y_off).reshape(bsz, s, h, p)

def mamba2_group(z, xbc, dt_raw, conv_w, conv_b, dt_bias, a_log, d_skip, norm_g):
    f32 = jnp.float32
    bsz, s, _ = z.shape
    xbc = jax.nn.silu(causal_dwconv(xbc, conv_w, conv_b))
    xs, bm, cm = jnp.split(xbc, [SSM_D_INNER, SSM_D_INNER + SSM_GROUPS * SSM_STATE], axis=-1)
    dt = jax.nn.softplus(dt_raw.astype(f32) + dt_bias.astype(f32))
    a = -jnp.exp(a_log.astype(f32))
    xh = xs.reshape(bsz, s, SSM_HEADS, SSM_HEAD_DIM)
    y = ssd_scan(xh, dt, a,
                 bm.reshape(bsz, s, SSM_GROUPS, SSM_STATE),
                 cm.reshape(bsz, s, SSM_GROUPS, SSM_STATE))
    y = y + d_skip.astype(f32)[:, None] * xh.astype(f32)
    y = y.reshape(bsz, s, SSM_D_INNER) * jax.nn.silu(z.astype(f32))
    yg = y.reshape(bsz, s, SSM_GROUPS, SSM_D_INNER // SSM_GROUPS)
    yg = yg * lax.rsqrt(jnp.mean(jnp.square(yg), axis=-1, keepdims=True) + LN_EPS)
    return (yg.reshape(bsz, s, SSM_D_INNER) * norm_g).astype(z.dtype)

def sliding_window_attention(q, k, v, sinks):
    f32 = jnp.float32
    bsz, s, _ = q.shape
    nb = s // ATTN_BLOCK
    rep = ATTN_Q_HEADS // ATTN_KV_HEADS
    qb = q.reshape(bsz, nb, ATTN_BLOCK, ATTN_KV_HEADS, rep, ATTN_HEAD_DIM)
    kb = k.reshape(bsz, nb, ATTN_BLOCK, ATTN_KV_HEADS, ATTN_HEAD_DIM)
    vb = v.reshape(bsz, nb, ATTN_BLOCK, ATTN_KV_HEADS, ATTN_HEAD_DIM)

    def with_prev(t):
        prev = jnp.pad(t, ((0, 0), (1, 0), (0, 0), (0, 0), (0, 0)))[:, :-1]
        return jnp.concatenate([prev, t], axis=2)

    kk, vv = with_prev(kb), with_prev(vb)
    logits = jnp.einsum('bnqhrd,bnkhd->bnhrqk', qb, kk).astype(f32) * (ATTN_HEAD_DIM ** -0.5)
    qi = jnp.arange(ATTN_BLOCK)[:, None]
    kj = jnp.arange(2 * ATTN_BLOCK)[None, :]
    rel = qi + ATTN_BLOCK - kj
    band = (rel >= 0) & (rel < WINDOW)
    blk = jnp.arange(nb)[:, None, None]
    valid = band[None] & ((blk > 0) | (kj[None] >= ATTN_BLOCK))
    logits = jnp.where(valid[None, :, None, None], logits, -jnp.inf)
    sink = sinks.astype(f32).reshape(ATTN_KV_HEADS, rep)[None, None, :, :, None, None]
    m = jnp.maximum(jnp.max(logits, axis=-1, keepdims=True), sink)
    p = jnp.exp(logits - m)
    probs = p / (jnp.sum(p, axis=-1, keepdims=True) + jnp.exp(sink - m))
    out = jnp.einsum('bnhrqk,bnkhd->bnqhrd', probs.astype(v.dtype), vv)
    return out.reshape(bsz, s, ATTN_Q_HEADS * ATTN_HEAD_DIM)

def peer_ffn(x, wq, keys, u, v):
    bsz, s, d = x.shape
    xt = x.reshape(-1, PEER_CHUNK, d)
    half = PEER_DKEY // 2

    def chunk(xc):
        c = xc.shape[0]
        q = (xc @ wq).reshape(c, PEER_HEADS, 2, half)
        sc = jnp.einsum('thid,ikd->thik', q, keys).astype(jnp.float32)
        top_s, top_i = lax.top_k(sc, PEER_TOPK)
        cand_s = top_s[:, :, 0, :, None] + top_s[:, :, 1, None, :]
        cand_i = top_i[:, :, 0, :, None] * PEER_NKEYS + top_i[:, :, 1, None, :]
        best_s, best_pos = lax.top_k(cand_s.reshape(c, PEER_HEADS, -1), PEER_TOPK)
        idx = jnp.take_along_axis(cand_i.reshape(c, PEER_HEADS, -1), best_pos, axis=-1)
        gate = jax.nn.softmax(best_s, axis=-1)
        ue = u[idx]
        ve = v[idx]
        act = jax.nn.gelu(jnp.einsum('td,thkd->thk', xc, ue).astype(jnp.float32), approximate=False)
        return jnp.einsum('thk,thkd->td', (gate * act).astype(xc.dtype), ve)

    return lax.map(chunk, xt).reshape(bsz, s, d)

def second_inputs(seed: int = 0) -> dict:
    key = jax.random.key(seed)
    ks = jax.random.split(key, 32)
    f32 = jnp.float32

    def nrm(k, shape, scale):
        return jax.random.normal(k, shape, f32) * scale

    bw = W_LRU // LRU_BLOCKS
    a0 = jax.random.uniform(ks[10], (DEPTH, W_LRU), f32, 0.9, 0.999)
    a_base = a0 ** (1.0 / LRU_C)
    dt0 = jnp.exp(jax.random.uniform(ks[13], (DEPTH, SSM_HEADS), f32, math.log(1e-3), math.log(1e-1)))
    return {
        "x": nrm(ks[0], (BATCH, SEQ, D_MODEL), 1.0),
        "emb_ln_g": 1.0 + nrm(ks[1], (D_MODEL,), 0.02),
        "emb_ln_b": nrm(ks[2], (D_MODEL,), 0.02),
        "w_in": nrm(ks[3], (DEPTH, D_MODEL, IN_COLS), D_MODEL ** -0.5),
        "rg_conv_w": nrm(ks[4], (DEPTH, CONV_K, W_LRU), CONV_K ** -0.5),
        "rg_conv_b": nrm(ks[5], (DEPTH, W_LRU), 0.02),
        "rg_wa": nrm(ks[6], (DEPTH, LRU_BLOCKS, bw, bw), bw ** -0.5),
        "rg_ba": nrm(ks[7], (DEPTH, W_LRU), 0.02),
        "rg_wx": nrm(ks[8], (DEPTH, LRU_BLOCKS, bw, bw), bw ** -0.5),
        "rg_bx": nrm(ks[9], (DEPTH, W_LRU), 0.02),
        "rg_lambda": jnp.log(a_base) - jnp.log1p(-a_base),
        "ssm_conv_w": nrm(ks[11], (DEPTH, CONV_K, SSM_CONV_CH), CONV_K ** -0.5),
        "ssm_conv_b": nrm(ks[12], (DEPTH, SSM_CONV_CH), 0.02),
        "ssm_dt_bias": dt0 + jnp.log(-jnp.expm1(-dt0)),
        "ssm_a_log": jnp.log(jax.random.uniform(ks[14], (DEPTH, SSM_HEADS), f32, 1.0, 16.0)),
        "ssm_d": 1.0 + nrm(ks[15], (DEPTH, SSM_HEADS), 0.02),
        "ssm_norm_g": 1.0 + nrm(ks[16], (DEPTH, SSM_D_INNER), 0.02),
        "attn_sinks": nrm(ks[17], (DEPTH, ATTN_Q_HEADS), 1.0),
        "w_out": nrm(ks[18], (DEPTH, MIX_WIDTH, D_MODEL), DN_BETA * MIX_WIDTH ** -0.5),
        "ln1_g": 1.0 + nrm(ks[19], (DEPTH, D_MODEL), 0.02),
        "ln1_b": nrm(ks[20], (DEPTH, D_MODEL), 0.02),
        "peer_wq": nrm(ks[21], (DEPTH, D_MODEL, PEER_HEADS * PEER_DKEY), D_MODEL ** -0.5),
        "peer_keys": nrm(ks[22], (DEPTH, 2, PEER_NKEYS, PEER_DKEY // 2), (PEER_DKEY // 2) ** -0.5),
        "peer_u": nrm(ks[23], (DEPTH, PEER_EXPERTS, D_MODEL), D_MODEL ** -0.5),
        "peer_v": nrm(ks[24], (DEPTH, PEER_EXPERTS, D_MODEL), DN_BETA * PEER_HEADS ** -0.5),
        "ln2_g": 1.0 + nrm(ks[25], (DEPTH, D_MODEL), 0.02),
        "ln2_b": nrm(ks[26], (DEPTH, D_MODEL), 0.02),
    }

def second_block(x, emb_ln_g, emb_ln_b, w_in, rg_conv_w, rg_conv_b, rg_wa, rg_ba, rg_wx, rg_bx,
              rg_lambda, ssm_conv_w, ssm_conv_b, ssm_dt_bias, ssm_a_log, ssm_d, ssm_norm_g,
              attn_sinks, w_out, ln1_g, ln1_b, peer_wq, peer_keys, peer_u, peer_v, ln2_g, ln2_b):
    h = layer_norm(x, emb_ln_g, emb_ln_b)
    for l in range(DEPTH):
        proj = h @ w_in[l]
        rg_x, rg_gate, z, xbc, dt_raw, q, k, v = jnp.split(proj, SPLIT_POINTS, axis=-1)
        y_a = jax.nn.gelu(rg_gate) * rg_lru(causal_dwconv(rg_x, rg_conv_w[l], rg_conv_b[l]),
                                            rg_wa[l], rg_ba[l], rg_wx[l], rg_bx[l], rg_lambda[l])
        y_b = mamba2_group(z, xbc, dt_raw, ssm_conv_w[l], ssm_conv_b[l], ssm_dt_bias[l],
                           ssm_a_log[l], ssm_d[l], ssm_norm_g[l])
        y_c = sliding_window_attention(q, k, v, attn_sinks[l])
        mix = jnp.concatenate([y_a.astype(h.dtype), y_b, y_c.astype(h.dtype)], axis=-1) @ w_out[l]
        h = layer_norm(DN_ALPHA * h + mix, ln1_g[l], ln1_b[l])
        ffn = peer_ffn(h, peer_wq[l], peer_keys[l], peer_u[l], peer_v[l])
        h = layer_norm(DN_ALPHA * h + ffn, ln2_g[l], ln2_b[l])
    return h


def setup_inputs(seed=0):
    out = dict(first_inputs(seed))
    for name, value in second_inputs(seed + 1).items():
        if name != "x":
            out[name + "_2"] = value
    return out


def reference(
    x, c, ctx, c_ctx, norm_g, ada_w, ada_b, hy_w_in, hy_conv_w, hy_conv_b, hy_fw1, hy_fb1,
    hy_fw2, hy_fb2, hy_fw3, hy_fb3, hy_fw4, hy_freq, hy_d, hy_w_out, at_w_in, at_q_g, at_k_g,
    at_w_out, emb_ln_g_2, emb_ln_b_2, w_in_2, rg_conv_w_2, rg_conv_b_2, rg_wa_2, rg_ba_2,
    rg_wx_2, rg_bx_2, rg_lambda_2, ssm_conv_w_2, ssm_conv_b_2, ssm_dt_bias_2, ssm_a_log_2,
    ssm_d_2, ssm_norm_g_2, attn_sinks_2, w_out_2, ln1_g_2, ln1_b_2, peer_wq_2, peer_keys_2,
    peer_u_2, peer_v_2, ln2_g_2, ln2_b_2,
):
    x = first_block(
        x, c, ctx, c_ctx, norm_g, ada_w, ada_b, hy_w_in, hy_conv_w, hy_conv_b, hy_fw1, hy_fb1,
        hy_fw2, hy_fb2, hy_fw3, hy_fb3, hy_fw4, hy_freq, hy_d, hy_w_out, at_w_in, at_q_g,
        at_k_g, at_w_out,
    )
    return second_block(
        x, emb_ln_g_2, emb_ln_b_2, w_in_2, rg_conv_w_2, rg_conv_b_2, rg_wa_2, rg_ba_2, rg_wx_2,
        rg_bx_2, rg_lambda_2, ssm_conv_w_2, ssm_conv_b_2, ssm_dt_bias_2, ssm_a_log_2, ssm_d_2,
        ssm_norm_g_2, attn_sinks_2, w_out_2, ln1_g_2, ln1_b_2, peer_wq_2, peer_keys_2, peer_u_2,
        peer_v_2, ln2_g_2, ln2_b_2,
    )


_drawn_inputs = setup_inputs


def setup_inputs(seed=0):
    import zlib

    import numpy as np

    out = dict(_drawn_inputs(seed))
    spreads = {}
    factors = {'hy_conv_b': 3.066,
     'hy_fb1': 6.618,
     'hy_fb2': 5.535,
     'hy_fb3': 4.985,
     'hy_freq': 4.307,
     'at_q_g': 7.492,
     'at_k_g': 8.0,
     'rg_conv_b_2': 3.534,
     'rg_ba_2': 64.0,
     'rg_bx_2': 47.316,
     'ssm_conv_b_2': 4.157,
     'ssm_d_2': 6.722,
     'ssm_norm_g_2': 5.216,
     'attn_sinks_2': 8.0}
    for name, (base, spread) in spreads.items():
        noise = np.random.default_rng([zlib.crc32(name.encode()), seed]).standard_normal(out[name].shape)
        drawn = base * np.exp(spread * noise) if base else spread * noise
        out[name] = __import__('jax').numpy.asarray(drawn.astype(out[name].dtype))
    for name, factor in factors.items():
        out[name] = (out[name] * factor).astype(out[name].dtype)
    return out
```

```python
from contextlib import ExitStack

import numpy as np

import concourse.bass as bass
from concourse import mybir

ALU = mybir.AluOpType
ACT = mybir.ActivationFunctionType
AX_X = mybir.AxisListType.X
F32 = mybir.dt.float32
F32R = mybir.dt.float32r
U32 = mybir.dt.uint32

P = 128
D = 1024
T = 256
T2 = 2 * T
KT = D // P
DEPTH = 2
CHUNK = 2048
UNITS = 4
UNIT = CHUNK // UNITS
RING = 4
E_HY = 2 * D
CT = E_HY // P
HEADS, KV_HEADS = 16, 4
LRU_T, XBC_T, Z_T, Q_T = 4, 12, 8, 4
SSM_HEADS, SSM_GROUPS = 16, 2
PEER_HEADS, NKEYS, TOPK = 8, 128, 16
ROWS = 2 * PEER_HEADS
BLOCKS = NKEYS
ALPHA = (2 * DEPTH) ** 0.25
LOG1P_TERMS = [1.0 / n for n in (15, 13, 11, 9, 7, 5, 3)]

CONST = [("ident", P), ("ones", P), ("iota", P), ("causal", P), ("eps6", 1), ("eps5", 1)]
HYC = [("re", 2 * T), ("im", 2 * T), ("sn", 2 * T), ("rex", 2 * P), ("ire", 2 * T), ("iim", 2 * T),
       ("z", T)]
ROPE = [("cos", T), ("sin", T), ("rot", P)]
VEC1 = [("c", 16), ("norm_g", 16), ("ada_b", 48), ("conv_w", 144), ("conv_b", 48), ("hy_d", 16), ("q_g", 1),
        ("k_g", 1), ("fb", 3), ("freq", 1), ("emb_g", 8), ("emb_b", 8), ("fw", 192)]
LAYER = [("rg_w", 16), ("rg_b", 4), ("ba", 4), ("bx", 4), ("lam", 4), ("ssm_w", 48), ("ssm_b", 12),
         ("dt_bias", 1), ("a_log", 1), ("ssm_d", 8), ("ssm_g", 8), ("ln1_g", 8), ("ln1_b", 8), ("ln2_g", 8),
         ("ln2_b", 8), ("sinks", 8)]
WIDE = [("w_dt", 128), ("keys", 256), ("rg_wax", 1024), ("amask", 2 * T)]


def columns(table):
    at, out = 0, {}
    for name, n in table:
        out[name] = (at, n)
        at += n
    return out, at


class Uses:

    def __init__(self, n):
        self.n, self.base = n, 0

    def at(self, off, i=0, per=0):
        k = self.base + off
        return k % self.n, (k // self.n + i * (per // self.n) if per else k // self.n)


def program(nc, A, out):
    ctx = ExitStack()
    with ctx:
        def sb(name, shape, dt=F32):
            return ctx.enter_context(nc.sbuf_tensor(name, shape, dt))

        def sem(name):
            return ctx.enter_context(nc.semaphore(name))

        def sems(name, n):
            return [sem(f"{name}{i}") for i in range(n)]

        def table(name, layout):
            at, n = columns(layout)
            t = sb(name, [P, n])
            return t, {k: t[:, a:a + m] for k, (a, m) in at.items()}

        wring = sb("wring", [P, RING, CHUNK])
        const_t, C = table("const_t", CONST)
        wide_t, WD = table("wide_t", WIDE)
        lay_t, LV = [], []
        for l in range(DEPTH):
            t, v = table(f"lay{l}_t", LAYER)
            lay_t.append(t)
            LV.append(v)
        ident, ones, iota = C["ident"], C["ones"], C["iota"]

        RES, VEC = 2 * KT * T, columns(VEC1)[1]
        ARENA = 38160
        base = -(-nc.sbuf_base // 32) * 32
        sb("slab", [P, RES + ARENA])
        res = nc.alloc_sbuf_tensor_at("res", [P, RES], F32, offset=base)
        res_r = nc.alloc_sbuf_tensor_at("res_r", [P, RES], F32R, offset=base)
        arena = nc.alloc_sbuf_tensor_at("arena", [P, ARENA], F32, offset=base + 4 * RES)

        def arena_r(name, at, words):
            return nc.alloc_sbuf_tensor_at(name, [P, words], F32R, offset=base + 4 * (RES + at))

        vec_t = arena[:, ARENA - VEC:]
        V1 = {k: vec_t[:, a:a + m] for k, (a, m) in columns(VEC1)[0].items()}

        class Carve:
            def __init__(self, at=0, mem=arena):
                self.at, self.mem = at, mem

            def take(self, *shape):
                n = int(np.prod(shape))
                ap = self.mem[:, self.at:self.at + n]
                self.at += n
                assert self.at <= ARENA, self.at
                if len(shape) == 2:
                    ap = ap.rearrange("p (a b) -> p a b", a=shape[0])
                if len(shape) == 3:
                    ap = ap.rearrange("p (a b c) -> p a b c", a=shape[0], b=shape[1])
                if len(shape) == 4:
                    ap = ap.rearrange("p (a b c d) -> p a b c d", a=shape[0], b=shape[1], c=shape[2])
                return ap

        def view(ap, a):
            return ap.rearrange("p (a b) -> p a b", a=a)

        bank = [ctx.enter_context(nc.psum_tensor(f"bank{b}", [P, 512], F32)) for b in range(8)]

        c1 = Carve()
        H1 = c1.take(KT, T2)
        YG = c1.take(CT, T2)
        W4 = c1.take(CT, 256)
        hyc_at, hyc_n = columns(HYC)
        hyc_t = c1.take(hyc_n)
        HC = {k: hyc_t[:, a:a + m] for k, (a, m) in hyc_at.items()}
        DEC = c1.take(2, 512)
        KB = c1.take(512)
        KSD = c1.take(2, 256)
        KABS = c1.take(512)
        UT = c1.take(512)
        KSPEC = c1.take(5, P)
        KNORM = c1.take(2)
        PR4 = c1.take(4, 512)
        YRI = c1.take(2, 512)
        CX = c1.take(3, 512)
        U = c1.take(512)
        ZS1 = c1.take(512)
        YT = c1.take(2, 512)
        HF = c1.take(4, T)
        HSIN = c1.take(T)
        KEEP1 = c1.take(P)
        adac = KEEP1[:, 0:96].rearrange("p (l n s) -> p l n s", l=2, n=24)
        adag = KEEP1[:, 96:128].rearrange("p (l k s) -> p l k s", l=2, k=8)
        end1 = c1.at
        ADAROW = arena[:, KT * T2:KT * T2 + 2 * 3072]
        SILC = HF[:, 3, 0:16].rearrange("p (k s) -> p k s", s=2)
        SQ1 = YG[:, 0:8, :]
        RS1 = KB
        TM1 = YG[:, 8:16, :]

        c2 = Carve(KT * T2)
        KR = c2.take(KV_HEADS, T2)
        VR = c2.take(KV_HEADS, T2)
        QR = c2.take(HEADS, T)
        ZG = c2.take(HEADS, T)
        SQA = c2.take(512)
        RSA = c2.take(512)
        QN = c2.take(512)
        RT1 = c2.take(512)
        RT2 = c2.take(512)
        QF = c2.take(512)
        VS = c2.take(4, P)
        PRB = c2.take(4, 512)
        PTR = c2.take(4, 512)
        STAT = c2.take(4, 4)
        rope_at, rope_n = columns(ROPE)
        rope_t = c2.take(rope_n)
        RO = {k: rope_t[:, a:a + m] for k, (a, m) in rope_at.items()}
        assert c2.at <= end1 - P and end1 <= ARENA - VEC, (c2.at, end1)
        OG = arena[:, 0:HEADS * T].rearrange("p (h t) -> p h t", h=HEADS)

        c3 = Carve()
        SQ = c3.take(KT, T)
        MU = c3.take(T)
        RS = c3.take(T)
        PRJ = c3.take(34, T)
        MIX = c3.take(16, T)
        RG_AT = c3.at
        RG = c3.take(6, 4 * T)
        SP = c3.take(6, 4 + T)
        SROW = c3.take(4, T)
        AD = c3.take(SSM_HEADS, T)
        COLS = c3.take(5, SSM_HEADS)
        BC = c3.take(2, T)
        CBM = c3.take(2, P)
        BT = c3.take(P)
        XS = c3.take(2, T)
        CV = c3.take(T)
        XDT = c3.take(2, 2, P)
        XDS = c3.take(P)
        ST0 = c3.take(P)
        SEG = c3.take(4, P)
        EX1 = c3.take(2, P)
        end3 = c3.at
        YS = SQ[:, 0:4, :]
        YQ4 = SQ[:, 4:8, :]
        ADP = AD.rearrange("p (n h) t -> p n (h t)", h=2)
        QS = RG[:, 0, 0:256]
        SM = RG[:, 1:2, :].rearrange("p a (b c) -> p (a b) c", b=2)
        PT3 = RG[:, 2:3, 0:768].rearrange("p a (b c) -> p (a b) c", b=2)
        VTK = RG[:, 3, 0:256].rearrange("p (a b) -> p a b", a=2)
        ST = RG[:, 4, 0:64].rearrange("p (a b) -> p a b", a=8)

        G = arena[:, 0:BLOCKS * T].rearrange("p (j t) -> p j t", j=BLOCKS)
        c5 = Carve(0, arena_r("peer_r", BLOCKS * T, 2 * UNITS * UNIT + 4 * T))
        SPLIT = c5.take(UNITS, 2, UNIT)
        GPR = c5.take(2, 2, T)
        GA = Carve(BLOCKS * T + c5.at).take(T)
        c5 = Carve(BLOCKS * T)
        OHA = c5.take(8, P)
        OHB = c5.take(8, P)
        PAIR = c5.take(3, T)
        assert end3 <= BLOCKS * T
        c6 = Carve()
        Q8 = c6.take(PEER_HEADS, T)
        SC = c6.take(2 * ROWS, NKEYS)
        TV = c6.take(2 * ROWS, TOPK)
        TIU = c6.take(2 * ROWS, TOPK).bitcast(U32)
        TIF = c6.take(2 * ROWS, TOPK)
        WK = c6.take(2, 2, 256)
        V16 = c6.take(2, TOPK)
        I16 = c6.take(2, TOPK).bitcast(U32)
        NR = 2 * PEER_HEADS
        BV = c6.take(NR, TOPK)
        BPU = c6.take(NR, TOPK).bitcast(U32)
        PAU = c6.take(2, NR * TOPK).bitcast(U32)
        PAF = c6.take(2, NR * TOPK)
        EQ = c6.take(NR, TOPK * TOPK)
        EQ2 = c6.take(NR, TOPK * TOPK)
        IJG = c6.take(3, NR * TOPK)
        MXS = c6.take(3, NR)

        X = view(res[:, :], KT)
        h = view(res[:, 0:KT * T], KT)
        tmp = view(res[:, KT * T:], KT)
        h_hi = view(res_r[:, KT * T:], KT)
        h_lo1 = view(arena_r("h_lo1", RG_AT, KT * T)[:, :], KT)
        h_lo2 = view(res_r[:, 0:KT * T], KT)

        setup_in = sem("setup_in")
        lru_done = sem("lru_done")
        w_landed = sems("w_landed", RING)
        chunk_done = sems("chunk_done", RING)
        split_hi = sem("split_hi")
        split_lo = sem("split_lo")
        unit_used = sem("unit_used")
        wide_in = sem("wide_in")
        first_done = sem("first_done")
        bank_free = sems("bank_free", 2)
        dec_landed = sems("dec_landed", 2)
        dec_free = sems("dec_free", 2)
        ada_rows = sem("ada_rows")
        silc_ready = sem("silc_ready")
        ada_cols = sem("ada_cols")
        mod_ready = sem("mod_ready")
        sq_ready = sem("sq_ready")
        ss_ready = sem("ss_ready")
        sd_ready = sem("sd_ready")
        rs_ready = sem("rs_ready")
        h_ready = sem("h_ready")
        f_mm = sem("f_mm")
        f_arg = sem("f_arg")
        f_sin = sem("f_sin")
        rope_in = sem("rope_in")

        W = Uses(RING)
        B = [Uses(1), Uses(1)]

        stored = sem("stored")

        def wide(ap, axis, n):
            shape = list(ap.shape)
            shape.insert(axis, n)
            return ap.unsqueeze(axis).to_broadcast(shape)

        def col(ap, c):
            return ap.unsqueeze(2)[:, c, :]

        PHASES = [("ada", 24, 1), ("hy_in", 32, 2), ("hy_out", 8, 1), ("kv", 4, 2), ("q", 8, 1), ("z", 8, 1),
                  ("at_out", 8, 1)]
        for l in range(DEPTH):
            PHASES += [(f"proj{l}", 17, 1), (f"out{l}", 8, 1), (f"wq{l}", 4, 1), (f"peer{l}", BLOCKS, 1)]
        first, uses, at, used = {}, {}, 0, [0, 0]
        for name, n, banks in PHASES:
            first[name], uses[name] = at, list(used)
            for k in range(n):
                for b in ((0, 1) if banks == 2 else ((at + k) % 2,)):
                    used[b] += 1
            at += n

        def turns(e, n):
            full, rest = divmod(n, RING)
            if full > 1:
                with e.Fori(0, full) as i:
                    for j in range(RING):
                        yield i, j
            else:
                for j in range(full * RING):
                    yield 0, j
            for j in range(rest):
                yield full, j

        def slot_of(name, i, j):
            k = first[name] + j
            return k % RING, k // RING + i

        def bank_of(name, i, j):
            b = (first[name] + j) % 2
            return b, uses[name][b] + j // 2 + (RING // 2) * i

        def wait_chunk(pe, name, i, j):
            s, r = slot_of(name, i, j)
            pe.wait_ge(w_landed[s], 16 * (r + 1))
            return wring[:, s, :]

        def wait_done(e, name, i, j):
            s, r = slot_of(name, i, j)
            e.wait_ge(chunk_done[s], r + 2)

        def stream_chunk(sp, name, src, i, j, idx):
            s, r = slot_of(name, i, j)
            sp.wait_ge(chunk_done[s], r + 1)
            sp.dma_start(wring[:, s, :], src[idx]).then_inc(w_landed[s], 16)

        def stream(sp, name, src, n):
            for i, j in turns(sp, n):
                stream_chunk(sp, name, src, i, j, i * RING + j)

        def product(pe, name, n, rhs, width, kt):
            for i, j in turns(pe, n):
                w = wait_chunk(pe, name, i, j)
                b, u = bank_of(name, i, j)
                pe.wait_ge(bank_free[b], u + 1)
                for t in range(CHUNK // (kt * P)):
                    for k in range(kt):
                        mm = pe.matmul(bank[b][:, t * width:(t + 1) * width], w[:, (t * kt + k) * P:(t * kt + k + 1) * P],
                                       rhs[:, k, :], start=(k == 0), stop=(k == kt - 1))
                mm.then_inc(chunk_done[slot_of(name, i, j)[0]], 1)

        SPLIT_PHASES = [(n, k) for l in range(DEPTH) for n, k in ((f"proj{l}", 17), (f"wq{l}", 4), (f"peer{l}", BLOCKS))]
        split_first, at = {}, 0
        for name, n in SPLIT_PHASES:
            split_first[name] = at
            at += n * UNITS

        def unit_of(name, i, q):
            return split_first[name] + UNITS * RING * i + q

        def raw_quarter(name, i, j, q):
            return wring[:, slot_of(name, i, j)[0], q * UNIT:(q + 1) * UNIT]

        def hi_quarter(act, name, i, j, q, n, buf):
            s, r = slot_of(name, i, j)
            act.wait_ge(w_landed[s], 16 * (r + 1))
            act.wait_ge(unit_used, n + 1)
            act.activation(SPLIT[:, buf, 0, :], raw_quarter(name, i, j, q), ACT.Copy).then_inc(split_hi, 1)

        def lo_quarter(v, name, i, j, q, n, buf, last):
            v.wait_ge(split_hi, n + 1)
            v.tensor_tensor(SPLIT[:, buf, 1, :], raw_quarter(name, i, j, q), SPLIT[:, buf, 0, :].bitcast(F32),
                            ALU.subtract).then_inc(split_lo, 1)
            if last:
                v.drain().then_inc(chunk_done[slot_of(name, i, j)[0]], 1)

        def split_activations(v, src, hi, lo):
            n = src.shape[1] // 2
            for k in range(2):
                v.tensor_copy(hi[:, k * n:(k + 1) * n, :], src[:, k * n:(k + 1) * n, :])
            v.drain()
            for k in range(2):
                v.tensor_tensor(lo[:, k * n:(k + 1) * n, :], src[:, k * n:(k + 1) * n, :],
                                hi[:, k * n:(k + 1) * n, :].bitcast(F32), ALU.subtract)

        def mm3(pe, out_ap, w_hi, w_lo, x_hi, x_lo, start, stop, **kw):
            pe.matmul(out_ap, w_hi, x_hi, start=start, stop=False, **kw)
            pe.matmul(out_ap, w_hi, x_lo, start=False, stop=False, **kw)
            return pe.matmul(out_ap, w_lo, x_hi, start=False, stop=stop, **kw)

        def product3(pe, name, n, x_hi, x_lo, width, kt):
            for i, j in turns(pe, n):
                b, u = bank_of(name, i, j)
                pe.wait_ge(bank_free[b], u + 1)
                for q in range(UNITS):
                    c = unit_of(name, i, UNITS * j + q)
                    pe.wait_ge(split_lo, c + 1)
                    for m in range(UNIT // P):
                        t, k = divmod(q * (UNIT // P) + m, kt)
                        w = slice(m * P, (m + 1) * P)
                        mm = mm3(pe, bank[b][:, t * width:(t + 1) * width], SPLIT[:, q, 0, w], SPLIT[:, q, 1, w],
                                 x_hi[:, k, :], x_lo[:, k, :], k == 0, k == kt - 1)
                    mm.then_inc(unit_used, 1)

        def ahead(e, n, work, drain):
            full, rest = divmod(n, RING)
            work(0, 0)
            if full > 1:
                with e.Fori(0, full - 1) as i:
                    for j in range(RING):
                        work(i, j + 1)
                        drain(i, j)
            lead = (full - 1) if full > 1 else 0
            for j in range(n - RING * lead):
                if RING * lead + j + 1 < n:
                    work(lead, j + 1)
                drain(lead, j)

        def hi_chunk(act, name):
            def work(i, j):
                for q in range(UNITS):
                    hi_quarter(act, name, i, j, q, unit_of(name, i, UNITS * j + q), q)
            return work

        def lo_chunk(v, name):
            def work(i, j):
                for q in range(UNITS):
                    lo_quarter(v, name, i, j, q, unit_of(name, i, UNITS * j + q), q, q == UNITS - 1)
            return work

        def wait_product(e, name, i, j):
            e.wait_ge(unit_used, unit_of(name, i, UNITS * j + UNITS - 1) + 1 + UNITS)

        def ada_scalar(act):
            act.wait_ge(setup_in, SETUP)
            act.activation(SILC, V1["c"].rearrange("p (k s) -> p k s", s=2), ACT.Silu).then_inc(silc_ready, 1)

        def ada_tensor(pe):
            pe.wait_ge(silc_ready, 1)
            for i, j in turns(pe, 24):
                w = wait_chunk(pe, "ada", i, j)
                b, u = bank_of("ada", i, j)
                pe.wait_ge(bank_free[b], u + 1)
                for k in range(KT):
                    mm = pe.matmul(bank[b][0:2, 0:256], SILC[:, k, :], w[:, k * 256:(k + 1) * 256],
                                   start=(k == 0), stop=(k == KT - 1))
                mm.then_inc(chunk_done[slot_of("ada", i, j)[0]], 1)
            pe.wait_ge(ada_rows, 1)
            for n in range(48):
                mm = pe.transpose(bank[2][:, 2 * n:2 * n + 2], ADAROW[0:2, n * P:(n + 1) * P], ident[0:2, 0:2])
            mm.then_inc(ada_cols, 1)

        def ada_vector(v):
            rows = ADAROW.rearrange("p (n c) -> p n c", n=24)
            for i, j in turns(v, 24):
                b, _ = bank_of("ada", i, j)
                wait_done(v, "ada", i, j)
                v.tensor_copy(rows[0:2, i * RING + j, :], bank[b][0:2, 0:256]).then_inc(bank_free[b], 1)
            v.drain().then_inc(ada_rows, 1)
            v.wait_ge(ada_cols, 1)
            v.tensor_tensor(KEEP1[:, 0:96].rearrange("p (n s) -> p n s", s=2),
                            bank[2][:, 0:96].rearrange("p (n s) -> p n s", s=2), wide(V1["ada_b"], 2, 2), ALU.add)
            v.drain()
            for l in range(DEPTH):
                v.scalar_tensor_tensor(adag[:, l], adac[:, l, 8:16], 1.0, wide(V1["norm_g"][:, 8 * l:8 * l + 8], 2, 2),
                                       ALU.add, ALU.mult)
            v.drain().then_inc(mod_ready, 1)

        def rms_scalar(act, l):
            if l == 0:
                act.wait_ge(ada_cols, 1)
            else:
                act.wait_ge(x_new, 1)
            for k in range(KT):
                act.activation(SQ1[:, k, :], X[:, k, :], ACT.Square).then_inc(sq_ready, 1)
            act.wait_ge(ss_ready, l + 1)
            act.activation(RS1, bank[3][:, :], ACT.Sqrt, scale=1.0 / D, bias=C["eps6"]).then_inc(sd_ready, 1)
            act.wait_ge(mod_ready, 1)
            act.wait_ge(rs_ready, l + 1)
            for k in range(KT):
                a = act.activation(H1[:, k, T:T2], TM1[:, k, T:T2], ACT.Identity, scale=adag[:, l, k, 1:2],
                                   bias=adac[:, l, k, 1:2])
            a.then_inc(h_ready, 1)

        def rms_tensor(pe, l):
            for k in range(KT):
                pe.wait_ge(sq_ready, KT * l + k + 1)
                mm = pe.matmul(bank[3][:, :], ones, SQ1[:, k, :], start=(k == 0), stop=(k == KT - 1))
            mm.then_inc(ss_ready, 1)
            pe.wait_ge(h_ready, 2 * (l + 1))

        def rms_vector(v, l):
            v.wait_ge(sd_ready, l + 1)
            v.reciprocal(RS1, RS1)
            v.drain()
            v.tensor_tensor(TM1, X, wide(RS1, 1, KT), ALU.mult).then_inc(rs_ready, 1)
            v.drain()
            for k in range(KT):
                a = v.tensor_scalar(H1[:, k, 0:T], TM1[:, k, 0:T], adag[:, l, k, 0:1], adac[:, l, k, 0:1],
                                    ALU.mult, ALU.add)
            a.then_inc(h_ready, 1)

        TWO_PI = 2 * np.pi
        PI_A, PI_B = 6.28125, TWO_PI - 6.28125
        PI_MAX = float(np.nextafter(np.float32(np.pi), np.float32(0)))
        MAGIC = 12582912.0

        def filter_tensor(pe):
            pe.wait_ge(setup_in, SETUP)
            for q in range(3):
                rows = 33 if q == 0 else 64
                rhs = HC["z"][0:33, :] if q == 0 else HF[0:64, 2, :]
                if q:
                    pe.wait_ge(f_sin, q)
                pe.matmul(bank[4][0:64, 0:T], V1["fw"][0:rows, 64 * q:64 * q + 64], rhs,
                          start=True, stop=True).then_inc(f_mm, 1)

        def filter_vector(v):
            v.wait_ge(setup_in, SETUP)
            a, n = HF[0:64, 0, :], HF[0:64, 1, :]
            for q in range(3):
                v.wait_ge(f_mm, q + 1)
                v.tensor_scalar(a, bank[4][0:64, 0:T], V1["fb"][0:64, q:q + 1], V1["freq"][0:64, :], ALU.add, ALU.mult)
                v.drain()
                v.tensor_scalar(n, a, 1.0 / TWO_PI, MAGIC, ALU.mult, ALU.add)
                v.drain()
                v.tensor_scalar(n, n, MAGIC, None, ALU.subtract)
                v.drain()
                v.scalar_tensor_tensor(a, n, -PI_A, a, ALU.mult, ALU.add)
                v.drain()
                v.scalar_tensor_tensor(a, n, -PI_B, a, ALU.mult, ALU.add)
                v.drain()
                v.tensor_scalar(a, a, PI_MAX, -PI_MAX, ALU.min, ALU.max).then_inc(f_arg, 1)

        def filter_scalar(act):
            for q in range(3):
                act.wait_ge(f_arg, q + 1)
                act.activation(HSIN[0:64, :] if q == 2 else HF[0:64, 2, :], HF[0:64, 0, :], ACT.Sin).then_inc(f_sin, 1)

        kf_done = sem("kf_done")
        kb_ready = sem("kb_ready")
        ksd_ready = sem("ksd_ready")
        kabs_ready = sem("kabs_ready")
        kdft_done = sem("kdft_done")
        kspec_ready = sem("kspec_ready")
        u_ready = sem("u_ready")
        t_done = sem("t_done")
        ut_ready = sem("ut_ready")
        udft_done = sem("udft_done")
        uspec_free = sem("uspec_free")
        y_ready = sem("y_ready")
        inv_done = sem("inv_done")
        zs_ready = sem("zs_ready")
        yg_done = sem("yg_done")
        x_new = sem("x_new")

        def hyena_sync(sp, w_src, dec_src):
            with sp.Fori(0, CT // 2) as i:
                for j in range(2):
                    sp.wait_ge(kb_ready, 2 * i + j + 1)
                    sp.dma_start(DEC[:, j, :], dec_src[2 * i + j]).then_inc(dec_landed[j], 16)
                    for q in range(2):
                        stream_chunk(sp, "hy_in", w_src, i, 2 * j + q, i * RING + 2 * j + q)

        def tile_product(pe, name, w, t, b, use, width):
            pe.wait_ge(bank_free[b], use + 1)
            for k in range(KT):
                mm = pe.matmul(bank[b][:, 0:width], w[:, (t * KT + k) * P:(t * KT + k + 1) * P], H1[:, k, 0:width],
                               start=(k == 0), stop=(k == KT - 1))
            return mm

        def hyena_tensor(pe):
            with pe.Fori(0, CT // 2) as i:
                for j in range(2):
                    c = 2 * i + j
                    pe.wait_ge(kb_ready, c + 2)
                    for tt in range(2):
                        mm = pe.matmul(bank[2][:, tt * 256:(tt + 1) * 256], HSIN[0:64, tt * P:(tt + 1) * P],
                                       W4[0:64, c, :], start=True, stop=True)
                    mm.then_inc(kf_done, 1)
                    q = 2 * j
                    w = wait_chunk(pe, "hy_in", i, q)
                    use = [uses["hy_in"][b] + q + RING * i for b in range(2)]
                    tile_product(pe, "hy_in", w, 0, 0, use[0], T2).then_inc(first_done, 1)
                    tile_product(pe, "hy_in", w, 1, 1, use[1], T2).then_inc(chunk_done[slot_of("hy_in", i, q)[0]], 1)
                    pe.wait_ge(ksd_ready, c + 1)
                    pe.wait_ge(kabs_ready, c + 1)
                    pe.wait_ge(kspec_ready, c + 1)
                    for f in range(2):
                        for tt in range(2):
                            pe.matmul(bank[3][:, f * P:(f + 1) * P], HC["re"][:, tt * T + f * P:tt * T + (f + 1) * P],
                                      KSD[:, 0, tt * P:(tt + 1) * P], start=(tt == 0), stop=(tt == 1))
                    for tt in range(2):
                        pe.matmul(bank[3][:, 2 * P:3 * P], HC["rex"][:, tt * P:(tt + 1) * P],
                                  KSD[:, 0, tt * P:(tt + 1) * P], start=(tt == 0), stop=(tt == 1))
                    for f in range(2):
                        for tt in range(2):
                            pe.matmul(bank[4][:, f * P:(f + 1) * P], HC["sn"][:, tt * T + f * P:tt * T + (f + 1) * P],
                                      KSD[:, 1, tt * P:(tt + 1) * P], start=(tt == 0), stop=(tt == 1))
                    for g in range(4):
                        mm = pe.matmul(bank[4][:, 2 * P:2 * P + 1], KABS[:, g * P:(g + 1) * P], ones[:, 0:1],
                                       start=(g == 0), stop=(g == 3))
                    mm.then_inc(kdft_done, 1)
                    q = 2 * j + 1
                    w = wait_chunk(pe, "hy_in", i, q)
                    use = [uses["hy_in"][b] + q + RING * i for b in range(2)]
                    tile_product(pe, "hy_in", w, 0, 0, use[0], T2).then_inc(first_done, 1)
                    pe.wait_ge(u_ready, c + 1)
                    pe.wait_ge(yg_done, c + 1)
                    for g in range(4):
                        mm = pe.transpose(bank[5][:, g * P:(g + 1) * P], U[:, g * P:(g + 1) * P], ident)
                    mm.then_inc(t_done, 1)
                    tile_product(pe, "hy_in", w, 1, 1, use[1], T2).then_inc(chunk_done[slot_of("hy_in", i, q)[0]], 1)
                    pe.wait_ge(ut_ready, c + 1)
                    pe.wait_ge(uspec_free, c + 1)
                    ut = UT.rearrange("p (s a c) -> p s a c", s=2, a=2)
                    for m, b in (("re", 6), ("im", 7)):
                        for f in range(2):
                            for tt in range(2):
                                mm = pe.matmul(bank[b][:, f * 256:(f + 1) * 256],
                                               HC[m][:, tt * T + f * P:tt * T + (f + 1) * P], ut[:, :, tt, :],
                                               start=(tt == 0), stop=(tt == 1))
                    mm.then_inc(udft_done, 1)
                    pe.wait_ge(y_ready, c + 1)
                    for s in range(2):
                        for n, (part, m, f) in enumerate([(0, "ire", 0), (0, "ire", 1), (1, "iim", 0), (1, "iim", 1)]):
                            mm = pe.matmul(bank[5][:, s * T:(s + 1) * T],
                                           YRI[:, part, f * 256 + s * P:f * 256 + (s + 1) * P],
                                           HC[m][:, f * T:(f + 1) * T], start=(n == 0), stop=(n == 3))
                    mm.then_inc(inv_done, 1)

        def hyena_scalar(act):
            act.sem_inc(kspec_ready, 1)
            with act.Fori(0, CT // 2) as i:
                for j in range(2):
                    c = 2 * i + j
                    act.wait_ge(kb_ready, c + 3)
                    act.activation(KABS, KB, ACT.Abs).then_inc(kabs_ready, 1)
                    act.wait_ge(kdft_done, c + 1)
                    act.wait_ge(uspec_free, c + 1)
                    act.activation(KSPEC[:, 0:3, :], view(bank[3][:, 0:3 * P], 3), ACT.Copy)
                    act.activation(KSPEC[:, 3:5, :], view(bank[4][:, 0:2 * P], 2), ACT.Copy)
                    act.activation(KNORM[:, 0:1], bank[4][:, 2 * P:2 * P + 1], ACT.Copy).then_inc(kspec_ready, 1)
                    act.wait_ge(t_done, c + 1)
                    act.activation(UT, bank[5][:, :], ACT.Copy).then_inc(ut_ready, 1)
                    wait_done(act, "hy_in", i, 2 * j + 1)
                    act.wait_ge(yg_done, c + 1)
                    act.activation(ZS1, bank[1][:, :], ACT.Silu).then_inc(bank_free[1], 1)
                    act.drain().then_inc(zs_ready, 1)

        def two(ap):
            return ap.rearrange("p (s t) -> p s t", s=2)

        def hyena_vector(v):
            v.sem_inc(kb_ready, 2)
            v.sem_inc(uspec_free, 1)
            v.sem_inc(yg_done, 1)
            conv_w = V1["conv_w"].rearrange("p (c q k) -> p c q k", c=CT, q=3)
            conv_b = V1["conv_b"].rearrange("p (c q) -> p c q", c=CT)

            def conv(c, q, src):
                o, s = two(CX[:, q, :]), two(src)
                v.tensor_scalar(o, s, conv_w[:, c, q, 1:2], conv_b[:, c, q:q + 1], ALU.mult, ALU.add)
                v.drain()
                v.scalar_tensor_tensor(o[:, :, 1:T], s[:, :, 0:T - 1], conv_w[:, c, q, 0:1], o[:, :, 1:T],
                                       ALU.mult, ALU.add)
                v.drain()
                return v.scalar_tensor_tensor(o[:, :, 0:T - 1], s[:, :, 1:T], conv_w[:, c, q, 2:3], o[:, :, 0:T - 1],
                                              ALU.mult, ALU.add)

            with v.Fori(0, CT // 2) as i:
                for j in range(2):
                    c = 2 * i + j
                    v.wait_ge(kf_done, c + 1)
                    v.wait_ge(dec_landed[j], 16 * (i + 1))
                    v.tensor_tensor(KB, bank[2][:, :], DEC[:, j, :], ALU.mult).then_inc(kb_ready, 1)
                    v.drain()
                    kb = KB.rearrange("p (a f c) -> p a f c", a=2, f=2)
                    v.tensor_tensor(view(KSD[:, 0, :], 2), kb[:, :, 0, :], kb[:, :, 1, :], ALU.add)
                    v.tensor_tensor(view(KSD[:, 1, :], 2), kb[:, :, 0, :], kb[:, :, 1, :],
                                    ALU.subtract).then_inc(ksd_ready, 1)
                    v.wait_ge(first_done, 4 * i + 2 * j + 1)
                    conv(c, 0, bank[0][:, :]).then_inc(bank_free[0], 1)
                    wait_done(v, "hy_in", i, 2 * j)
                    conv(c, 1, bank[1][:, :]).then_inc(bank_free[1], 1)
                    v.drain()
                    v.tensor_tensor(U, CX[:, 0, :], CX[:, 1, :], ALU.mult).then_inc(u_ready, 1)
                    v.wait_ge(first_done, 4 * i + 2 * j + 2)
                    conv(c, 2, bank[0][:, :]).then_inc(bank_free[0], 1)
                    v.wait_ge(kspec_ready, c + 2)
                    v.reciprocal(KNORM[:, 1:2], KNORM[:, 0:1])
                    v.tensor_scalar(YT[:, 0, :], U, col(V1["hy_d"], c), None, ALU.mult)
                    v.wait_ge(udft_done, c + 1)
                    ur = bank[6][:, :].rearrange("p (f s c) -> p f s c", f=2, s=2)
                    ui = bank[7][:, :].rearrange("p (f s c) -> p f s c", f=2, s=2)
                    pr = [PR4[:, n, :].rearrange("p (f s c) -> p f s c", f=2, s=2) for n in range(4)]
                    v.tensor_tensor(pr[0], ur, wide(KSPEC[:, 0:2, :], 2, 2), ALU.mult)
                    v.tensor_tensor(pr[1], ui, wide(KSPEC[:, 3:5, :], 2, 2), ALU.mult)
                    v.tensor_tensor(pr[2], ur, wide(KSPEC[:, 3:5, :], 2, 2), ALU.mult)
                    v.tensor_tensor(pr[3][:, 0], ui[:, 0], wide(KSPEC[:, 2, :], 1, 2), ALU.mult)
                    v.tensor_tensor(pr[3][:, 1], ui[:, 1], wide(KSPEC[:, 1, :], 1, 2), ALU.mult).then_inc(uspec_free, 1)
                    v.drain()
                    v.tensor_tensor(YRI[:, 0, :], PR4[:, 0, :], PR4[:, 1, :], ALU.subtract)
                    v.tensor_tensor(YRI[:, 1, :], PR4[:, 2, :], PR4[:, 3, :], ALU.add).then_inc(y_ready, 1)
                    v.wait_ge(inv_done, c + 1)
                    v.scalar_tensor_tensor(YT[:, 1, :], bank[5][:, :], KNORM[:, 1:2], YT[:, 0, :], ALU.mult, ALU.add)
                    v.drain()
                    v.tensor_tensor(YT[:, 1, :], YT[:, 1, :], CX[:, 2, :], ALU.mult)
                    v.drain()
                    v.wait_ge(zs_ready, c + 1)
                    v.tensor_tensor(YG[:, c, :], YT[:, 1, :], ZS1, ALU.mult).then_inc(yg_done, 1)

        def add_gated(v, name, l, seqs):
            for i, j in turns(v, 8):
                n = i * RING + j
                b, _ = bank_of(name, i, j)
                wait_done(v, name, i, j)
                for s in range(seqs):
                    a = v.scalar_tensor_tensor(X[:, n, s * T:(s + 1) * T], bank[b][:, s * T:(s + 1) * T],
                                               adac[:, l, 16 + n, s:s + 1], X[:, n, s * T:(s + 1) * T],
                                               ALU.mult, ALU.add)
                a.then_inc(bank_free[b], 1)
            v.drain().then_inc(x_new, 1)

        ksq = sem("ksq")
        kss = sem("kss")
        ksd = sem("ksd")
        kn_ready = sem("kn_ready")
        krot = sem("krot")
        k_ready = sem("k_ready")
        vt_done = sem("vt_done")
        v_ready = sem("v_ready")
        q_in = sem("q_in")
        qsq, qss, qsd, qn_ready, qrot, qf_ready = (sem(n) for n in ("qsq", "qss", "qsd", "qn_ready", "qrot", "qf_ready"))
        vs_ready = sem("vs_ready")
        s_done = sem("s_done")
        nmax_ready = sem("nmax_ready")
        p_exp = sem("p_exp")
        p_ready = sem("p_ready")
        pt_done = sem("pt_done")
        pt_ready = sem("pt_ready")
        pv_done = sem("pv_done")
        og_done = sem("og_done")
        SCALE = float(P) ** -0.5
        PTV = PTR.rearrange("p a (k c) -> p (a k) c", k=2).rearrange("p (h k) c -> p h k c", h=2)

        def kv_tensor(pe):
            for i, j in turns(pe, 4):
                w = wait_chunk(pe, "kv", i, j)
                use = [uses["kv"][b] + j + RING * i for b in range(2)]
                tile_product(pe, "kv", w, 0, 0, use[0], T2).then_inc(first_done, 1)
                tile_product(pe, "kv", w, 1, 1, use[1], T2).then_inc(chunk_done[slot_of("kv", i, j)[0]], 1)

        def kv_scalar(act):
            for g in range(KV_HEADS):
                act.wait_ge(first_done, 2 * CT + g + 1)
                act.activation(KR[:, g, :], bank[0][:, :], ACT.Copy).then_inc(bank_free[0], 1)
                wait_done(act, "kv", 0, g)
                act.activation(VR[:, g, :], bank[1][:, :], ACT.Copy).then_inc(bank_free[1], 1)
            act.drain()
            for g in range(KV_HEADS):
                act.activation(PRB[:, g, :], KR[:, g, :], ACT.Square).then_inc(ksq, 1)

        def gather(act, name, dst, func, n):
            for i, j in turns(act, n):
                b, _ = bank_of(name, i, j)
                wait_done(act, name, i, j)
                act.activation(dst[:, i * RING + j, :], bank[b][:, :], func).then_inc(bank_free[b], 1)

        pairs = lambda ap: ap.rearrange("p (n a) t -> p n (a t)", a=2)

        def prep_tensor(pe):
            for g in range(KV_HEADS):
                pe.wait_ge(ksq, g + 1)
                pe.matmul(bank[2 + g][:, :], ones, PRB[:, g, :], start=True, stop=True).then_inc(kss, 1)
            for g in range(KV_HEADS):
                if g >= 2:
                    pe.wait_ge(v_ready, g - 1)
                for k in range(4):
                    mm = pe.transpose(bank[6 + g % 2][:, k * P:(k + 1) * P], VR[:, g, k * P:(k + 1) * P], ident)
                mm.then_inc(vt_done, 1)
            for g in range(KV_HEADS):
                pe.wait_ge(kn_ready, g + 1)
                pe.wait_ge(rope_in, 16)
                pe.matmul(bank[2 + g][:, 0:T], RO["rot"], KR[:, g, 0:T], start=True, stop=True).then_inc(krot, 1)

        def prep_scalar(act):
            for g in range(KV_HEADS):
                act.wait_ge(kss, g + 1)
                act.activation(PTR[:, g, :], bank[2 + g][:, :], ACT.Sqrt, scale=1.0 / P, bias=C["eps6"]).then_inc(ksd, 1)
            for g in range(KV_HEADS):
                act.wait_ge(vt_done, g + 1)
                act.activation(VR[:, g, :], bank[6 + g % 2][:, :], ACT.Copy).then_inc(v_ready, 1)

        def prep_vector(v):
            for g in range(KV_HEADS):
                v.wait_ge(ksd, g + 1)
                v.reciprocal(PTR[:, g, :], PTR[:, g, :])
                v.drain()
                v.scalar_tensor_tensor(KR[:, g, :], KR[:, g, :], V1["k_g"], PTR[:, g, :],
                                       ALU.mult, ALU.mult).then_inc(kn_ready, 1)
            for g in range(KV_HEADS):
                v.drain()
                v.wait_ge(krot, g + 1)
                v.tensor_tensor(RT1[:, 0:T], KR[:, g, 0:T], RO["cos"], ALU.mult)
                v.tensor_tensor(RT2[:, 0:T], bank[2 + g][:, 0:T], RO["sin"], ALU.mult)
                v.drain()
                v.tensor_tensor(KR[:, g, 0:T], RT1[:, 0:T], RT2[:, 0:T], ALU.add).then_inc(k_ready, 1)

        def heads_tensor(pe):
            pe.wait_ge(q_in, 1)
            with pe.Fori(0, KV_HEADS) as g:
                for pp in range(2):
                    n = 2 * g + pp
                    pe.wait_ge(qsq, n + 1)
                    pe.wait_ge(og_done, 2 * n + 2)
                    pe.matmul(bank[2][:, :], ones, SQA, start=True, stop=True).then_inc(qss, 1)
                    pe.wait_ge(qn_ready, n + 1)
                    pe.matmul(bank[3][:, :], RO["rot"], QN, start=True, stop=True).then_inc(qrot, 1)
                    pe.wait_ge(k_ready, KV_HEADS)
                    pe.wait_ge(qf_ready, n + 1)
                    for q in range(4):
                        pe.matmul(bank[4 + q][:, :], QF[:, q * P:(q + 1) * P], KR[:, g, :],
                                  start=True, stop=True).then_inc(s_done, 1)
                    for q in range(4):
                        pe.wait_ge(p_ready, 4 * n + q + 1)
                        for k in range(4):
                            mm = pe.transpose(bank[4 + q][:, k * P:(k + 1) * P], PRB[:, q, k * P:(k + 1) * P], ident)
                        mm.then_inc(pt_done, 1)
                    pe.wait_ge(vs_ready, g + 1)
                    for a in range(2):
                        pe.wait_ge(pt_ready, 4 * n + 2 * a + 2)
                        for k in range(4):
                            mm = pe.matmul(bank[2 + a][:, 0:T], VS[:, k, :], PTV[:, a, k, :], start=(k == 0), stop=(k == 3))
                        mm.then_inc(pv_done, 1)

        def heads_scalar(act):
            act.drain().then_inc(q_in, 1)
            qr = pairs(QR)
            with act.Fori(0, KV_HEADS) as g:
                for pp in range(2):
                    n = 2 * g + pp
                    act.activation(SQA, qr[:, n, :], ACT.Square).then_inc(qsq, 1)
                    if pp == 0:
                        act.wait_ge(og_done, 2 * n + 2)
                        act.activation(VS, view2(VR[:, g, :], 4), ACT.Copy).then_inc(vs_ready, 1)
                    act.wait_ge(qss, n + 1)
                    act.activation(RSA, bank[2][:, :], ACT.Sqrt, scale=1.0 / P, bias=C["eps6"]).then_inc(qsd, 1)
                    for q in range(4):
                        act.wait_ge(nmax_ready, 4 * n + q + 1)
                        act.activation(PRB[:, q, :], bank[4 + q][:, :], ACT.Exp, scale=SCALE, bias=STAT[:, 1, q:q + 1],
                                       accum_out=STAT[:, 2, q:q + 1]).then_inc(p_exp, 1)
                    for q in range(4):
                        act.wait_ge(pt_done, 4 * n + q + 1)
                        act.activation(PTV[:, q // 2, :, (q % 2) * P:(q % 2 + 1) * P], view2(bank[4 + q][:, :], 4),
                                       ACT.Copy).then_inc(pt_ready, 1)

        def view2(ap, a):
            return ap.rearrange("p (a b) -> p a b", a=a)

        def heads_vector(v):
            v.sem_inc(og_done, 2)
            v.wait_ge(rope_in, 16)
            v.wait_ge(q_in, 1)
            with v.Fori(0, KV_HEADS) as g:
                for pp in range(2):
                    n = 2 * g + pp
                    v.drain()
                    v.wait_ge(qsd, n + 1)
                    v.reciprocal(RSA, RSA)
                    v.drain()
                    v.scalar_tensor_tensor(QN, pairs(QR)[:, n, :], V1["q_g"], RSA, ALU.mult, ALU.mult).then_inc(qn_ready, 1)
                    v.drain()
                    v.tensor_tensor(two(RT1), two(QN), wide(RO["cos"], 1, 2), ALU.mult)
                    v.wait_ge(qrot, n + 1)
                    v.tensor_tensor(two(RT2), two(bank[3][:, :]), wide(RO["sin"], 1, 2), ALU.mult)
                    v.drain()
                    v.tensor_tensor(QF, RT1, RT2, ALU.add).then_inc(qf_ready, 1)
                    for q in range(4):
                        v.wait_ge(s_done, 4 * n + q + 1)
                        v.reduce_max(STAT[:, 0, q:q + 1], bank[4 + q][:, :], AX_X)
                        v.drain()
                        v.tensor_scalar(STAT[:, 1, q:q + 1], STAT[:, 0, q:q + 1], -SCALE, None, ALU.mult).then_inc(nmax_ready, 1)
                    for q in range(4):
                        v.wait_ge(p_exp, 4 * n + q + 1)
                        v.reciprocal(STAT[:, 3, q:q + 1], STAT[:, 2, q:q + 1])
                        v.drain()
                        v.tensor_scalar(PRB[:, q, :], PRB[:, q, :], STAT[:, 3, q:q + 1], None, ALU.mult).then_inc(p_ready, 1)
                    for a in range(2):
                        v.wait_ge(pv_done, 2 * n + a + 1)
                        v.tensor_tensor(OG[:, 2 * n + a, :], bank[2 + a][:, 0:T], ZG[:, 2 * n + a, :],
                                        ALU.mult).then_inc(og_done, 1)

        ln_in = sem("ln_in")
        ln_sum, ln_mu, ln_xc, ln_sq, ln_var, ln_sd = (sem(n) for n in ("ln_sum", "ln_mu", "ln_xc", "ln_sq", "ln_var", "ln_sd"))
        h_new = sem("h_new")

        def norm_tensor(pe, q, src):
            pe.wait_ge(ln_in, q + 1)
            for k in range(KT):
                mm = pe.matmul(bank[2][:, 0:T], ones, src[:, k, 0:T], start=(k == 0), stop=(k == KT - 1))
            mm.then_inc(ln_sum, 1)
            pe.wait_ge(ln_sq, q + 1)
            for k in range(KT):
                mm = pe.matmul(bank[3][:, 0:T], ones, SQ[:, k, :], start=(k == 0), stop=(k == KT - 1))
            mm.then_inc(ln_var, 1)
            pe.wait_ge(h_new, q + 1)

        def norm_scalar(act, q, centred):
            act.wait_ge(ln_sum, q + 1)
            act.activation(MU, bank[2][:, 0:T], ACT.Copy, scale=1.0 / D).then_inc(ln_mu, 1)
            act.wait_ge(ln_xc, q + 1)
            act.activation(SQ, centred, ACT.Square).then_inc(ln_sq, 1)
            act.wait_ge(ln_var, q + 1)
            act.activation(RS, bank[3][:, 0:T], ACT.Sqrt, scale=1.0 / D, bias=C["eps5"]).then_inc(ln_sd, 1)

        def norm_vector(v, q, src, centred, g, b, dst, parts):
            v.drain().then_inc(ln_in, 1)
            v.wait_ge(ln_mu, q + 1)
            v.tensor_tensor(centred, src, wide(MU, 1, KT), ALU.subtract).then_inc(ln_xc, 1)
            v.wait_ge(ln_sd, q + 1)
            v.reciprocal(RS, RS)
            v.drain()
            v.tensor_tensor(centred, centred, wide(RS, 1, KT), ALU.mult)
            v.drain()
            for k in range(KT):
                v.tensor_scalar(dst[:, k, :], centred[:, k, :], g[:, k:k + 1], b[:, k:k + 1], ALU.mult, ALU.add)
            v.drain()
            if parts:
                split_activations(v, dst, *parts)
            v.drain().then_inc(h_new, 1)

        XBC0, Q0, K0, V0, GATE0, Z0 = 4, 16, 20, 21, 22, 26
        prj_x = sem("prj_x")
        prj_all = sem("prj_all")
        dt_mm, dt_in = sem("dt_mm"), sem("dt_in")
        rgx_ready = sem("rgx_ready")
        rg_mm = sem("rg_mm")
        rg_act = sem("rg_act")
        sp_abs, sp_exp, sp_done = sem("sp_abs"), sem("sp_exp"), sem("sp_done")
        rg_gates = sem("rg_gates")
        a_ready = sem("a_ready")
        root_in, root_out = sem("root_in"), sem("root_out")
        alog_in, alog_out = sem("alog_in"), sem("alog_out")
        dec_in, dec_out = sem("dec_in"), sem("dec_out")
        colt_done, cols_ready = sem("colt_done"), sem("cols_ready")
        bc_conv = sem("bc_conv")
        bc_ready = sem("bc_ready")
        cb_done = sem("cb_done")
        cb_ready = sem("cb_ready")
        x_conv, x_ready = sem("x_conv"), sem("x_ready")
        xt_done, xdt_ready = sem("xt_done"), sem("xdt_ready")
        bcast_done = sem("bcast_done")
        seg_ready = sem("seg_ready")
        ex_ready = sem("ex_ready")
        m_ready = sem("m_ready")
        st_done, st_ready = sem("st_done"), sem("st_ready")
        y_done = sem("y_done")
        ys_ready, yq_ready = sem("ys_ready"), sem("yq_ready")
        gss_done, gsd_ready = sem("gss_done"), sem("gsd_ready")
        ys_used = sem("ys_used")
        qs_ready = sem("qs_ready")
        vtk_mm, vtk_ready = sem("vtk_mm"), sem("vtk_ready")
        sw_done, sw_max, sw_exp, sw_p, sw_t, sw_tc, sw_pv, sw_out = (
            sem(n) for n in ("sw_done", "sw_max", "sw_exp", "sw_p", "sw_t", "sw_tc", "sw_pv", "sw_out"))
        mix_ready = sem("mix_ready")
        NB_T = XBC_T
        PRJ2 = PRJ.rearrange("p (n a) t -> p n (a t)", a=2)
        HALF_SCALE = 64.0 ** -0.5

        def proj_tensor(pe, l):
            product3(pe, f"proj{l}", 17, h_hi, h_lo1, T, KT)
            pe.wait_ge(wide_in, 16 * (l + 1))
            for k in range(KT):
                mm = pe.matmul(bank[6][0:16, 0:T], WD["w_dt"][:, 16 * k:16 * k + 16], h[:, k, :],
                               start=(k == 0), stop=(k == KT - 1))
            mm.then_inc(dt_mm, 1)

        def proj_scalar(act, l):
            name = f"proj{l}"

            def drain_bank(i, j):
                b, _ = bank_of(name, i, j)
                wait_product(act, name, i, j)
                act.activation(PRJ2[:, i * RING + j, :], bank[b][:, :], ACT.Copy).then_inc(bank_free[b], 1)

            ahead(act, 17, hi_chunk(act, name), drain_bank)
            act.drain().then_inc(prj_x, 1)
            act.activation(PRJ[:, GATE0:GATE0 + 4, :], PRJ[:, GATE0:GATE0 + 4, :], ACT.Gelu_apprx_tanh)
            act.activation(PRJ[:, Z0:Z0 + 8, :], PRJ[:, Z0:Z0 + 8, :], ACT.Silu)
            act.drain().then_inc(prj_all, 1)

        def causal_conv(v, o, x, w, b):
            v.tensor_scalar(o, x, w(3), b, ALU.mult, ALU.add)
            for k in (2, 1, 0):
                s = 3 - k
                v.drain()
                a = v.scalar_tensor_tensor(o[:, s:T], x[:, 0:T - s], w(k), o[:, s:T], ALU.mult, ALU.add)
            return a

        def softplus_vector(v, l):
            L = LV[l]
            x, ax, s, s2, p = (SP[:, n, :] for n in range(5))
            v.drain()
            v.memset(x, 0.0)
            v.drain()
            v.tensor_scalar(x[:, 0:4], L["lam"], -1.0, None, ALU.mult)
            v.wait_ge(dt_mm, l + 1)
            v.tensor_scalar(x[0:16, 4:], bank[6][0:16, 0:T], L["dt_bias"][0:16, :], None, ALU.add)
            v.drain()
            v.scalar_tensor_tensor(ax, x, -1.0, x, ALU.mult, ALU.max).then_inc(sp_abs, 1)
            v.wait_ge(sp_exp, l + 1)
            v.tensor_scalar(s2, ax, 2.0, None, ALU.add)
            v.drain()
            v.reciprocal(s2, s2)
            v.drain()
            v.tensor_tensor(s, ax, s2, ALU.mult)
            v.drain()
            v.tensor_tensor(s2, s, s, ALU.mult)
            v.drain()
            v.tensor_scalar(p, s2, LOG1P_TERMS[0], None, ALU.mult)
            for term in LOG1P_TERMS[1:]:
                v.drain()
                v.scalar_tensor_tensor(p, p, term, s2, ALU.add, ALU.mult)
            v.drain()
            v.scalar_tensor_tensor(p, p, 1.0, s, ALU.add, ALU.mult)
            v.tensor_scalar(x, x, 0.0, None, ALU.max)
            v.drain()
            v.scalar_tensor_tensor(p, p, 2.0, x, ALU.mult, ALU.add)
            v.drain().then_inc(sp_done, 1)

        def lru_tensor(pe, l):
            pe.wait_ge(rgx_ready, l + 1)
            for n in range(8):
                m, t = n // 4, n % 4
                pe.wait_ge(rg_act, 8 * l + n + 1)
                pe.matmul(bank[4 + n % 2][:, 0:T], WD["rg_wax"][:, n * P:(n + 1) * P], RG[:, 0, t * T:(t + 1) * T],
                          start=True, stop=True).then_inc(rg_mm, 1)

        def lru_scalar(act, l):
            L = LV[l]
            act.wait_ge(sp_abs, l + 1)
            act.activation(SP[:, 1, :], SP[:, 1, :], ACT.Exp, scale=-1.0).then_inc(sp_exp, 1)
            act.activation(SROW[0:16, 3, 0:1], L["a_log"][0:16, :], ACT.Exp).then_inc(alog_out, 1)
            for n in range(8):
                m, t = n // 4, n % 4
                act.wait_ge(rg_mm, 8 * l + n + 1)
                act.activation(RG[:, 1 + m, t * T:(t + 1) * T], bank[4 + n % 2][:, 0:T], ACT.Sigmoid,
                               bias=L["bx" if m else "ba"][:, t:t + 1]).then_inc(rg_act, 1)
            act.wait_ge(rg_gates, l + 1)
            act.drain()
            for t in range(4):
                r = RG[:, 1, t * T:(t + 1) * T]
                act.activation(RG[:, 3, t * T:(t + 1) * T], r, ACT.Exp, scale=MU[:, t:t + 1])
                act.activation(RG[:, 4, t * T:(t + 1) * T], r, ACT.Tanh, scale=MU[:, 4 + t:5 + t])
            act.drain().then_inc(a_ready, 1)
            act.wait_ge(root_in, l + 1)
            act.activation(RG[:, 5, :], RG[:, 5, :], ACT.Sqrt).then_inc(root_out, 1)

        def lru_vector(v, l):
            L = LV[l]
            work = lo_chunk(v, f"proj{l}")
            for i, j in turns(v, 17):
                work(i, j)
            v.drain()
            v.wait_ge(prj_x, l + 1)
            w = L["rg_w"].rearrange("p (t k) -> p t k", k=4)
            for t in range(4):
                causal_conv(v, RG[:, 0, t * T:(t + 1) * T], PRJ[:, t, :], lambda k: w[:, t, k:k + 1], L["rg_b"][:, t:t + 1])
            v.drain().then_inc(rgx_ready, 1)
            softplus_vector(v, l)
            v.tensor_scalar(MU[:, 0:4], SP[:, 4, 0:4], -8.0, None, ALU.mult)
            v.tensor_scalar(MU[:, 4:8], SP[:, 4, 0:4], 8.0, None, ALU.mult)
            v.drain().then_inc(rg_gates, 1)
            v.wait_ge(a_ready, l + 1)
            th, u = RG[:, 4, :], RG[:, 5, :]
            v.tensor_scalar(u, th, 1.0, None, ALU.add)
            v.drain()
            v.reciprocal(u, u)
            v.drain()
            v.scalar_tensor_tensor(u, th, 2.0, u, ALU.mult, ALU.mult).then_inc(root_in, 1)
            v.tensor_tensor(RG[:, 2, :], RG[:, 2, :], RG[:, 0, :], ALU.mult)
            v.drain()
            v.wait_ge(root_out, l + 1)
            v.tensor_tensor(u, u, RG[:, 2, :], ALU.mult)
            v.drain()
            for t in range(4):
                c = slice(t * T, (t + 1) * T)
                v.tensor_tensor_scan(RG[:, 4, c], RG[:, 3, c], RG[:, 5, c], 0.0, ALU.mult, ALU.add)
            v.drain()
            v.wait_ge(prj_all, l + 1)
            v.tensor_tensor(MIX[:, 0:4, :], view(RG[:, 4, :], 4), PRJ[:, GATE0:GATE0 + 4, :], ALU.mult)

        def rows_vector(v, l):
            dt = SP[0:16, 4, 4:]
            da, cum, st = (SROW[0:16, n, :] for n in range(3))
            v.wait_ge(alog_out, l + 1)
            v.tensor_scalar(da, dt, SROW[0:16, 3, 0:1], -1.0, ALU.mult, ALU.mult)
            v.drain()
            for c in range(2):
                s = slice(c * P, (c + 1) * P)
                v.tensor_tensor_scan(cum[:, s], ones[0:16, :], da[:, s], 0.0, ALU.mult, ALU.add)
            v.drain().then_inc(dec_in, 1)
            v.tensor_tensor(AD[0:16], wide(cum, 1, SSM_HEADS), wide(ident[0:16, 0:16], 2, T), ALU.mult)
            v.wait_ge(colt_done, l + 1)
            v.tensor_copy(COLS, view(bank[4][:, 0:80], 5))
            v.drain().then_inc(cols_ready, 1)

        def rows_scalar(act, l):
            act.wait_ge(dec_in, l + 1)
            act.activation(SROW[0:16, 2, 0:P], SROW[0:16, 1, 0:P], ACT.Exp, scale=-1.0,
                           bias=SROW[0:16, 1, P - 1:P]).then_inc(dec_out, 1)

        def rows_tensor(pe, l):
            pe.wait_ge(sp_done, l + 1)
            pe.wait_ge(dec_out, l + 1)
            pe.wait_ge(rg_act, 8 * (l + 1) + 2)
            for n, ap in enumerate((SP[0:16, 4, 4:4 + P], SP[0:16, 4, 4 + P:4 + 2 * P], SROW[0:16, 1, 0:P],
                                    SROW[0:16, 1, P:2 * P], SROW[0:16, 2, 0:P])):
                mm = pe.transpose(bank[4][:, 16 * n:16 * n + 16], ap, ident[0:16, 0:16])
            mm.then_inc(colt_done, 1)

        def ssm_tensor(pe, l):
            pe.wait_ge(cols_ready, l + 1)
            with pe.Fori(0, SSM_GROUPS) as g:
                n = 2 * l + g
                pe.wait_ge(bc_ready, 2 * n + 2)
                for c in range(2):
                    s = slice(c * P, (c + 1) * P)
                    pe.matmul(bank[2][:, s], BC[:, 0, s], BC[:, 1, s], start=True, stop=True)
                pe.transpose(bank[3][:, 0:P], BC[:, 0, 0:P], ident).then_inc(cb_done, 1)
                for t in range(4):
                    m = 4 * n + t
                    par = t % 2
                    pe.wait_ge(x_ready, m + 1)
                    pe.wait_ge(ys_ready, m + 1)
                    for c in range(2):
                        mm = pe.transpose(bank[4][:, c * P:(c + 1) * P], XS[:, par, c * P:(c + 1) * P], ident)
                    mm.then_inc(xt_done, 1)
                    pe.matmul(bank[5][:, :], ones[0:16, :], ADP[0:16, 4 * g + t, :], start=True, stop=True).then_inc(bcast_done, 1)
                    pe.wait_ge(cb_ready, n + 1)
                    pe.wait_ge(xdt_ready, m + 1)
                    pe.matmul(bank[6][:, 0:P], BT, XDS, start=True, stop=True).then_inc(st_done, 1)
                    pe.wait_ge(m_ready, m + 1)
                    pe.wait_ge(st_ready, m + 1)
                    for hh in range(2):
                        q = slice(hh * 64, hh * 64 + 64)
                        pe.matmul(bank[7][q, 0:P], XDT[:, 0, par, q], SEG[:, 2 * hh, :], start=True, stop=True)
                        pe.matmul(bank[7][q, P:2 * P], XDT[:, 1, par, q], SEG[:, 2 * hh + 1, :], start=True, stop=False)
                        mm = pe.matmul(bank[7][q, P:2 * P], ST0[:, q], EX1[:, hh, :], start=False, stop=True)
                    mm.then_inc(y_done, 1)
                for t in range(4):
                    pe.wait_ge(yq_ready, 4 * n + t + 1)
                    mm = pe.matmul(bank[3][:, 256:512], ones, YQ4[:, t, :], start=(t == 0), stop=(t == 3))
                mm.then_inc(gss_done, 1)

        def ssm_scalar(act, l):
            with act.Fori(0, SSM_GROUPS) as g:
                n = 2 * l + g
                for q in range(2):
                    act.wait_ge(bc_conv, 2 * n + q + 1)
                    act.activation(BC[:, q, :], BC[:, q, :], ACT.Silu).then_inc(bc_ready, 1)
                for t in range(4):
                    m = 4 * n + t
                    par = t % 2
                    act.wait_ge(x_conv, m + 1)
                    act.activation(XS[:, par, :], CV, ACT.Silu).then_inc(x_ready, 1)
                    act.wait_ge(seg_ready, m + 1)
                    act.activation(SEG, SEG, ACT.Exp)
                    act.activation(EX1, bank[5][:, :].rearrange("p (h c l) -> p h c l", h=2, c=2)[:, :, 1, :],
                                   ACT.Exp).then_inc(ex_ready, 1)
                    act.wait_ge(st_done, m + 1)
                    act.activation(ST0, bank[6][:, 0:P], ACT.Copy).then_inc(st_ready, 1)
                    act.wait_ge(ys_ready, m + 2)
                    act.activation(YQ4[:, t, :], YS[:, t, :], ACT.Square).then_inc(yq_ready, 1)
                act.wait_ge(gss_done, n + 1)
                act.activation(RS, bank[3][:, 256:512], ACT.Sqrt, scale=1.0 / 512, bias=C["eps5"]).then_inc(gsd_ready, 1)

        def ssm_vector(v, l):
            L = LV[l]
            w = L["ssm_w"].rearrange("p (t k) -> p t k", k=4)
            bias = L["ssm_b"].unsqueeze(2)
            dskip = L["ssm_d"].unsqueeze(2)
            gain = L["ssm_g"].unsqueeze(2)

            def conv(o, x, t):
                return causal_conv(v, o, PRJ[:, x, :], lambda k: w[:, t, k:k + 1], bias[:, t, :])

            with v.Fori(0, SSM_GROUPS) as g:
                n = 2 * l + g
                v.drain()
                conv(BC[:, 0, :], XBC0 + 8 + g, 8 + g).then_inc(bc_conv, 1)
                conv(BC[:, 1, :], XBC0 + 10 + g, 10 + g).then_inc(bc_conv, 1)
                v.wait_ge(cb_done, n + 1)
                v.tensor_tensor(CBM, view(bank[2][:, 0:2 * P], 2), wide(C["causal"], 1, 2), ALU.mult)
                v.tensor_copy(BT, bank[3][:, 0:P]).then_inc(cb_ready, 1)
                for t in range(4):
                    m = 4 * n + t
                    par = t % 2
                    tile = 4 * g + t
                    v.drain()
                    conv(CV, XBC0 + tile, tile).then_inc(x_conv, 1)
                    v.wait_ge(xt_done, m + 1)
                    cols4 = COLS.rearrange("p a (n h) -> p a n h", h=2)
                    v.tensor_tensor(XDT[:, :, par, :].rearrange("p c (h d) -> p c h d", h=2),
                                    bank[4][:, 0:2 * P].rearrange("p (c h d) -> p c h d", c=2, h=2),
                                    wide(cols4[:, 0:2, tile, :], 3, 64), ALU.mult)
                    v.drain()
                    v.tensor_tensor(view(XDS, 2), view(XDT[:, 0, par, :], 2), wide(cols4[:, 4, tile, :], 2, 64),
                                    ALU.mult).then_inc(xdt_ready, 1)
                    v.wait_ge(bcast_done, m + 1)
                    for hh in range(2):
                        for c in range(2):
                            v.tensor_scalar(SEG[:, 2 * hh + c, :], bank[5][:, (2 * hh + c) * P:(2 * hh + c + 1) * P],
                                            cols4[:, 2 + c, tile, hh:hh + 1], 0.0, ALU.subtract, ALU.min)
                    v.drain().then_inc(seg_ready, 1)
                    v.wait_ge(ex_ready, m + 1)
                    seg = SEG.rearrange("p (h c) l -> p h c l", h=2)
                    v.tensor_tensor(seg, seg, wide(CBM, 1, 2), ALU.mult)
                    v.tensor_tensor(EX1, EX1, wide(BC[:, 1, P:2 * P], 1, 2), ALU.mult).then_inc(m_ready, 1)
                    v.wait_ge(y_done, m + 1)
                    v.scalar_tensor_tensor(YS[:, t, :], XS[:, par, :], dskip[:, tile, :], bank[7][:, 0:T], ALU.mult, ALU.add)
                    v.drain()
                    v.tensor_tensor(YS[:, t, :], YS[:, t, :], PRJ[:, Z0 + tile, :], ALU.mult).then_inc(ys_ready, 1)
                v.wait_ge(gsd_ready, n + 1)
                v.reciprocal(RS, RS)
                v.drain()
                for t in range(4):
                    v.scalar_tensor_tensor(MIX[:, 4 + 4 * g + t, :], YS[:, t, :], gain[:, 4 * g + t, :], RS,
                                           ALU.mult, ALU.mult)
            v.drain()

        def window_tensor(pe, l):
            pe.wait_ge(prj_all, l + 1)
            for c in range(2):
                mm = pe.transpose(bank[2][:, c * P:(c + 1) * P], PRJ[:, V0, c * P:(c + 1) * P], ident)
            mm.then_inc(vtk_mm, 1)
            with pe.Fori(0, 4) as m0:
                m = 4 * l + m0
                pe.wait_ge(qs_ready, m + 1)
                for hh in range(2):
                    q = slice(hh * 64, hh * 64 + 64)
                    for b in range(2):
                        mm = pe.matmul(bank[4 + hh][:, b * T:(b + 1) * T], QS[q, b * P:(b + 1) * P], PRJ[q, K0, :],
                                       start=True, stop=True)
                    mm.then_inc(sw_done, 1)
                for hh in range(2):
                    pe.wait_ge(sw_p, 2 * m + hh + 1)
                    for k, src in enumerate((0, T, T + P)):
                        mm = pe.transpose(bank[6 + hh][:, k * P:(k + 1) * P], SM[:, hh, src:src + P], ident)
                    mm.then_inc(sw_t, 1)
                pe.wait_ge(vtk_ready, l + 1)
                pe.wait_ge(sw_out, m + 1)
                for hh in range(2):
                    q = slice(hh * 64, hh * 64 + 64)
                    pe.wait_ge(sw_tc, 2 * m + hh + 1)
                    pe.matmul(bank[3][q, 0:P], VTK[:, 0, q], PT3[:, hh, 0:P], start=True, stop=True)
                    pe.matmul(bank[3][q, P:2 * P], VTK[:, 0, q], PT3[:, hh, P:2 * P], start=True, stop=False)
                    mm = pe.matmul(bank[3][q, P:2 * P], VTK[:, 1, q], PT3[:, hh, 2 * P:3 * P], start=False, stop=True)
                mm.then_inc(sw_pv, 1)

        def window_scalar(act, l):
            act.wait_ge(lru_done, l + 1)
            act.wait_ge(vtk_mm, l + 1)
            act.activation(VTK, view(bank[2][:, 0:2 * P], 2), ACT.Copy).then_inc(vtk_ready, 1)
            with act.Fori(0, 4) as m0:
                m = 4 * l + m0
                act.wait_ge(sw_out, m + 1)
                act.activation(QS, PRJ[:, Q0 + m0, :], ACT.Copy).then_inc(qs_ready, 1)
                for hh in range(2):
                    act.wait_ge(sw_max, 2 * m + hh + 1)
                    for b in range(2):
                        act.activation(SM[:, hh, b * T:(b + 1) * T], SM[:, hh, b * T:(b + 1) * T], ACT.Exp,
                                       bias=ST[:, 1, 2 * hh + b:2 * hh + b + 1], accum_out=ST[:, 2, 2 * hh + b:2 * hh + b + 1])
                    act.activation(ST[:, 3, 2 * hh:2 * hh + 2], ST[:, 3, 2 * hh:2 * hh + 2], ACT.Exp).then_inc(sw_exp, 1)
                for hh in range(2):
                    act.wait_ge(sw_t, 2 * m + hh + 1)
                    act.activation(PT3[:, hh, :], bank[6 + hh][:, 0:3 * P], ACT.Copy).then_inc(sw_tc, 1)

        def window_vector(v, l):
            sinks = LV[l]["sinks"].rearrange("p (m h) -> p m h", h=2)
            v.drain().then_inc(lru_done, 1)
            with v.Fori(0, 4) as m0:
                m = 4 * l + m0
                for hh in range(2):
                    c = slice(2 * hh, 2 * hh + 2)
                    v.drain()
                    v.wait_ge(sw_done, 2 * m + hh + 1)
                    v.scalar_tensor_tensor(SM[:, hh, :], bank[4 + hh][:, :], HALF_SCALE, WD["amask"], ALU.mult, ALU.add)
                    v.drain()
                    v.reduce_max(ST[:, 0, c], view(SM[:, hh, :], 2), AX_X)
                    v.drain()
                    v.tensor_scalar(ST[:, 1, c], ST[:, 0, c], sinks[:, m0, hh:hh + 1], -1.0, ALU.max, ALU.mult)
                    v.drain()
                    v.tensor_scalar(ST[:, 3, c], ST[:, 1, c], sinks[:, m0, hh:hh + 1], None, ALU.add).then_inc(sw_max, 1)
                for hh in range(2):
                    c = slice(2 * hh, 2 * hh + 2)
                    v.wait_ge(sw_exp, 2 * m + hh + 1)
                    v.tensor_tensor(ST[:, 2, c], ST[:, 2, c], ST[:, 3, c], ALU.add)
                    v.drain()
                    v.reciprocal(ST[:, 4, c], ST[:, 2, c])
                    v.drain()
                    v.tensor_tensor(view(SM[:, hh, :], 2), view(SM[:, hh, :], 2), wide(ST[:, 4, c], 2, T),
                                    ALU.mult).then_inc(sw_p, 1)
                v.wait_ge(sw_pv, m + 1)
                v.tensor_copy(MIX[:, 12 + m0, :], bank[3][:, 0:T]).then_inc(sw_out, 1)
            v.drain().then_inc(mix_ready, 1)

        def residual_vector(v, l):
            for i, j in turns(v, 8):
                n = i * RING + j
                b, _ = bank_of(f"out{l}", i, j)
                wait_done(v, f"out{l}", i, j)
                v.scalar_tensor_tensor(tmp[:, n, :], h[:, n, :], ALPHA, bank[b][:, 0:T], ALU.mult,
                                       ALU.add).then_inc(bank_free[b], 1)

        q8_ready, sc_done, sc_in = sem("q8_ready"), sem("sc_done"), sem("sc_in")
        gate_in, gate_exp = sem("gate_in"), sem("gate_exp")
        ijg_ready, ijt_done, pair_ready = sem("ijg_ready"), sem("ijt_done"), sem("pair_ready")
        hot = sem("hot")
        g_done = sem("g_done")
        g_in = sem("g_in")
        acc_zero = sem("acc_zero")
        u_done = sem("u_done")
        gp_ready = sem("gp_ready")
        G4 = G.rearrange("p j (n t) -> p n t j", t=4)
        GROUPS = T // 4

        def peer_units(e, name, unit, begin=None, middle=None):
            def step(i, j, more):
                n = UNITS * j + 2
                if more:
                    unit(i, j + 1, 0, unit_of(name, i, n), 2)
                if middle:
                    middle(i, j)
                if more:
                    unit(i, j + 1, 1, unit_of(name, i, n + 1), 3)
                    n += 2
                unit(i, j, 2, unit_of(name, i, n), n % UNITS)
                unit(i, j, 3, unit_of(name, i, n + 1), (n + 1) % UNITS)

            for q in range(2):
                unit(0, 0, q, unit_of(name, 0, q), q)
            if begin:
                begin()
            with e.Fori(0, BLOCKS // RING - 1) as i:
                for j in range(RING):
                    step(i, j, True)
            for j in range(RING):
                step(BLOCKS // RING - 1, j, j < RING - 1)

        def peer_tensor(pe, l):
            name = f"peer{l}"
            product3(pe, f"wq{l}", 4, h_hi, h_lo2, T, KT)
            pe.wait_ge(q8_ready, l + 1)
            for f in range(8):
                tt, hp = f // 4, f % 4
                if f >= 4:
                    pe.wait_ge(sc_in, 8 * l + f - 3)
                for a in range(2):
                    mm = pe.matmul(bank[2 + f % 4][:, a * 256:(a + 1) * 256], Q8[:, 2 * hp + a, tt * P:(tt + 1) * P],
                                   WD["keys"], start=True, stop=True)
                mm.then_inc(sc_done, 1)
            pe.wait_ge(ijg_ready, l + 1)
            for tt in range(2):
                for q in range(3):
                    mm = pe.transpose(bank[2 + tt][:, q * P:(q + 1) * P], IJG[:, q, tt * P:(tt + 1) * P], ident)
                mm.then_inc(ijt_done, 1)
            with pe.Fori(0, GROUPS // 2) as i:
                for half in range(2):
                    x = GROUPS * l + 2 * i + half
                    pe.wait_ge(hot, x + 1)
                    pe.wait_ge(g_in, x + 1)
                    for s in range(4):
                        mm = pe.matmul(bank[4 + half][:, s * P:(s + 1) * P], OHA[:, 4 * half + s, :],
                                       OHB[:, 4 * half + s, :], start=True, stop=True)
                    mm.then_inc(g_done, 1)

            def tensor_unit(i, j, q, n, buf):
                if q == 0:
                    b, use = bank_of(name, i, j)
                    pe.wait_ge(bank_free[b], use + 1)
                if q == 2:
                    pe.wait_ge(gp_ready, BLOCKS * l + RING * i + j + 3)
                    if j == 0:
                        pe.wait_ge(acc_zero, l + 1)
                pe.wait_ge(split_lo, n + 1)
                for m in range(4):
                    w = slice(m * P, (m + 1) * P)
                    w_hi, w_lo = SPLIT[:, buf, 0, w], SPLIT[:, buf, 1, w]
                    if q < 2:
                        k = 4 * q + m
                        mm = mm3(pe, bank[bank_of(name, i, j)[0]][:, 0:T], w_hi, w_lo, h_hi[:, k, :], h_lo2[:, k, :],
                                 k == 0, k == KT - 1)
                    else:
                        d = 4 * (q - 2) + m
                        mm = mm3(pe, bank[4 + d // 2][:, (d % 2) * T:(d % 2 + 1) * T], w_hi, w_lo, GPR[:, j % 2, 0, :],
                                 GPR[:, j % 2, 1, :], False, True, skip_group_check=True)
                mm.then_inc(unit_used, 1)

            peer_units(pe, name, tensor_unit)

        def peer_scalar(act, l):
            name = f"peer{l}"

            def drain_q(i, j):
                b, _ = bank_of(f"wq{l}", i, j)
                wait_product(act, f"wq{l}", i, j)
                act.activation(pairs(Q8)[:, j, :], bank[b][:, :], ACT.Copy).then_inc(bank_free[b], 1)

            ahead(act, 4, hi_chunk(act, f"wq{l}"), drain_q)
            act.drain().then_inc(q8_ready, 1)
            for f in range(8):
                act.wait_ge(sc_done, 8 * l + f + 1)
                act.activation(SC[:, 4 * f:4 * f + 4, :], view(bank[2 + f % 4][:, :], 4), ACT.Copy).then_inc(sc_in, 1)
            if l + 1 < DEPTH:
                act.dma_start(wide_t[:], A["wide"][l + 1]).then_inc(wide_in, 16)
            act.wait_ge(gate_in, l + 1)
            act.activation(IJG[:, 0, :], IJG[:, 0, :], ACT.Exp).then_inc(gate_exp, 1)
            for tt in range(2):
                act.wait_ge(ijt_done, 2 * l + tt + 1)
                a = act.activation(PAIR[:, :, tt * P:(tt + 1) * P], view(bank[2 + tt][:, 0:3 * P], 3), ACT.Copy)
            a.then_inc(pair_ready, 1)
            with act.Fori(0, GROUPS // 2) as i:
                for half in range(2):
                    act.wait_ge(g_done, GROUPS * l + 2 * i + half + 3)
                    act.activation(G4[:, 2 * i + half], view(bank[4 + half][:, :], 4), ACT.Copy).then_inc(g_in, 1)

            def gelu(i, j):
                b, _ = bank_of(name, i, j)
                act.wait_ge(unit_used, unit_of(name, i, UNITS * j) + UNITS)
                act.wait_ge(gp_ready, BLOCKS * l + RING * i + j + 2)
                act.activation(GA, bank[b][:, 0:T], ACT.Gelu).then_inc(bank_free[b], 1)

            peer_units(act, name, lambda *a: hi_quarter(act, name, *a),
                       begin=lambda: act.wait_ge(unit_used, unit_of(name, 0, 2) + UNITS), middle=gelu)

        def top16(v, n, width):
            for a in range(2):
                v.max(V16[:, a, 0:8], WK[:, a, 0, 0:width])
            v.drain()
            for a in range(2):
                v.max_index(I16[:, a, 0:8], V16[:, a, 0:8], WK[:, a, 0, 0:width])
                v.match_replace(WK[:, a, 1, 0:width], V16[:, a, 0:8], WK[:, a, 0, 0:width], -3.0e38)
            v.drain()
            for a in range(2):
                v.max(V16[:, a, 8:16], WK[:, a, 1, 0:width])
            v.drain()
            for a in range(2):
                v.max_index(I16[:, a, 8:16], V16[:, a, 8:16], WK[:, a, 1, 0:width])
            v.drain()

        def peer_vector(v, l):
            name = f"peer{l}"
            rows2 = lambda ap: ap.rearrange("p (n a) k -> p n a k", a=2)
            work = lo_chunk(v, f"wq{l}")
            for j in range(4):
                work(0, j)
            v.wait_ge(sc_in, 8 * (l + 1))
            with v.Fori(0, ROWS) as i:
                v.tensor_copy(WK[:, :, 0, 0:NKEYS], rows2(SC)[:, i])
                v.drain()
                top16(v, i, NKEYS)
                v.tensor_copy(rows2(TV)[:, i], V16)
                v.tensor_copy(rows2(TIU)[:, i], I16)
            v.drain()
            tv4 = TV.rearrange("p (n a m) k -> p n a m k", a=2, m=2)
            with v.Fori(0, NR // 2) as i:
                for a in range(2):
                    v.tensor_tensor(view(WK[:, a, 0, :], TOPK), wide(tv4[:, i, a, 0, :], 2, TOPK),
                                    wide(tv4[:, i, a, 1, :], 1, TOPK), ALU.add)
                v.drain()
                top16(v, i, TOPK * TOPK)
                v.tensor_copy(rows2(BV)[:, i], V16)
                v.tensor_copy(rows2(BPU)[:, i], I16)
            v.drain()
            g0 = view(IJG[:, 0, :], NR)
            v.tensor_tensor(g0, BV, wide(BV[:, :, 0], 2, TOPK), ALU.subtract).then_inc(gate_in, 1)
            bp = BPU.rearrange("p a b -> p (a b)")
            v.tensor_scalar(PAU[:, 0, :], bp, 4, None, ALU.logical_shift_right)
            v.tensor_scalar(PAU[:, 1, :], bp, 15, None, ALU.bitwise_and)
            v.tensor_copy(TIF, TIU)
            v.drain()
            v.tensor_copy(PAF, PAU)
            tif = TIF.rearrange("p (n m) k -> p n m k", m=2)
            eq, eq2 = EQ.rearrange("p n (k a) -> p (n k) a", a=TOPK), EQ2.rearrange("p n (k a) -> p (n k) a", a=TOPK)
            for m in range(2):
                v.drain()
                v.tensor_tensor(eq, wide(PAF[:, m, :], 2, TOPK), wide(iota[:, 0:TOPK], 1, NR * TOPK), ALU.is_equal)
                v.drain()
                v.tensor_tensor(EQ2.rearrange("p n (k a) -> p n k a", a=TOPK), EQ.rearrange("p n (k a) -> p n k a", a=TOPK),
                                wide(tif[:, :, m, :], 2, TOPK), ALU.mult)
                v.drain()
                v.reduce_sum(IJG[:, 1 + m, :], eq2, AX_X)
            v.wait_ge(gate_exp, l + 1)
            v.reduce_sum(MXS[:, 0, :], g0, AX_X)
            v.drain()
            v.reciprocal(MXS[:, 1, :], MXS[:, 0, :])
            v.drain()
            v.tensor_tensor(g0, g0, wide(MXS[:, 1, :], 2, TOPK), ALU.mult)
            v.drain().then_inc(ijg_ready, 1)
            v.wait_ge(pair_ready, l + 1)
            pair = PAIR.rearrange("p q (n t) -> p q n t", t=8).unsqueeze(4)
            with v.Fori(0, GROUPS // 2) as i:
                for half in range(2):
                    v.wait_ge(g_done, GROUPS * l + 2 * i + half + 1)
                    for s in range(4):
                        t = 4 * half + s
                        v.tensor_scalar(OHA[:, t, :], iota, pair[:, 1, i, t, :], pair[:, 0, i, t, :],
                                        ALU.is_equal, ALU.mult)
                        a = v.tensor_scalar(OHB[:, t, :], iota, pair[:, 2, i, t, :], None, ALU.is_equal)
                    a.then_inc(hot, 1)
            v.wait_ge(g_in, GROUPS * (l + 1) + 2)
            for b in range(4, 8):
                a = v.memset(bank[b][:, :], 0.0)
            a.then_inc(acc_zero, 1)

            def gate(i, j):
                b, use = bank_of(name, i, j)
                v.wait_ge(bank_free[b], use + 2)
                v.wait_ge(unit_used, unit_of(name, i, UNITS * j - 2) + UNITS)
                g_hi, g_lo = GPR[:, j % 2, 0, :], GPR[:, j % 2, 1, :]
                v.tensor_tensor(GA, GA, G[:, i * RING + j, :], ALU.mult)
                v.drain()
                v.tensor_copy(g_hi, GA)
                v.drain()
                v.tensor_tensor(g_lo, GA, g_hi.bitcast(F32), ALU.subtract).then_inc(gp_ready, 1)

            peer_units(v, name, lambda i, j, q, n, buf: lo_quarter(v, name, i, j, q, n, buf, q == 3), middle=gate)
            v.wait_ge(unit_used, unit_of(name, 0, UNITS * BLOCKS) + UNITS)
            for b in range(4):
                v.scalar_tensor_tensor(pairs(tmp)[:, b, :], pairs(h_hi)[:, b, :].bitcast(F32), ALPHA, bank[4 + b][:, :],
                                       ALU.mult, ALU.add)
            v.drain()
            for b in range(4):
                v.scalar_tensor_tensor(pairs(tmp)[:, b, :], pairs(h_lo2)[:, b, :].bitcast(F32), ALPHA,
                                       pairs(tmp)[:, b, :], ALU.mult, ALU.add)

        block = ctx.enter_context(nc.Block())

        SETUP = 16 * 7

        @block.sync
        def _(sp):
            for dst, src in ((const_t[:], A["const"]), (vec_t, A["vec"]), (lay_t[0][:], A["lay"][0]),
                             (lay_t[1][:], A["lay"][1]), (hyc_t, A["hyc"]), (W4[0:64], A["w4"]), (X, A["xin"])):
                sp.dma_start(dst, src).then_inc(setup_in, 16)
            sp.dma_start(wide_t[:], A["wide"][0]).then_inc(wide_in, 16)
            stream(sp, "ada", A["w_ada"], 24)
            hyena_sync(sp, A["w_hy"], A["decay"])
            stream(sp, "hy_out", A["w_hyout"], 8)
            stream(sp, "kv", A["w_kv"], 4)
            stream(sp, "q", A["w_q"], 8)
            stream(sp, "z", A["w_z"], 8)
            stream(sp, "at_out", A["w_atout"], 8)
            for l in range(DEPTH):
                stream(sp, f"proj{l}", A[f"w_proj{l}"], 17)
                stream(sp, f"out{l}", A[f"w_out{l}"], 8)
                stream(sp, f"wq{l}", A[f"w_wq{l}"], 4)
                stream(sp, f"peer{l}", A[f"w_peer{l}"], BLOCKS)
            sp.wait_ge(h_new, 2 * DEPTH + 1)
            sp.dma_start(out, h).then_inc(stored, 16)
            sp.wait_ge(stored, 16)

        @block.gpsimd
        def _(pool):
            pool.wait_ge(h_ready, 4)
            pool.dma_start(rope_t, A["rope"]).then_inc(rope_in, 16)

        @block.scalar
        def _(act):
            ada_scalar(act)
            filter_scalar(act)
            rms_scalar(act, 0)
            hyena_scalar(act)
            rms_scalar(act, 1)
            kv_scalar(act)
            gather(act, "q", pairs(QR), ACT.Copy, 8)
            prep_scalar(act)
            gather(act, "z", pairs(ZG), ACT.Silu, 8)
            heads_scalar(act)
            norm_scalar(act, 0, PRJ[:, 0:8, :])
            for l in range(DEPTH):
                proj_scalar(act, l)
                lru_scalar(act, l)
                rows_scalar(act, l)
                ssm_scalar(act, l)
                window_scalar(act, l)
                norm_scalar(act, 2 * l + 1, tmp)
                peer_scalar(act, l)
                norm_scalar(act, 2 * l + 2, tmp)

        @block.vector
        def _(v):
            filter_vector(v)
            ada_vector(v)
            rms_vector(v, 0)
            hyena_vector(v)
            add_gated(v, "hy_out", 0, 2)
            rms_vector(v, 1)
            prep_vector(v)
            heads_vector(v)
            add_gated(v, "at_out", 1, 1)
            norm_vector(v, 0, X[:, :, 0:T], PRJ[:, 0:8, :], V1["emb_g"], V1["emb_b"], h, (h_hi, h_lo1))
            v.sem_inc(ys_ready, 1)
            v.sem_inc(sw_out, 1)
            v.sem_inc(gp_ready, 2)
            for l in range(DEPTH):
                lru_vector(v, l)
                rows_vector(v, l)
                ssm_vector(v, l)
                window_vector(v, l)
                residual_vector(v, l)
                norm_vector(v, 2 * l + 1, tmp, tmp, LV[l]["ln1_g"], LV[l]["ln1_b"], h, (h_hi, h_lo2))
                peer_vector(v, l)
                norm_vector(v, 2 * l + 2, tmp, tmp, LV[l]["ln2_g"], LV[l]["ln2_b"], h,
                            (h_hi, h_lo1) if l < DEPTH - 1 else None)

        @block.tensor
        def _(pe):
            for s in chunk_done:
                pe.sem_inc(s, 1)
            for s in bank_free:
                pe.sem_inc(s, 1)
            pe.sem_inc(unit_used, UNITS)
            filter_tensor(pe)
            ada_tensor(pe)
            rms_tensor(pe, 0)
            hyena_tensor(pe)
            pe.wait_ge(yg_done, CT + 1)
            product(pe, "hy_out", 8, YG, T2, 16)
            rms_tensor(pe, 1)
            kv_tensor(pe)
            product(pe, "q", 8, H1[:, :, 0:T], T, KT)
            prep_tensor(pe)
            product(pe, "z", 8, H1[:, :, 0:T], T, KT)
            heads_tensor(pe)
            pe.wait_ge(og_done, HEADS + 2)
            product(pe, "at_out", 8, OG, T, 16)
            norm_tensor(pe, 0, X)
            pe.sem_inc(rg_act, 2)
            pe.sem_inc(g_done, 2)
            pe.sem_inc(g_in, 2)
            for l in range(DEPTH):
                proj_tensor(pe, l)
                lru_tensor(pe, l)
                rows_tensor(pe, l)
                ssm_tensor(pe, l)
                window_tensor(pe, l)
                pe.wait_ge(mix_ready, l + 1)
                product(pe, f"out{l}", 8, MIX, T, 16)
                norm_tensor(pe, 2 * l + 1, tmp)
                peer_tensor(pe, l)
                norm_tensor(pe, 2 * l + 2, tmp)


def tiles(w, order, kt):
    k, n = w.shape
    t = w.reshape(kt, P, n // P, P).transpose(2, 1, 0, 3)[list(order)].reshape(len(order), P, kt * P)
    per = CHUNK // (kt * P)
    return np.ascontiguousarray(t.reshape(-1, per, P, kt * P).transpose(0, 2, 1, 3).reshape(-1, P, CHUNK))


def cols(v):
    return np.asarray(v).reshape(-1, P).T


def rows_to(a, rows=P):
    a = np.asarray(a)
    return np.concatenate([a, np.zeros((rows - a.shape[0],) + a.shape[1:], a.dtype)], 0) if a.shape[0] < rows else a


def constants():
    f = np.float32
    s = np.arange(P)
    q, k = np.arange(P)[:, None], np.arange(T)[None, :]
    block0 = (k <= q)
    block1 = np.where(k < P, k > q, k - P <= q)
    amask = np.where(np.stack([block0, block1], 1), 0.0, -1e30).astype(f)
    const = np.concatenate([np.eye(P), np.ones((P, P)), np.tile(s, (P, 1)), (s[:, None] <= s[None, :]),
                            np.full((P, 1), 1e-6), np.full((P, 1), 1e-5)], 1).astype(f)
    t, fr = np.arange(T)[:, None], np.arange(T)[None, :]
    ang = 2 * np.pi * ((t * fr) % T2) / T2
    alt = (-1.0) ** np.arange(T)
    re, sn = np.cos(ang), -np.sin(ang)
    im = sn.copy()
    im[:, 0] = alt
    rex = re[:, 0:P].copy()
    rex[:, 0] = alt
    ire = np.cos(ang).T * (2.0 / T2)
    ire[0] /= 2
    iim = -np.sin(ang).T * (2.0 / T2)
    iim[0] = alt / T2
    split = lambda m: m.reshape(2, P, -1).transpose(1, 0, 2).reshape(P, -1)
    lin = np.linspace(0.0, 1.0, T, dtype=f)[:, None]
    wv = (f(2 * np.pi) * np.arange(T, dtype=f)[:, None] / f(T)).astype(f)
    bands = np.linspace(1e-4, 15, 16, dtype=f)[None, :]
    arg = (bands * wv).astype(f)
    z = np.concatenate([lin, np.cos(arg), -np.sin(arg)], 1).astype(f).T
    hyc = np.concatenate([split(re), split(im), split(sn), split(rex), split(ire), split(iim), rows_to(z)], 1).astype(f)
    lo, hi = np.log(1e-2) / 1.5, np.log(1e-2) / 0.3
    deltas = np.abs(np.linspace(lo, hi, E_HY, dtype=f))
    dec = np.exp(-lin * deltas[None, :]).astype(f)
    back = dec.copy()
    back[0] = 0
    d = np.stack([dec, back], 1).reshape(2, P, 2, CT, P).transpose(3, 1, 0, 2, 4).reshape(CT, P, 512)
    inv = (1.0 / (10000.0 ** (np.arange(0, 64, 2, dtype=f) / f(64)))).astype(f)
    row, col = (np.arange(T) // 64).astype(f), (np.arange(T) % 64).astype(f)
    angle = np.concatenate([row[:, None] * inv, row[:, None] * inv, col[:, None] * inv, col[:, None] * inv], 1)
    rot = np.zeros((P, P))
    for base in (0, 64):
        for c in range(32):
            rot[base + c + 32, base + c] = -1
            rot[base + c, base + c + 32] = 1
    rope = np.concatenate([np.cos(angle.astype(f)).T, np.sin(angle.astype(f)).T, rot], 1).astype(f)
    return const, amask.reshape(P, -1), hyc, np.ascontiguousarray(d.astype(f)), rope


def layout(a):
    f = np.float32
    one = lambda v: rows_to(np.asarray(v).reshape(-1, 1))
    const, amask, hyc, decay, rope = constants()
    x = np.concatenate([a["x"][0].T.reshape(KT, P, T), a["ctx"][0].T.reshape(KT, P, T)], 2).transpose(1, 0, 2)
    inner = CT
    conv_w = a["hy_conv_w"][0].reshape(3, 3, CT, P)[:, [1, 2, 0]]
    conv_b = a["hy_conv_b"][0].reshape(3, CT, P)[[1, 2, 0]]
    vec = np.concatenate([
        np.stack([cols(a["c"][0]), cols(a["c_ctx"])], 2).reshape(P, 16),
        np.concatenate([cols(a["norm_g"][l]) for l in range(2)], 1),
        np.concatenate([cols(a["ada_b"][l]) for l in range(2)], 1),
        conv_w.transpose(3, 2, 1, 0).reshape(P, 144), conv_b.transpose(2, 1, 0).reshape(P, 48),
        cols(a["hy_d"][0]), one(a["at_q_g"][0]), one(a["at_k_g"][0]),
        one(a["hy_fb1"][0]), one(a["hy_fb2"][0]), one(a["hy_fb3"][0]), one(a["hy_freq"][0]),
        cols(a["emb_ln_g_2"]), cols(a["emb_ln_b_2"]),
        rows_to(a["hy_fw1"][0]), rows_to(a["hy_fw2"][0]), rows_to(a["hy_fw3"][0])], 1)
    lay, wide = [], []
    for l in range(DEPTH):
        wax = np.zeros((2, LRU_T, P, P), f)
        for m, name in enumerate(("rg_wa_2", "rg_wx_2")):
            for b in range(8):
                o = 64 * (b % 2)
                wax[m, b // 2, o:o + 64, o:o + 64] = a[name][l, b]
        keys = np.zeros((P, 256), f)
        keys[0:64, 0:P] = a["peer_keys_2"][l, 0].T
        keys[64:P, P:] = a["peer_keys_2"][l, 1].T
        lay.append(np.concatenate([
            a["rg_conv_w_2"][l].reshape(4, LRU_T, P).transpose(2, 1, 0).reshape(P, 16), cols(a["rg_conv_b_2"][l]),
            cols(a["rg_ba_2"][l]), cols(a["rg_bx_2"][l]), cols(a["rg_lambda_2"][l]),
            a["ssm_conv_w_2"][l].reshape(4, XBC_T, P).transpose(2, 1, 0).reshape(P, 48), cols(a["ssm_conv_b_2"][l]),
            one(a["ssm_dt_bias_2"][l]), one(a["ssm_a_log_2"][l]), cols(np.repeat(a["ssm_d_2"][l], 64)),
            cols(a["ssm_norm_g_2"][l]), cols(a["ln1_g_2"][l]), cols(a["ln1_b_2"][l]), cols(a["ln2_g_2"][l]),
            cols(a["ln2_b_2"][l]), np.tile(a["attn_sinks_2"][l][[0, 4, 1, 5, 2, 6, 3, 7]][None], (P, 1))], 1))
        wide.append(np.concatenate([
            a["w_in_2"][l][:, 3584:3600].reshape(KT, P, 16).transpose(1, 0, 2).reshape(P, 128), keys,
            wax.transpose(2, 0, 1, 3).reshape(P, 1024), amask], 1))
    hy = [t for c in range(CT) for t in (CT + c, 2 * CT + c, c, 3 * CT + c)]
    w4 = a["hy_fw4"][0].reshape(64, 2, CT, P).transpose(0, 2, 1, 3).reshape(64, CT, 256)
    at = a["at_w_in"][0]
    arrays = {
        "const": const, "vec": vec, "lay": np.stack(lay), "wide": np.stack(wide), "hyc": hyc, "decay": decay, "rope": rope, "w4": w4, "xin": x,
        "w_ada": a["ada_w"].reshape(2, KT, P, 12, 256).transpose(0, 3, 2, 1, 4).reshape(24, P, CHUNK),
        "w_hy": tiles(a["hy_w_in"][0], hy, KT), "w_hyout": tiles(a["hy_w_out"][0], range(8), 16),
        "w_kv": tiles(at, [t for g in range(4) for t in (16 + g, 20 + g)], KT),
        "w_q": tiles(at, range(16), KT), "w_z": tiles(at, range(24, 40), KT),
        "w_atout": tiles(a["at_w_out"][0], range(8), 16),
    }
    for l in range(DEPTH):
        w = a["w_in_2"][l]
        heads = [hd for m in range(4) for hd in (m, m + 4)]
        wq = w[:, 3600:4112].reshape(D, 8, 64)[:, heads].reshape(D, 512)
        wcat = np.concatenate([w[:, 0:512], w[:, 2048:3584], wq, w[:, 4112:4368], w[:, 512:2048]], 1)
        arrays[f"w_proj{l}"] = tiles(wcat, range(34), KT)
        wo = a["w_out_2"][l]
        wo = np.concatenate([wo[0:1536], wo[1536:].reshape(8, 64, D)[heads].reshape(512, D)], 0)
        arrays[f"w_out{l}"] = tiles(wo, range(8), 16)
        arrays[f"w_wq{l}"] = tiles(a["peer_wq_2"][l], range(8), KT)
        u = a["peer_u_2"][l].reshape(P, BLOCKS, KT, P).transpose(1, 3, 2, 0).reshape(BLOCKS, P, D)
        v = a["peer_v_2"][l].reshape(P, BLOCKS, D).transpose(1, 0, 2)
        arrays[f"w_peer{l}"] = np.concatenate([u, v], 2)
    return {k: np.ascontiguousarray(v) for k, v in arrays.items()}


def kernel(**inputs):
    import concourse.bacc as bacc
    from concourse.bass_utils import run_bass_kernel_spmd

    arrays = layout({k: np.asarray(v) for k, v in inputs.items()})
    nc = bacc.Bacc("TRN2", target_bir_lowering=False, num_devices=1)
    handles = {k: nc.dram_tensor(f"in_{k}", v.shape, F32, kind="ExternalInput").ap() for k, v in arrays.items()}
    out = nc.dram_tensor("out_h", (P, KT, T), F32, kind="ExternalOutput").ap()
    program(nc, handles, out)
    r = run_bass_kernel_spmd(nc, [{f"in_{k}": v for k, v in arrays.items()}], core_ids=[0])
    return r.results[0]["out_h"].transpose(2, 1, 0).reshape(1, T, D)
```

```python
from contextlib import ExitStack

import numpy as np

import concourse.bass as bass
from concourse import mybir

ALU = mybir.AluOpType
ACT = mybir.ActivationFunctionType
AX_X = mybir.AxisListType.X
F32 = mybir.dt.float32
F32R = mybir.dt.float32r
U32 = mybir.dt.uint32

P = 128
D = 1024
T = 256
T2 = 2 * T
KT = D // P
DEPTH = 2
CHUNK = 2048
UNITS = 4
UNIT = CHUNK // UNITS
RING = 4
E_HY = 2 * D
CT = E_HY // P
HEADS, KV_HEADS = 16, 4
LRU_T, XBC_T, Z_T, Q_T = 4, 12, 8, 4
SSM_HEADS, SSM_GROUPS = 16, 2
PEER_HEADS, NKEYS, TOPK = 8, 128, 16
ROWS = 2 * PEER_HEADS
TOP = 16
BLOCKS = NKEYS
ALPHA = (2 * DEPTH) ** 0.25
LOG1P_TERMS = [1.0 / n for n in (15, 13, 11, 9, 7, 5, 3)]

CONST = [("ident", P), ("ones", P), ("iota", P), ("causal", P), ("eps6", 1), ("eps5", 1)]
HYC = [("re", 2 * T), ("im", 2 * T), ("sn", 2 * T), ("rex", 2 * P), ("ire", 2 * T), ("iim", 2 * T),
       ("z", T)]
ROPE = [("cos", T), ("sin", T), ("rot", P)]
VEC1 = [("c", 16), ("norm_g", 16), ("ada_b", 48), ("conv_w", 144), ("conv_b", 48), ("hy_d", 16), ("q_g", 1),
        ("k_g", 1), ("fb", 3), ("freq", 1), ("emb_g", 8), ("emb_b", 8), ("fw", 192)]
LAYER = [("rg_w", 16), ("rg_b", 4), ("ba", 4), ("bx", 4), ("lam", 4), ("ssm_w", 48), ("ssm_b", 12),
         ("dt_bias", 1), ("a_log", 1), ("ssm_d", 8), ("ssm_g", 8), ("ln1_g", 8), ("ln1_b", 8), ("ln2_g", 8),
         ("ln2_b", 8), ("sinks", 8)]
WIDE = [("w_dt", 128), ("keys", 256), ("rg_wax", 1024), ("amask", 2 * T)]


def columns(table):
    at, out = 0, {}
    for name, n in table:
        out[name] = (at, n)
        at += n
    return out, at


class Uses:

    def __init__(self, n):
        self.n, self.base = n, 0

    def at(self, off, i=0, per=0):
        k = self.base + off
        return k % self.n, (k // self.n + i * (per // self.n) if per else k // self.n)


def program(nc, A, out):
    ctx = ExitStack()
    with ctx:
        def sb(name, shape, dt=F32):
            return ctx.enter_context(nc.sbuf_tensor(name, shape, dt))

        def sem(name):
            return ctx.enter_context(nc.semaphore(name))

        def sems(name, n):
            return [sem(f"{name}{i}") for i in range(n)]

        def table(name, layout):
            at, n = columns(layout)
            t = sb(name, [P, n])
            return t, {k: t[:, a:a + m] for k, (a, m) in at.items()}

        wring = sb("wring", [P, RING, CHUNK])
        const_t, C = table("const_t", CONST)
        wide_t, WD = table("wide_t", WIDE)
        lay_t, LV = [], []
        for l in range(DEPTH):
            t, v = table(f"lay{l}_t", LAYER)
            lay_t.append(t)
            LV.append(v)
        ident, ones, iota = C["ident"], C["ones"], C["iota"]

        RES, VEC = 2 * KT * T, columns(VEC1)[1]
        ARENA = 38160
        base = -(-nc.sbuf_base // 32) * 32
        sb("slab", [P, RES + ARENA])
        res = nc.alloc_sbuf_tensor_at("res", [P, RES], F32, offset=base)
        res_r = nc.alloc_sbuf_tensor_at("res_r", [P, RES], F32R, offset=base)
        arena = nc.alloc_sbuf_tensor_at("arena", [P, ARENA], F32, offset=base + 4 * RES)

        def arena_r(name, at, words):
            return nc.alloc_sbuf_tensor_at(name, [P, words], F32R, offset=base + 4 * (RES + at))

        vec_t = arena[:, ARENA - VEC:]
        V1 = {k: vec_t[:, a:a + m] for k, (a, m) in columns(VEC1)[0].items()}

        class Carve:
            def __init__(self, at=0, mem=arena):
                self.at, self.mem = at, mem

            def take(self, *shape):
                n = int(np.prod(shape))
                ap = self.mem[:, self.at:self.at + n]
                self.at += n
                assert self.at <= ARENA, self.at
                if len(shape) == 2:
                    ap = ap.rearrange("p (a b) -> p a b", a=shape[0])
                if len(shape) == 3:
                    ap = ap.rearrange("p (a b c) -> p a b c", a=shape[0], b=shape[1])
                if len(shape) == 4:
                    ap = ap.rearrange("p (a b c d) -> p a b c d", a=shape[0], b=shape[1], c=shape[2])
                return ap

        def view(ap, a):
            return ap.rearrange("p (a b) -> p a b", a=a)

        bank = [ctx.enter_context(nc.psum_tensor(f"bank{b}", [P, 512], F32)) for b in range(8)]

        H1_R = view(arena_r("h1_r", 0, 2 * KT * T2)[:, :], 2 * KT)
        H1_HI, H1_LO = H1_R[:, 0:KT, :], H1_R[:, KT:, :]
        c1 = Carve(2 * KT * T2)
        YG_AT = c1.at
        YG = c1.take(CT, T2)
        YG_HI = H1_R
        YG_LO = view(arena_r("yg_r", YG_AT, CT * T2)[:, :], CT)
        hyc_at, hyc_n = columns(HYC)
        hyc_t = c1.take(hyc_n)
        HC = {k: hyc_t[:, a:a + m] for k, (a, m) in hyc_at.items()}
        DEC = c1.take(2, 768)
        KB = c1.take(512)
        KSD = c1.take(2, 256)
        KABS = c1.take(512)
        UT = c1.take(512)
        KSPEC = c1.take(5, P)
        KNORM = c1.take(2)
        PR4_AT = c1.at
        PR4 = c1.take(4, 512)
        CX = c1.take(3, 512)
        U = c1.take(512)
        ZS1 = c1.take(512)
        YT = c1.take(2, 512)
        HSIN = c1.take(T)
        end1 = c1.at
        ADAROW = arena[:, YG_AT:YG_AT + 2 * 3072]
        HF = Carve(YG_AT + 2 * 3072).take(4, T)
        KEEP1 = arena[:, BLOCKS * T + 2 * UNITS * UNIT:][:, 0:P]
        adac = KEEP1[:, 0:96].rearrange("p (l n s) -> p l n s", l=2, n=24)
        adag = KEEP1[:, 96:128].rearrange("p (l k s) -> p l k s", l=2, k=8)
        SILC = HF[:, 3, 0:16].rearrange("p (k s) -> p k s", s=2)
        SQ1 = arena[:, 0:KT * T2].rearrange("p (k t) -> p k t", k=KT)
        RS1 = KB
        TM1 = Carve(PR4_AT).take(KT, T2)
        assert PR4_AT + KT * T2 <= BLOCKS * T

        c2 = Carve(2 * KT * T2)
        KR = c2.take(KV_HEADS, T2)
        VR = c2.take(KV_HEADS, T2)
        QR = c2.take(HEADS, T)
        ZG = c2.take(HEADS, T)
        SQA = c2.take(512)
        RSA = c2.take(512)
        QN = c2.take(512)
        RT1 = c2.take(512)
        RT2 = c2.take(512)
        QF = c2.take(512)
        VS = c2.take(4, P)
        PRB = c2.take(4, 512)
        PTR = c2.take(4, 512)
        STAT = c2.take(4, 4)
        rope_at, rope_n = columns(ROPE)
        rope_t = c2.take(rope_n)
        RO = {k: rope_t[:, a:a + m] for k, (a, m) in rope_at.items()}
        assert max(c2.at, end1) <= BLOCKS * T, (c2.at, end1)
        OG = arena[:, 0:HEADS * T].rearrange("p (h t) -> p h t", h=HEADS)
        og_r = H1_R.rearrange("p a t -> p (a t)")
        OG_LO, OG_HI = view(og_r[:, 0:HEADS * T], HEADS), view(og_r[:, HEADS * T:2 * HEADS * T], HEADS)

        c3 = Carve()
        SQ = c3.take(KT, T)
        MU = c3.take(T)
        RS = c3.take(T)
        PRJ_AT = c3.at
        PRJ = c3.take(34, T)
        MIX_AT = c3.at
        MIX = c3.take(16, T)
        RG_AT = c3.at
        RG = c3.take(6, 4 * T)
        SP = c3.take(6, 4 + T)
        SROW = c3.take(4, T)
        AD = c3.take(SSM_HEADS, T)
        COLS = c3.take(5, SSM_HEADS)
        BC = c3.take(2, T)
        CBM = c3.take(2, P)
        BT = c3.take(P)
        XS = c3.take(2, T)
        CV = c3.take(T)
        XDT = c3.take(2, 2, P)
        XDS = c3.take(P)
        ST0 = c3.take(P)
        SEG = c3.take(2, 4, P)
        EX1 = c3.take(2, 2, P)
        end3 = c3.at
        MIX_LO = view(arena_r("mix_lo", MIX_AT, 16 * T)[:, :], 16)
        MIX_HI = view(arena_r("mix_hi", PRJ_AT, 16 * T)[:, :], 16)
        YS = SQ[:, 0:4, :]
        YQ4 = SQ[:, 4:8, :]
        ADP = AD.rearrange("p (n h) t -> p n (h t)", h=2)
        QS = RG[:, 0, 0:2 * T].rearrange("p (a b) -> p a b", a=2)
        SM = [RG[:, n, :].rearrange("p (a b) -> p a b", a=2) for n in (1, 5)]
        PT3 = RG[:, 2:3, 0:768].rearrange("p a (b c) -> p (a b) c", b=2)
        VTK = RG[:, 3, 0:256].rearrange("p (a b) -> p a b", a=2)
        ST = [RG[:, 4, 64 * n:64 * n + 64].rearrange("p (a b) -> p a b", a=8) for n in range(2)]

        G = arena[:, 0:BLOCKS * T].rearrange("p (j t) -> p j t", j=BLOCKS)
        c5 = Carve(0, arena_r("peer_r", BLOCKS * T, 2 * UNITS * UNIT + 4 * T))
        SPLIT = c5.take(UNITS, 2, UNIT)
        GPR = c5.take(2, 2, T)
        GA = Carve(BLOCKS * T + c5.at).take(T)
        c5 = Carve(BLOCKS * T)
        OHA = c5.take(8, P)
        OHB = c5.take(8, P)
        PAIR = c5.take(3, T)
        assert end3 <= BLOCKS * T
        c6 = Carve()
        Q8 = c6.take(PEER_HEADS, T)
        SC = c6.take(2 * ROWS, NKEYS)
        TV = c6.take(2 * ROWS, TOPK)
        TIU = c6.take(2 * ROWS, TOPK).bitcast(U32)
        TIF = c6.take(2 * ROWS, TOPK)
        WK = c6.take(TOP, 2, 256)
        V16 = c6.take(TOP, TOPK)
        I16 = c6.take(TOP, TOPK).bitcast(U32)
        NR = 2 * PEER_HEADS
        BV = c6.take(NR, TOPK)
        BPU = c6.take(NR, TOPK).bitcast(U32)
        PAU = c6.take(2, NR * TOPK).bitcast(U32)
        PAF = c6.take(2, NR * TOPK)
        EQ = c6.take(NR, TOPK * TOPK)
        EQ2 = c6.take(NR, TOPK * TOPK)
        IJG = c6.take(3, NR * TOPK)
        MXS = c6.take(3, NR)

        X = view(res[:, :], KT)
        h = view(res[:, 0:KT * T], KT)
        tmp = view(res[:, KT * T:], KT)
        h_hi = view(res_r[:, KT * T:], KT)
        h_lo1 = view(arena_r("h_lo1", MIX_AT + 8 * T, KT * T)[:, :], KT)
        h_lo2 = view(res_r[:, 0:KT * T], KT)

        setup_in = sem("setup_in")
        lru_done = sem("lru_done")
        w_landed = sems("w_landed", RING)
        chunk_done = sems("chunk_done", RING)
        split_hi = sem("split_hi")
        split_lo = sem("split_lo")
        unit_used = sem("unit_used")
        wide_in = sem("wide_in")
        part_hi = sem("part_hi")
        part_lo = sem("part_lo")
        bank_free = sems("bank_free", 2)
        dec_landed = sems("dec_landed", 2)
        dec_free = sems("dec_free", 2)
        ada_rows = sem("ada_rows")
        silc_ready = sem("silc_ready")
        ada_cols = sem("ada_cols")
        mod_ready = sem("mod_ready")
        sq_ready = sem("sq_ready")
        ss_ready = sem("ss_ready")
        sd_ready = sem("sd_ready")
        rs_ready = sem("rs_ready")
        h_ready = sem("h_ready")
        f_mm = sem("f_mm")
        f_arg = sem("f_arg")
        f_sin = sem("f_sin")
        rope_in = sem("rope_in")

        W = Uses(RING)
        B = [Uses(1), Uses(1)]

        stored = sem("stored")

        def wide(ap, axis, n):
            shape = list(ap.shape)
            shape.insert(axis, n)
            return ap.unsqueeze(axis).to_broadcast(shape)

        def col(ap, c):
            return ap.unsqueeze(2)[:, c, :]

        PHASES = [("ada", 24, 1), ("hy_in", 32, 2), ("hy_out", 8, 1), ("kv", 4, 2), ("q", 8, 1), ("z", 8, 1),
                  ("at_out", 8, 1)]
        for l in range(DEPTH):
            PHASES += [(f"proj{l}", 17, 1), (f"out{l}", 8, 1), (f"wq{l}", 4, 1), (f"peer{l}", BLOCKS, 1)]
        first, uses, at, used = {}, {}, 0, [0, 0]
        for name, n, banks in PHASES:
            first[name], uses[name] = at, list(used)
            for k in range(n):
                for b in ((0, 1) if banks == 2 else ((at + k) % 2,)):
                    used[b] += 1
            at += n

        def turns(e, n):
            full, rest = divmod(n, RING)
            if full > 1:
                with e.Fori(0, full) as i:
                    for j in range(RING):
                        yield i, j
            else:
                for j in range(full * RING):
                    yield 0, j
            for j in range(rest):
                yield full, j

        def slot_of(name, i, j):
            k = first[name] + j
            return k % RING, k // RING + i

        def bank_of(name, i, j):
            b = (first[name] + j) % 2
            return b, uses[name][b] + j // 2 + (RING // 2) * i

        def wait_chunk(pe, name, i, j):
            s, r = slot_of(name, i, j)
            pe.wait_ge(w_landed[s], 16 * (r + 1))
            return wring[:, s, :]

        def wait_done(e, name, i, j):
            s, r = slot_of(name, i, j)
            e.wait_ge(chunk_done[s], r + 2)

        def stream_chunk(sp, name, src, i, j, idx):
            s, r = slot_of(name, i, j)
            sp.wait_ge(chunk_done[s], r + 1)
            sp.dma_start(wring[:, s, :], src[idx]).then_inc(w_landed[s], 16)

        def stream(sp, name, src, n):
            for i, j in turns(sp, n):
                stream_chunk(sp, name, src, i, j, i * RING + j)

        SPLIT_PHASES = [(name, n) for name, n, _ in PHASES if name != "ada"]
        split_first, at = {}, 0
        for name, n in SPLIT_PHASES:
            split_first[name] = at
            at += n * UNITS

        def unit_of(name, i, q):
            return split_first[name] + UNITS * RING * i + q

        def raw_quarter(name, i, j, q):
            return wring[:, slot_of(name, i, j)[0], q * UNIT:(q + 1) * UNIT]

        def hi_quarter(act, name, i, j, q, n, buf):
            s, r = slot_of(name, i, j)
            act.wait_ge(w_landed[s], 16 * (r + 1))
            act.wait_ge(unit_used, n + 1)
            act.activation(SPLIT[:, buf, 0, :], raw_quarter(name, i, j, q), ACT.Copy).then_inc(split_hi, 1)

        def lo_quarter(v, name, i, j, q, n, buf, last):
            v.wait_ge(split_hi, n + 1)
            v.tensor_tensor(SPLIT[:, buf, 1, :], raw_quarter(name, i, j, q), SPLIT[:, buf, 0, :].bitcast(F32),
                            ALU.subtract).then_inc(split_lo, 1)
            if last:
                v.drain().then_inc(chunk_done[slot_of(name, i, j)[0]], 1)

        def split_activations(v, src, hi, lo):
            n = src.shape[1] // 2
            for k in range(2):
                v.tensor_copy(hi[:, k * n:(k + 1) * n, :], src[:, k * n:(k + 1) * n, :])
            v.drain()
            for k in range(2):
                v.tensor_tensor(lo[:, k * n:(k + 1) * n, :], src[:, k * n:(k + 1) * n, :],
                                hi[:, k * n:(k + 1) * n, :].bitcast(F32), ALU.subtract)

        def mm3(pe, out_ap, w_hi, w_lo, x_hi, x_lo, start, stop, **kw):
            pe.matmul(out_ap, w_hi, x_hi, start=start, stop=False, **kw)
            pe.matmul(out_ap, w_hi, x_lo, start=False, stop=False, **kw)
            return pe.matmul(out_ap, w_lo, x_hi, start=False, stop=stop, **kw)

        piece = lambda ap, q: ap[:, 4 * q:4 * q + 4, :]

        def parts_scalar(act, src, hi):
            for q in range(UNITS):
                act.activation(piece(hi, q), piece(src, q), ACT.Copy).then_inc(part_hi, 1)

        def parts_vector(v, src, hi, lo, base):
            for q in range(UNITS):
                v.wait_ge(part_hi, base + q + 1)
                v.tensor_tensor(piece(lo, q), piece(src, q), piece(hi, q).bitcast(F32), ALU.subtract).then_inc(part_lo, 1)

        def product3(pe, name, n, x_hi, x_lo, width, kt, parts=None):
            for i, j in turns(pe, n):
                b, u = bank_of(name, i, j)
                pe.wait_ge(bank_free[b], u + 1)
                for q in range(UNITS):
                    c = unit_of(name, i, UNITS * j + q)
                    pe.wait_ge(split_lo, c + 1)
                    if parts is not None:
                        pe.wait_ge(part_lo, parts + q + 1)
                    for m in range(UNIT // P):
                        t, k = divmod(q * (UNIT // P) + m, kt)
                        w = slice(m * P, (m + 1) * P)
                        mm = mm3(pe, bank[b][:, t * width:(t + 1) * width], SPLIT[:, q, 0, w], SPLIT[:, q, 1, w],
                                 x_hi[:, k, :], x_lo[:, k, :], k == 0, k == kt - 1)
                    mm.then_inc(unit_used, 1)

        def ahead(e, n, work, drain, started=False):
            full, rest = divmod(n, RING)
            if not started:
                work(0, 0)
            if full > 1:
                with e.Fori(0, full - 1) as i:
                    for j in range(RING):
                        work(i, j + 1)
                        drain(i, j)
            lead = (full - 1) if full > 1 else 0
            for j in range(n - RING * lead):
                if RING * lead + j + 1 < n:
                    work(lead, j + 1)
                drain(lead, j)

        def hi_chunk(act, name):
            def work(i, j):
                for q in range(UNITS):
                    hi_quarter(act, name, i, j, q, unit_of(name, i, UNITS * j + q), q)
            return work

        def hi_rest(act, name):
            work = hi_chunk(act, name)
            for j in range(1, 8):
                work(0, j)

        def lo_chunk(v, name):
            def work(i, j):
                for q in range(UNITS):
                    lo_quarter(v, name, i, j, q, unit_of(name, i, UNITS * j + q), q, q == UNITS - 1)
            return work

        def wait_product(e, name, i, j):
            e.wait_ge(unit_used, unit_of(name, i, UNITS * j + UNITS - 1) + 1 + UNITS)

        def ada_scalar(act):
            act.wait_ge(setup_in, SETUP)
            act.activation(SILC, V1["c"].rearrange("p (k s) -> p k s", s=2), ACT.Silu).then_inc(silc_ready, 1)

        def ada_tensor(pe):
            pe.wait_ge(silc_ready, 1)
            for i, j in turns(pe, 24):
                w = wait_chunk(pe, "ada", i, j)
                b, u = bank_of("ada", i, j)
                pe.wait_ge(bank_free[b], u + 1)
                for k in range(KT):
                    mm = pe.matmul(bank[b][0:2, 0:256], SILC[:, k, :], w[:, k * 256:(k + 1) * 256],
                                   start=(k == 0), stop=(k == KT - 1))
                mm.then_inc(chunk_done[slot_of("ada", i, j)[0]], 1)
            pe.wait_ge(ada_rows, 1)
            for n in range(48):
                mm = pe.transpose(bank[2][:, 2 * n:2 * n + 2], ADAROW[0:2, n * P:(n + 1) * P], ident[0:2, 0:2])
            mm.then_inc(ada_cols, 1)

        def ada_vector(v):
            rows = ADAROW.rearrange("p (n c) -> p n c", n=24)
            for i, j in turns(v, 24):
                b, _ = bank_of("ada", i, j)
                wait_done(v, "ada", i, j)
                v.tensor_copy(rows[0:2, i * RING + j, :], bank[b][0:2, 0:256]).then_inc(bank_free[b], 1)
            v.drain().then_inc(ada_rows, 1)
            sums_vector(v, 0)
            v.wait_ge(ada_cols, 1)
            v.tensor_tensor(KEEP1[:, 0:96].rearrange("p (n s) -> p n s", s=2),
                            bank[2][:, 0:96].rearrange("p (n s) -> p n s", s=2), wide(V1["ada_b"], 2, 2), ALU.add)
            v.drain()
            for l in range(DEPTH):
                v.scalar_tensor_tensor(adag[:, l], adac[:, l, 8:16], 1.0, wide(V1["norm_g"][:, 8 * l:8 * l + 8], 2, 2),
                                       ALU.add, ALU.mult)
            v.drain().then_inc(mod_ready, 1)

        def sums_scalar(act, l):
            if l:
                act.wait_ge(x_new, 1)
            for k in range(KT):
                act.activation(SQ1[:, k, :], X[:, k, :], ACT.Square).then_inc(sq_ready, 1)
            act.wait_ge(ss_ready, l + 1)
            act.activation(RS1, bank[3][:, :], ACT.Sqrt, scale=1.0 / D, bias=C["eps6"]).then_inc(sd_ready, 1)

        def rms_scalar(act, l):
            act.wait_ge(mod_ready, 1)
            act.wait_ge(rs_ready, l + 1)
            for k in range(KT):
                act.activation(TM1[:, k, T:T2], TM1[:, k, T:T2], ACT.Identity, scale=adag[:, l, k, 1:2],
                               bias=adac[:, l, k, 1:2])
            act.drain()
            act.activation(H1_HI[:, :, T:T2], TM1[:, :, T:T2], ACT.Copy).then_inc(h_ready, 1)

        def sums_tensor(pe, l):
            for k in range(KT):
                pe.wait_ge(sq_ready, KT * l + k + 1)
                mm = pe.matmul(bank[3][:, :], ones, SQ1[:, k, :], start=(k == 0), stop=(k == KT - 1))
            mm.then_inc(ss_ready, 1)

        def sums_vector(v, l):
            v.wait_ge(sd_ready, l + 1)
            v.reciprocal(RS1, RS1)
            v.drain()
            v.tensor_tensor(TM1, X, wide(RS1, 1, KT), ALU.mult).then_inc(rs_ready, 1)

        def rms_vector(v, l):
            v.drain()
            for k in range(KT):
                v.tensor_scalar(TM1[:, k, 0:T], TM1[:, k, 0:T], adag[:, l, k, 0:1], adac[:, l, k, 0:1],
                                ALU.mult, ALU.add)
            v.drain()
            v.tensor_copy(H1_HI[:, :, 0:T], TM1[:, :, 0:T])
            v.drain()
            v.tensor_tensor(H1_LO[:, :, 0:T], TM1[:, :, 0:T], H1_HI[:, :, 0:T].bitcast(F32), ALU.subtract)
            v.wait_ge(h_ready, 2 * l + 1)
            v.tensor_tensor(H1_LO[:, :, T:T2], TM1[:, :, T:T2], H1_HI[:, :, T:T2].bitcast(F32),
                            ALU.subtract).then_inc(h_ready, 1)

        TWO_PI = 2 * np.pi
        PI_A, PI_B = 6.28125, TWO_PI - 6.28125
        PI_MAX = float(np.nextafter(np.float32(np.pi), np.float32(0)))
        MAGIC = 12582912.0

        def filter_tensor(pe):
            pe.wait_ge(setup_in, SETUP)
            for q in range(3):
                rows = 33 if q == 0 else 64
                rhs = HC["z"][0:33, :] if q == 0 else HF[0:64, 2, :]
                if q:
                    pe.wait_ge(f_sin, q)
                pe.matmul(bank[4][0:64, 0:T], V1["fw"][0:rows, 64 * q:64 * q + 64], rhs,
                          start=True, stop=True).then_inc(f_mm, 1)

        def filter_vector(v):
            v.wait_ge(setup_in, SETUP)
            a, n = HF[0:64, 0, :], HF[0:64, 1, :]
            for q in range(3):
                v.wait_ge(f_mm, q + 1)
                v.tensor_scalar(a, bank[4][0:64, 0:T], V1["fb"][0:64, q:q + 1], V1["freq"][0:64, :], ALU.add, ALU.mult)
                v.drain()
                v.tensor_scalar(n, a, 1.0 / TWO_PI, MAGIC, ALU.mult, ALU.add)
                v.drain()
                v.tensor_scalar(n, n, MAGIC, None, ALU.subtract)
                v.drain()
                v.scalar_tensor_tensor(a, n, -PI_A, a, ALU.mult, ALU.add)
                v.drain()
                v.scalar_tensor_tensor(a, n, -PI_B, a, ALU.mult, ALU.add)
                v.drain()
                v.tensor_scalar(a, a, PI_MAX, -PI_MAX, ALU.min, ALU.max).then_inc(f_arg, 1)

        def filter_scalar(act):
            for q in range(3):
                act.wait_ge(f_arg, q + 1)
                act.activation(HSIN[0:64, :] if q == 2 else HF[0:64, 2, :], HF[0:64, 0, :], ACT.Sin).then_inc(f_sin, 1)

        kf_done = sem("kf_done")
        kb_ready = sem("kb_ready")
        ksd_ready = sem("ksd_ready")
        kabs_ready = sem("kabs_ready")
        kdft_done = sem("kdft_done")
        kspec_ready = sem("kspec_ready")
        u_ready = sem("u_ready")
        t_done = sem("t_done")
        ut_ready = sem("ut_ready")
        udft_done = sem("udft_done")
        uspec_free = sem("uspec_free")
        y_ready = sem("y_ready")
        inv_done = sem("inv_done")
        zs_ready = sem("zs_ready")
        yg_done = sem("yg_done")
        x_new = sem("x_new")

        def hyena_tiles(e, head, tail, back):
            head(0, 0)
            with e.Fori(0, CT // 2 - 1) as i:
                for j in range(2):
                    tail(i, j)
                    head(i + (j + 1) // 2, (j + 1) % 2)
                    back(i, j)
            i = CT // 2 - 1
            tail(i, 0)
            head(i, 1)
            back(i, 0)
            tail(i, 1)
            back(i, 1)

        def hyena_sync(sp, w_src, dec_src, w4_src):
            with sp.Fori(0, CT // 2) as i:
                for j in range(2):
                    sp.wait_ge(kb_ready, 2 * i + j + 1)
                    sp.dma_start(DEC[:, j, 0:512], dec_src[2 * i + j]).then_inc(dec_landed[j], 16)
                    sp.dma_start(DEC[0:64, j, 512:], w4_src[2 * i + j]).then_inc(dec_landed[j], 16)
                    for q in range(2):
                        stream_chunk(sp, "hy_in", w_src, i, 2 * j + q, i * RING + 2 * j + q)

        def tile_product3(pe, name, i, j, t, width):
            pe.wait_ge(bank_free[t], uses[name][t] + j + RING * i + 1)
            for q in (2 * t, 2 * t + 1):
                pe.wait_ge(split_lo, unit_of(name, i, UNITS * j + q) + 1)
                for m in range(UNIT // P):
                    k = (q % 2) * (UNIT // P) + m
                    w = slice(m * P, (m + 1) * P)
                    mm = mm3(pe, bank[t][:, 0:width], SPLIT[:, q, 0, w], SPLIT[:, q, 1, w], H1_HI[:, k, 0:width],
                             H1_LO[:, k, 0:width], k == 0, k == KT - 1)
                mm.then_inc(unit_used, 1)

        def wait_tile(e, name, i, j, t):
            e.wait_ge(unit_used, unit_of(name, i, UNITS * j + 2 * t + 1) + 1 + UNITS)

        def hyena_tensor(pe):
            def head(i, j):
                c = 2 * i + j
                pe.wait_ge(kb_ready, c + 2)
                pe.wait_ge(dec_landed[j], 32 * (i + 1))
                for tt in range(2):
                    mm = pe.matmul(bank[2][:, tt * 256:(tt + 1) * 256], HSIN[0:64, tt * P:(tt + 1) * P],
                                   DEC[0:64, j, 512:], start=True, stop=True)
                mm.then_inc(kf_done, 1)
                tile_product3(pe, "hy_in", i, 2 * j, 0, T2)
                tile_product3(pe, "hy_in", i, 2 * j, 1, T2)

            def tail(i, j):
                c = 2 * i + j
                pe.wait_ge(ksd_ready, c + 1)
                pe.wait_ge(kabs_ready, c + 1)
                pe.wait_ge(kspec_ready, c + 1)
                for f in range(2):
                    for tt in range(2):
                        pe.matmul(bank[3][:, f * P:(f + 1) * P], HC["re"][:, tt * T + f * P:tt * T + (f + 1) * P],
                                  KSD[:, 0, tt * P:(tt + 1) * P], start=(tt == 0), stop=(tt == 1))
                for tt in range(2):
                    pe.matmul(bank[3][:, 2 * P:3 * P], HC["rex"][:, tt * P:(tt + 1) * P],
                              KSD[:, 0, tt * P:(tt + 1) * P], start=(tt == 0), stop=(tt == 1))
                for f in range(2):
                    for tt in range(2):
                        pe.matmul(bank[4][:, f * P:(f + 1) * P], HC["sn"][:, tt * T + f * P:tt * T + (f + 1) * P],
                                  KSD[:, 1, tt * P:(tt + 1) * P], start=(tt == 0), stop=(tt == 1))
                for g in range(4):
                    mm = pe.matmul(bank[4][:, 2 * P:2 * P + 1], KABS[:, g * P:(g + 1) * P], ones[:, 0:1],
                                   start=(g == 0), stop=(g == 3))
                mm.then_inc(kdft_done, 1)
                tile_product3(pe, "hy_in", i, 2 * j + 1, 0, T2)
                pe.wait_ge(u_ready, c + 1)
                pe.wait_ge(yg_done, c + 1)
                for g in range(4):
                    mm = pe.transpose(bank[5][:, g * P:(g + 1) * P], U[:, g * P:(g + 1) * P], ident)
                mm.then_inc(t_done, 1)
                tile_product3(pe, "hy_in", i, 2 * j + 1, 1, T2)
                pe.wait_ge(ut_ready, c + 1)
                pe.wait_ge(uspec_free, c + 1)
                ut = UT.rearrange("p (s a c) -> p s a c", s=2, a=2)
                for m, b in (("re", 6), ("im", 7)):
                    for f in range(2):
                        for tt in range(2):
                            mm = pe.matmul(bank[b][:, f * 256:(f + 1) * 256],
                                           HC[m][:, tt * T + f * P:tt * T + (f + 1) * P], ut[:, :, tt, :],
                                           start=(tt == 0), stop=(tt == 1))
                mm.then_inc(udft_done, 1)

            def back(i, j):
                c = 2 * i + j
                pe.wait_ge(y_ready, c + 1)
                for s in range(2):
                    for n, (part, m, f) in enumerate([(0, "ire", 0), (0, "ire", 1), (1, "iim", 0), (1, "iim", 1)]):
                        mm = pe.matmul(bank[5][:, s * T:(s + 1) * T],
                                       PR4[:, 2 * part, f * 256 + s * P:f * 256 + (s + 1) * P],
                                       HC[m][:, f * T:(f + 1) * T], start=(n == 0), stop=(n == 3))
                mm.then_inc(inv_done, 1)

            hyena_tiles(pe, head, tail, back)

        def hyena_scalar(act):
            act.sem_inc(kspec_ready, 1)

            def hi(i, j, part):
                for q in (2 * part, 2 * part + 1):
                    hi_quarter(act, "hy_in", i, j, q, unit_of("hy_in", i, UNITS * j + q), q)

            hi(0, 0, 0)
            hi(0, 0, 1)
            with act.Fori(0, CT // 2) as i:
                for j in range(2):
                    c = 2 * i + j
                    act.wait_ge(kb_ready, c + 3)
                    act.activation(KABS, KB, ACT.Abs).then_inc(kabs_ready, 1)
                    hi(i, 2 * j + 1, 0)
                    act.wait_ge(kdft_done, c + 1)
                    act.wait_ge(uspec_free, c + 1)
                    act.activation(KSPEC[:, 0:3, :], view(bank[3][:, 0:3 * P], 3), ACT.Copy)
                    act.activation(KSPEC[:, 3:5, :], view(bank[4][:, 0:2 * P], 2), ACT.Copy)
                    act.activation(KNORM[:, 0:1], bank[4][:, 2 * P:2 * P + 1], ACT.Copy).then_inc(kspec_ready, 1)
                    hi(i, 2 * j + 1, 1)
                    act.wait_ge(t_done, c + 1)
                    act.activation(UT, bank[5][:, :], ACT.Copy).then_inc(ut_ready, 1)
                    hi(i, 2 * j + 2, 0)
                    wait_tile(act, "hy_in", i, 2 * j + 1, 1)
                    act.wait_ge(yg_done, c + 1)
                    act.activation(ZS1, bank[1][:, :], ACT.Silu).then_inc(bank_free[1], 1)
                    act.drain().then_inc(zs_ready, 1)
                    hi(i, 2 * j + 2, 1)

        def two(ap):
            return ap.rearrange("p (s t) -> p s t", s=2)

        def hyena_vector(v):
            v.sem_inc(kb_ready, 2)
            v.sem_inc(uspec_free, 1)
            v.sem_inc(yg_done, 1)
            conv_w = V1["conv_w"].rearrange("p (c q k) -> p c q k", c=CT, q=3)
            conv_b = V1["conv_b"].rearrange("p (c q) -> p c q", c=CT)

            def conv(c, q, src):
                o, s = two(CX[:, q, :]), two(src)
                v.tensor_scalar(o, s, conv_w[:, c, q, 1:2], conv_b[:, c, q:q + 1], ALU.mult, ALU.add)
                v.drain()
                v.scalar_tensor_tensor(o[:, :, 1:T], s[:, :, 0:T - 1], conv_w[:, c, q, 0:1], o[:, :, 1:T],
                                       ALU.mult, ALU.add)
                v.drain()
                return v.scalar_tensor_tensor(o[:, :, 0:T - 1], s[:, :, 1:T], conv_w[:, c, q, 2:3], o[:, :, 0:T - 1],
                                              ALU.mult, ALU.add)

            def lo(i, j, part):
                for q in (2 * part, 2 * part + 1):
                    lo_quarter(v, "hy_in", i, j, q, unit_of("hy_in", i, UNITS * j + q), q, q == UNITS - 1)

            lo(0, 0, 0)
            lo(0, 0, 1)
            def head(i, j):
                c = 2 * i + j
                v.wait_ge(kf_done, c + 1)
                v.wait_ge(dec_landed[j], 32 * (i + 1))
                v.tensor_tensor(KB, bank[2][:, :], DEC[:, j, 0:512], ALU.mult).then_inc(kb_ready, 1)
                v.drain()
                kb = KB.rearrange("p (a f c) -> p a f c", a=2, f=2)
                v.tensor_tensor(view(KSD[:, 0, :], 2), kb[:, :, 0, :], kb[:, :, 1, :], ALU.add)
                v.tensor_tensor(view(KSD[:, 1, :], 2), kb[:, :, 0, :], kb[:, :, 1, :],
                                ALU.subtract).then_inc(ksd_ready, 1)
                wait_tile(v, "hy_in", i, 2 * j, 0)
                conv(c, 0, bank[0][:, :]).then_inc(bank_free[0], 1)
                lo(i, 2 * j + 1, 0)
                wait_tile(v, "hy_in", i, 2 * j, 1)
                conv(c, 1, bank[1][:, :]).then_inc(bank_free[1], 1)
                v.drain()
                v.tensor_tensor(U, CX[:, 0, :], CX[:, 1, :], ALU.mult).then_inc(u_ready, 1)

            def tail(i, j):
                c = 2 * i + j
                lo(i, 2 * j + 1, 1)
                wait_tile(v, "hy_in", i, 2 * j + 1, 0)
                conv(c, 2, bank[0][:, :]).then_inc(bank_free[0], 1)
                lo(i, 2 * j + 2, 0)
                v.wait_ge(kspec_ready, c + 2)
                v.reciprocal(KNORM[:, 1:2], KNORM[:, 0:1])
                v.tensor_scalar(YT[:, 0, :], U, col(V1["hy_d"], c), None, ALU.mult)
                lo(i, 2 * j + 2, 1)
                v.wait_ge(udft_done, c + 1)
                ur = bank[6][:, :].rearrange("p (f s c) -> p f s c", f=2, s=2)
                ui = bank[7][:, :].rearrange("p (f s c) -> p f s c", f=2, s=2)
                pr = [PR4[:, n, :].rearrange("p (f s c) -> p f s c", f=2, s=2) for n in range(4)]
                v.tensor_tensor(pr[0], ur, wide(KSPEC[:, 0:2, :], 2, 2), ALU.mult)
                v.tensor_tensor(pr[1], ui, wide(KSPEC[:, 3:5, :], 2, 2), ALU.mult)
                v.tensor_tensor(pr[2], ur, wide(KSPEC[:, 3:5, :], 2, 2), ALU.mult)
                v.tensor_tensor(pr[3][:, 0], ui[:, 0], wide(KSPEC[:, 2, :], 1, 2), ALU.mult)
                v.tensor_tensor(pr[3][:, 1], ui[:, 1], wide(KSPEC[:, 1, :], 1, 2), ALU.mult).then_inc(uspec_free, 1)
                v.drain()
                v.tensor_tensor(PR4[:, 0, :], PR4[:, 0, :], PR4[:, 1, :], ALU.subtract)
                v.tensor_tensor(PR4[:, 2, :], PR4[:, 2, :], PR4[:, 3, :], ALU.add).then_inc(y_ready, 1)

            def back(i, j):
                c = 2 * i + j
                v.wait_ge(inv_done, c + 1)
                v.scalar_tensor_tensor(YT[:, 1, :], bank[5][:, :], KNORM[:, 1:2], YT[:, 0, :], ALU.mult, ALU.add)
                v.drain()
                v.tensor_tensor(YT[:, 1, :], YT[:, 1, :], CX[:, 2, :], ALU.mult)
                v.drain()
                v.wait_ge(zs_ready, c + 1)
                v.tensor_tensor(YG[:, c, :], YT[:, 1, :], ZS1, ALU.mult).then_inc(yg_done, 1)

            hyena_tiles(v, head, tail, back)

        def add_gated(v, name, l, seqs):
            def add(i, j):
                n = i * RING + j
                b, _ = bank_of(name, i, j)
                wait_product(v, name, i, j)
                for s in range(seqs):
                    a = v.scalar_tensor_tensor(X[:, n, s * T:(s + 1) * T], bank[b][:, s * T:(s + 1) * T],
                                               adac[:, l, 16 + n, s:s + 1], X[:, n, s * T:(s + 1) * T],
                                               ALU.mult, ALU.add)
                a.then_inc(bank_free[b], 1)

            ahead(v, 8, lo_chunk(v, name), add, started=True)
            v.drain().then_inc(x_new, 1)

        ksq = sem("ksq")
        kss = sem("kss")
        ksd = sem("ksd")
        kn_ready = sem("kn_ready")
        krot = sem("krot")
        k_ready = sem("k_ready")
        vt_done = sem("vt_done")
        v_ready = sem("v_ready")
        q_in = sem("q_in")
        qsq, qss, qsd, qn_ready, qrot, qf_ready = (sem(n) for n in ("qsq", "qss", "qsd", "qn_ready", "qrot", "qf_ready"))
        vs_ready = sem("vs_ready")
        s_done = sem("s_done")
        nmax_ready = sem("nmax_ready")
        p_exp = sem("p_exp")
        p_ready = sem("p_ready")
        pt_done = sem("pt_done")
        pt_ready = sem("pt_ready")
        pv_done = sem("pv_done")
        og_done = sem("og_done")
        SCALE = float(P) ** -0.5
        PTV = PTR.rearrange("p a (k c) -> p (a k) c", k=2).rearrange("p (h k) c -> p h k c", h=2)

        def kv_tensor(pe):
            for i, j in turns(pe, 4):
                tile_product3(pe, "kv", i, j, 0, T2)
                tile_product3(pe, "kv", i, j, 1, T2)

        def kv_scalar(act):
            def drain_head(i, g):
                wait_tile(act, "kv", i, g, 0)
                act.activation(KR[:, g, :], bank[0][:, :], ACT.Copy).then_inc(bank_free[0], 1)
                wait_tile(act, "kv", i, g, 1)
                act.activation(VR[:, g, :], bank[1][:, :], ACT.Copy).then_inc(bank_free[1], 1)

            ahead(act, KV_HEADS, hi_chunk(act, "kv"), drain_head)
            hi_chunk(act, "q")(0, 0)
            act.drain()
            for g in range(KV_HEADS):
                act.activation(PRB[:, g, :], KR[:, g, :], ACT.Square).then_inc(ksq, 1)

        def gather(act, name, dst, func, n, started=False):
            def drain_bank(i, j):
                b, _ = bank_of(name, i, j)
                wait_product(act, name, i, j)
                act.activation(dst[:, i * RING + j, :], bank[b][:, :], func).then_inc(bank_free[b], 1)

            ahead(act, n, hi_chunk(act, name), drain_bank, started)

        pairs = lambda ap: ap.rearrange("p (n a) t -> p n (a t)", a=2)

        def prep_tensor(pe):
            for g in range(KV_HEADS):
                pe.wait_ge(ksq, g + 1)
                pe.matmul(bank[2 + g][:, :], ones, PRB[:, g, :], start=True, stop=True).then_inc(kss, 1)
            for g in range(KV_HEADS):
                if g >= 2:
                    pe.wait_ge(v_ready, g - 1)
                for k in range(4):
                    mm = pe.transpose(bank[6 + g % 2][:, k * P:(k + 1) * P], VR[:, g, k * P:(k + 1) * P], ident)
                mm.then_inc(vt_done, 1)

        def turn_tensor(pe):
            for g in range(KV_HEADS):
                pe.wait_ge(kn_ready, g + 1)
                pe.wait_ge(rope_in, 16)
                pe.matmul(bank[2 + g][:, 0:T], RO["rot"], KR[:, g, 0:T], start=True, stop=True).then_inc(krot, 1)

        def prep_scalar(act):
            for g in range(KV_HEADS):
                act.wait_ge(kss, g + 1)
                act.activation(PTR[:, g, :], bank[2 + g][:, :], ACT.Sqrt, scale=1.0 / P, bias=C["eps6"]).then_inc(ksd, 1)
            for g in range(KV_HEADS):
                act.wait_ge(vt_done, g + 1)
                act.activation(VR[:, g, :], bank[6 + g % 2][:, :], ACT.Copy).then_inc(v_ready, 1)

        def prep_vector(v):
            for name, n in (("kv", KV_HEADS), ("q", 8)):
                work = lo_chunk(v, name)
                for i, j in turns(v, n):
                    work(i, j)
            work = lo_chunk(v, "z")
            for g in range(KV_HEADS):
                work(0, g)
                v.wait_ge(ksd, g + 1)
                v.reciprocal(PTR[:, g, :], PTR[:, g, :])
                v.drain()
                v.scalar_tensor_tensor(KR[:, g, :], KR[:, g, :], V1["k_g"], PTR[:, g, :],
                                       ALU.mult, ALU.mult).then_inc(kn_ready, 1)
            for j in range(KV_HEADS, 8):
                work(0, j)
            for g in range(KV_HEADS):
                v.drain()
                v.wait_ge(krot, g + 1)
                v.tensor_tensor(RT1[:, 0:T], KR[:, g, 0:T], RO["cos"], ALU.mult)
                v.tensor_tensor(RT2[:, 0:T], bank[2 + g][:, 0:T], RO["sin"], ALU.mult)
                v.drain()
                v.tensor_tensor(KR[:, g, 0:T], RT1[:, 0:T], RT2[:, 0:T], ALU.add).then_inc(k_ready, 1)

        def head_pairs(e, first, pair):
            first()
            with e.Fori(0, KV_HEADS - 1) as g:
                for pp in range(2):
                    pair(g, pp, True)
            for pp in range(2):
                pair(KV_HEADS - 1, pp, pp == 0)

        def heads_tensor(pe):
            pe.wait_ge(q_in, 1)

            def squares(n):
                pe.wait_ge(qsq, n + 1)
                pe.matmul(bank[0][:, :], ones, SQA, start=True, stop=True).then_inc(qss, 1)

            def rotate(n):
                pe.wait_ge(qn_ready, n + 1)
                pe.matmul(bank[1][:, :], RO["rot"], QN, start=True, stop=True).then_inc(qrot, 1)

            def first():
                squares(0)
                rotate(0)
                pe.wait_ge(k_ready, KV_HEADS)

            def pair(g, pp, more):
                n = 2 * g + pp
                pe.wait_ge(qf_ready, n + 1)
                for q in range(4):
                    pe.matmul(bank[4 + q][:, :], QF[:, q * P:(q + 1) * P], KR[:, g, :],
                              start=True, stop=True).then_inc(s_done, 1)
                if more:
                    squares(n + 1)
                for q in range(4):
                    pe.wait_ge(p_ready, 4 * n + q + 1)
                    for k in range(4):
                        mm = pe.transpose(bank[4 + q][:, k * P:(k + 1) * P], PRB[:, q, k * P:(k + 1) * P], ident)
                    mm.then_inc(pt_done, 1)
                pe.wait_ge(vs_ready, g + 1)
                pe.wait_ge(og_done, 2 * n + 2)
                for a in range(2):
                    pe.wait_ge(pt_ready, 4 * n + 2 * a + 2)
                    for k in range(4):
                        mm = pe.matmul(bank[2 + a][:, 0:T], VS[:, k, :], PTV[:, a, k, :], start=(k == 0), stop=(k == 3))
                    mm.then_inc(pv_done, 1)
                if more:
                    rotate(n + 1)

            head_pairs(pe, first, pair)

        def heads_scalar(act):
            act.drain().then_inc(q_in, 1)
            qr = pairs(QR)

            def square(n):
                act.activation(SQA, qr[:, n, :], ACT.Square).then_inc(qsq, 1)

            def root(n):
                act.wait_ge(qss, n + 1)
                act.activation(RSA, bank[0][:, :], ACT.Sqrt, scale=1.0 / P, bias=C["eps6"]).then_inc(qsd, 1)

            def first():
                square(0)
                root(0)

            def pair(g, pp, more):
                n = 2 * g + pp
                if more:
                    square(n + 1)
                for q in range(4):
                    act.wait_ge(nmax_ready, 4 * n + q + 1)
                    act.activation(PRB[:, q, :], bank[4 + q][:, :], ACT.Exp, scale=SCALE, bias=STAT[:, 1, q:q + 1],
                                   accum_out=STAT[:, 2, q:q + 1]).then_inc(p_exp, 1)
                if pp == 0:
                    act.wait_ge(og_done, 2 * n + 2)
                    act.activation(VS, view2(VR[:, g, :], 4), ACT.Copy).then_inc(vs_ready, 1)
                if more:
                    root(n + 1)
                for q in range(4):
                    act.wait_ge(pt_done, 4 * n + q + 1)
                    act.activation(PTV[:, q // 2, :, (q % 2) * P:(q % 2 + 1) * P], view2(bank[4 + q][:, :], 4),
                                   ACT.Copy).then_inc(pt_ready, 1)

            head_pairs(act, first, pair)

        def view2(ap, a):
            return ap.rearrange("p (a b) -> p a b", a=a)

        def heads_vector(v):
            v.sem_inc(og_done, 2)
            v.wait_ge(rope_in, 16)
            v.wait_ge(q_in, 1)

            def normed(n):
                v.wait_ge(qsd, n + 1)
                v.reciprocal(RSA, RSA)
                v.drain()
                v.scalar_tensor_tensor(QN, pairs(QR)[:, n, :], V1["q_g"], RSA, ALU.mult, ALU.mult).then_inc(qn_ready, 1)
                v.drain()
                v.tensor_tensor(two(RT1), two(QN), wide(RO["cos"], 1, 2), ALU.mult)

            def rotated(n):
                v.wait_ge(qrot, n + 1)
                v.tensor_tensor(two(RT2), two(bank[1][:, :]), wide(RO["sin"], 1, 2), ALU.mult)
                v.drain()
                v.tensor_tensor(QF, RT1, RT2, ALU.add).then_inc(qf_ready, 1)

            def first():
                v.drain()
                normed(0)
                rotated(0)

            def pair(g, pp, more):
                n = 2 * g + pp
                for q in range(4):
                    v.wait_ge(s_done, 4 * n + q + 1)
                    v.reduce_max(STAT[:, 0, q:q + 1], bank[4 + q][:, :], AX_X)
                    v.drain()
                    v.tensor_scalar(STAT[:, 1, q:q + 1], STAT[:, 0, q:q + 1], -SCALE, None, ALU.mult).then_inc(nmax_ready, 1)
                for q in range(4):
                    v.wait_ge(p_exp, 4 * n + q + 1)
                    v.reciprocal(STAT[:, 3, q:q + 1], STAT[:, 2, q:q + 1])
                    v.drain()
                    v.tensor_scalar(PRB[:, q, :], PRB[:, q, :], STAT[:, 3, q:q + 1], None, ALU.mult).then_inc(p_ready, 1)
                if more:
                    normed(n + 1)
                for a in range(2):
                    v.wait_ge(pv_done, 2 * n + a + 1)
                    v.tensor_tensor(OG[:, 2 * n + a, :], bank[2 + a][:, 0:T], ZG[:, 2 * n + a, :],
                                    ALU.mult).then_inc(og_done, 1)
                if more:
                    rotated(n + 1)

            head_pairs(v, first, pair)

        ln_in = sem("ln_in")
        ln_sum, ln_mu, ln_xc, ln_sq, ln_var, ln_sd = (sem(n) for n in ("ln_sum", "ln_mu", "ln_xc", "ln_sq", "ln_var", "ln_sd"))
        h_new = sem("h_new")

        def norm_tensor(pe, q, src):
            pe.wait_ge(ln_in, q + 1)
            for k in range(KT):
                mm = pe.matmul(bank[2][:, 0:T], ones, src[:, k, 0:T], start=(k == 0), stop=(k == KT - 1))
            mm.then_inc(ln_sum, 1)
            pe.wait_ge(ln_sq, q + 1)
            for k in range(KT):
                mm = pe.matmul(bank[3][:, 0:T], ones, SQ[:, k, :], start=(k == 0), stop=(k == KT - 1))
            mm.then_inc(ln_var, 1)
            pe.wait_ge(h_new, q + 1)

        def norm_scalar(act, q, centred):
            act.wait_ge(ln_sum, q + 1)
            act.activation(MU, bank[2][:, 0:T], ACT.Copy, scale=1.0 / D).then_inc(ln_mu, 1)
            act.wait_ge(ln_xc, q + 1)
            act.activation(SQ, centred, ACT.Square).then_inc(ln_sq, 1)
            act.wait_ge(ln_var, q + 1)
            act.activation(RS, bank[3][:, 0:T], ACT.Sqrt, scale=1.0 / D, bias=C["eps5"]).then_inc(ln_sd, 1)

        def norm_vector(v, q, src, centred, g, b, dst, parts):
            v.drain().then_inc(ln_in, 1)
            v.wait_ge(ln_mu, q + 1)
            v.tensor_tensor(centred, src, wide(MU, 1, KT), ALU.subtract).then_inc(ln_xc, 1)
            v.wait_ge(ln_sd, q + 1)
            v.reciprocal(RS, RS)
            v.drain()
            v.tensor_tensor(centred, centred, wide(RS, 1, KT), ALU.mult)
            v.drain()
            for k in range(KT):
                v.tensor_scalar(dst[:, k, :], centred[:, k, :], g[:, k:k + 1], b[:, k:k + 1], ALU.mult, ALU.add)
            v.drain()
            if parts:
                split_activations(v, dst, *parts)
            v.drain().then_inc(h_new, 1)

        XBC0, Q0, K0, V0, GATE0, Z0 = 4, 16, 20, 21, 22, 26
        prj_x = sem("prj_x")
        prj_all = sem("prj_all")
        dt_mm, dt_in = sem("dt_mm"), sem("dt_in")
        rgx_ready = sem("rgx_ready")
        rg_mm = sem("rg_mm")
        rg_act = sem("rg_act")
        sp_abs, sp_exp, sp_done = sem("sp_abs"), sem("sp_exp"), sem("sp_done")
        rg_gates = sem("rg_gates")
        a_ready = sem("a_ready")
        root_in, root_out = sem("root_in"), sem("root_out")
        alog_in, alog_out = sem("alog_in"), sem("alog_out")
        dec_in, dec_out = sem("dec_in"), sem("dec_out")
        colt_done, cols_ready = sem("colt_done"), sem("cols_ready")
        bc_conv = sem("bc_conv")
        bc_ready = sem("bc_ready")
        cb_done = sem("cb_done")
        cb_ready = sem("cb_ready")
        x_conv, x_ready = sem("x_conv"), sem("x_ready")
        xt_done, xdt_ready = sem("xt_done"), sem("xdt_ready")
        bcast_done = sem("bcast_done")
        seg_ready = sem("seg_ready")
        ex_ready = sem("ex_ready")
        m_ready = sem("m_ready")
        st_done, st_ready = sem("st_done"), sem("st_ready")
        y_done = sem("y_done")
        ys_ready, yq_ready = sem("ys_ready"), sem("yq_ready")
        gss_done, gsd_ready = sem("gss_done"), sem("gsd_ready")
        ys_used = sem("ys_used")
        qs_ready = sem("qs_ready")
        vtk_mm, vtk_ready = sem("vtk_mm"), sem("vtk_ready")
        sw_done, sw_max, sw_exp, sw_p, sw_t, sw_tc, sw_pv, sw_out = (
            sem(n) for n in ("sw_done", "sw_max", "sw_exp", "sw_p", "sw_t", "sw_tc", "sw_pv", "sw_out"))
        mix_ready = sem("mix_ready")
        NB_T = XBC_T
        PRJ2 = PRJ.rearrange("p (n a) t -> p n (a t)", a=2)
        HALF_SCALE = 64.0 ** -0.5

        def proj_tensor(pe, l):
            pe.wait_ge(wide_in, 16 * (l + 1))
            for k in range(KT):
                mm = pe.matmul(bank[6][0:16, 0:T], WD["w_dt"][:, 16 * k:16 * k + 16], h[:, k, :],
                               start=(k == 0), stop=(k == KT - 1))
            mm.then_inc(dt_mm, 1)
            product3(pe, f"proj{l}", 17, h_hi, h_lo1, T, KT)

        def proj_scalar(act, l):
            name = f"proj{l}"

            def drain_bank(i, j):
                b, _ = bank_of(name, i, j)
                wait_product(act, name, i, j)
                act.activation(PRJ2[:, i * RING + j, :], bank[b][:, :], ACT.Copy).then_inc(bank_free[b], 1)

            ahead(act, 17, hi_chunk(act, name), drain_bank)
            act.drain().then_inc(prj_x, 1)
            act.wait_ge(sp_abs, l + 1)
            act.activation(SP[:, 1, :], SP[:, 1, :], ACT.Exp, scale=-1.0).then_inc(sp_exp, 1)
            act.activation(SROW[0:16, 3, 0:1], LV[l]["a_log"][0:16, :], ACT.Exp).then_inc(alog_out, 1)

        def causal_conv(v, o, x, w, b):
            v.tensor_scalar(o, x, w(3), b, ALU.mult, ALU.add)
            for k in (2, 1, 0):
                s = 3 - k
                v.drain()
                a = v.scalar_tensor_tensor(o[:, s:T], x[:, 0:T - s], w(k), o[:, s:T], ALU.mult, ALU.add)
            return a

        def softplus_inputs(v, l):
            L = LV[l]
            x, ax = SP[:, 0, :], SP[:, 1, :]
            v.memset(x, 0.0)
            v.drain()
            v.tensor_scalar(x[:, 0:4], L["lam"], -1.0, None, ALU.mult)
            v.wait_ge(dt_mm, l + 1)
            v.tensor_scalar(x[0:16, 4:], bank[6][0:16, 0:T], L["dt_bias"][0:16, :], None, ALU.add)
            v.drain()
            v.scalar_tensor_tensor(ax, x, -1.0, x, ALU.mult, ALU.max).then_inc(sp_abs, 1)

        def softplus_vector(v, l):
            x, ax, s, s2, p = (SP[:, n, :] for n in range(5))
            v.wait_ge(sp_exp, l + 1)
            v.tensor_scalar(s2, ax, 2.0, None, ALU.add)
            v.drain()
            v.reciprocal(s2, s2)
            v.drain()
            v.tensor_tensor(s, ax, s2, ALU.mult)
            v.drain()
            v.tensor_tensor(s2, s, s, ALU.mult)
            v.drain()
            v.tensor_scalar(p, s2, LOG1P_TERMS[0], None, ALU.mult)
            for term in LOG1P_TERMS[1:]:
                v.drain()
                v.scalar_tensor_tensor(p, p, term, s2, ALU.add, ALU.mult)
            v.drain()
            v.scalar_tensor_tensor(p, p, 1.0, s, ALU.add, ALU.mult)
            v.tensor_scalar(x, x, 0.0, None, ALU.max)
            v.drain()
            v.scalar_tensor_tensor(p, p, 2.0, x, ALU.mult, ALU.add)
            v.drain().then_inc(sp_done, 1)

        def lru_tensor(pe, l):
            pe.wait_ge(rgx_ready, l + 1)
            for n in range(8):
                m, t = n // 4, n % 4
                pe.wait_ge(rg_act, 8 * l + n + 1)
                pe.matmul(bank[4 + n % 2][:, 0:T], WD["rg_wax"][:, n * P:(n + 1) * P], RG[:, 0, t * T:(t + 1) * T],
                          start=True, stop=True).then_inc(rg_mm, 1)

        def lru_scalar(act, l):
            L = LV[l]
            for n in range(8):
                m, t = n // 4, n % 4
                act.wait_ge(rg_mm, 8 * l + n + 1)
                act.activation(RG[:, 1 + m, t * T:(t + 1) * T], bank[4 + n % 2][:, 0:T], ACT.Sigmoid,
                               bias=L["bx" if m else "ba"][:, t:t + 1]).then_inc(rg_act, 1)
            act.wait_ge(rg_gates, l + 1)
            act.drain()
            for t in range(4):
                r = RG[:, 1, t * T:(t + 1) * T]
                act.activation(RG[:, 3, t * T:(t + 1) * T], r, ACT.Exp, scale=MU[:, t:t + 1])
                act.activation(RG[:, 4, t * T:(t + 1) * T], r, ACT.Tanh, scale=MU[:, 4 + t:5 + t])
            act.drain().then_inc(a_ready, 1)
            act.activation(PRJ[:, GATE0:GATE0 + 4, :], PRJ[:, GATE0:GATE0 + 4, :], ACT.Gelu_apprx_tanh)
            act.activation(PRJ[:, Z0:Z0 + 8, :], PRJ[:, Z0:Z0 + 8, :], ACT.Silu)
            act.drain().then_inc(prj_all, 1)
            act.wait_ge(root_in, l + 1)
            act.activation(RG[:, 5, :], RG[:, 5, :], ACT.Sqrt).then_inc(root_out, 1)

        def lru_vector(v, l):
            L = LV[l]
            name = f"proj{l}"
            work = lo_chunk(v, name)
            w = L["rg_w"].rearrange("p (t k) -> p t k", k=4)
            with v.Fori(0, 2) as i:
                for j in range(RING):
                    work(i, j)
            for t in range(4):
                work(2, t)
                b, u = bank_of(name, 0, t // 2)
                v.wait_ge(bank_free[b], u + 2)
                v.drain()
                causal_conv(v, RG[:, 0, t * T:(t + 1) * T], PRJ[:, t, :], lambda k: w[:, t, k:k + 1], L["rg_b"][:, t:t + 1])
            softplus_inputs(v, l)
            for j in range(RING):
                work(3, j)
            work(4, 0)
            v.wait_ge(prj_x, l + 1)
            v.drain().then_inc(rgx_ready, 1)
            softplus_vector(v, l)
            v.tensor_scalar(MU[:, 0:4], SP[:, 4, 0:4], -8.0, None, ALU.mult)
            v.tensor_scalar(MU[:, 4:8], SP[:, 4, 0:4], 8.0, None, ALU.mult)
            v.drain().then_inc(rg_gates, 1)
            v.wait_ge(a_ready, l + 1)
            th, u = RG[:, 4, :], RG[:, 5, :]
            v.tensor_scalar(u, th, 1.0, None, ALU.add)
            v.drain()
            v.reciprocal(u, u)
            v.drain()
            v.scalar_tensor_tensor(u, th, 2.0, u, ALU.mult, ALU.mult).then_inc(root_in, 1)
            v.tensor_tensor(RG[:, 2, :], RG[:, 2, :], RG[:, 0, :], ALU.mult)
            v.drain()
            v.wait_ge(root_out, l + 1)
            v.tensor_tensor(u, u, RG[:, 2, :], ALU.mult)
            v.drain()
            for t in range(4):
                c = slice(t * T, (t + 1) * T)
                v.tensor_tensor_scan(RG[:, 4, c], RG[:, 3, c], RG[:, 5, c], 0.0, ALU.mult, ALU.add)
            v.drain()
            v.wait_ge(prj_all, l + 1)
            v.tensor_tensor(MIX[:, 0:4, :], view(RG[:, 4, :], 4), PRJ[:, GATE0:GATE0 + 4, :], ALU.mult)

        def rows_vector(v, l):
            dt = SP[0:16, 4, 4:]
            da, cum, st = (SROW[0:16, n, :] for n in range(3))
            v.wait_ge(alog_out, l + 1)
            v.tensor_scalar(da, dt, SROW[0:16, 3, 0:1], -1.0, ALU.mult, ALU.mult)
            v.drain()
            for c in range(2):
                s = slice(c * P, (c + 1) * P)
                v.tensor_tensor_scan(cum[:, s], ones[0:16, :], da[:, s], 0.0, ALU.mult, ALU.add)
            v.drain().then_inc(dec_in, 1)
            v.tensor_tensor(AD[0:16], wide(cum, 1, SSM_HEADS), wide(ident[0:16, 0:16], 2, T), ALU.mult)
            v.wait_ge(colt_done, l + 1)
            v.tensor_copy(COLS, view(bank[4][:, 0:80], 5))
            v.drain().then_inc(cols_ready, 1)

        def rows_scalar(act, l):
            act.wait_ge(dec_in, l + 1)
            act.activation(SROW[0:16, 2, 0:P], SROW[0:16, 1, 0:P], ACT.Exp, scale=-1.0,
                           bias=SROW[0:16, 1, P - 1:P]).then_inc(dec_out, 1)

        def rows_tensor(pe, l):
            pe.wait_ge(sp_done, l + 1)
            pe.wait_ge(dec_out, l + 1)
            pe.wait_ge(rg_act, 8 * (l + 1) + 2)
            for n, ap in enumerate((SP[0:16, 4, 4:4 + P], SP[0:16, 4, 4 + P:4 + 2 * P], SROW[0:16, 1, 0:P],
                                    SROW[0:16, 1, P:2 * P], SROW[0:16, 2, 0:P])):
                mm = pe.transpose(bank[4][:, 16 * n:16 * n + 16], ap, ident[0:16, 0:16])
            mm.then_inc(colt_done, 1)

        def ssm_tensor(pe, l):
            pe.wait_ge(cols_ready, l + 1)
            with pe.Fori(0, SSM_GROUPS) as g:
                n = 2 * l + g
                pe.wait_ge(bc_ready, 2 * n + 2)
                for c in range(2):
                    s = slice(c * P, (c + 1) * P)
                    pe.matmul(bank[2][:, s], BC[:, 0, s], BC[:, 1, s], start=True, stop=True)
                pe.transpose(bank[3][:, 0:P], BC[:, 0, 0:P], ident).then_inc(cb_done, 1)

                def front(t):
                    m = 4 * n + t
                    pe.wait_ge(x_ready, m + 1)
                    if t == 0:
                        pe.wait_ge(ys_ready, m + 1)
                    for c in range(2):
                        mm = pe.transpose(bank[4][:, c * P:(c + 1) * P], XS[:, t % 2, c * P:(c + 1) * P], ident)
                    mm.then_inc(xt_done, 1)
                    if t:
                        pe.wait_ge(ex_ready, m)
                    pe.matmul(bank[5][:, :], ones[0:16, :], ADP[0:16, 4 * g + t, :], start=True, stop=True).then_inc(bcast_done, 1)

                def output(t):
                    m = 4 * n + t
                    par = t % 2
                    pe.wait_ge(m_ready, m + 1)
                    pe.wait_ge(st_ready, m + 1)
                    pe.wait_ge(ys_ready, m + 1)
                    for hh in range(2):
                        q = slice(hh * 64, hh * 64 + 64)
                        pe.matmul(bank[7][q, 0:P], XDT[:, 0, par, q], SEG[:, par, 2 * hh, :], start=True, stop=True)
                        pe.matmul(bank[7][q, P:2 * P], XDT[:, 1, par, q], SEG[:, par, 2 * hh + 1, :], start=True, stop=False)
                        mm = pe.matmul(bank[7][q, P:2 * P], ST0[:, q], EX1[:, par, hh, :], start=False, stop=True)
                    mm.then_inc(y_done, 1)

                def state(t):
                    pe.wait_ge(cb_ready, n + 1)
                    pe.wait_ge(xdt_ready, 4 * n + t + 1)
                    pe.matmul(bank[6][:, 0:P], BT, XDS, start=True, stop=True).then_inc(st_done, 1)

                front(0)
                state(0)
                for t in range(4):
                    if t < 3:
                        front(t + 1)
                    output(t)
                    if t < 3:
                        state(t + 1)
                for t in range(4):
                    pe.wait_ge(yq_ready, 4 * n + t + 1)
                    mm = pe.matmul(bank[3][:, 256:512], ones, YQ4[:, t, :], start=(t == 0), stop=(t == 3))
                mm.then_inc(gss_done, 1)

        def ssm_scalar(act, l):
            with act.Fori(0, SSM_GROUPS) as g:
                n = 2 * l + g
                for q in range(2):
                    act.wait_ge(bc_conv, 2 * n + q + 1)
                    act.activation(BC[:, q, :], BC[:, q, :], ACT.Silu).then_inc(bc_ready, 1)
                for t in range(-1, 4):
                    if t < 3:
                        m, par = 4 * n + t + 1, (t + 1) % 2
                        act.wait_ge(x_conv, m + 1)
                        act.activation(XS[:, par, :], CV, ACT.Silu).then_inc(x_ready, 1)
                        act.wait_ge(seg_ready, m + 1)
                        act.activation(SEG[:, par], SEG[:, par], ACT.Exp)
                        act.activation(EX1[:, par], bank[5][:, :].rearrange("p (h c l) -> p h c l", h=2, c=2)[:, :, 1, :],
                                       ACT.Exp).then_inc(ex_ready, 1)
                        act.wait_ge(st_done, m + 1)
                        act.activation(ST0, bank[6][:, 0:P], ACT.Copy).then_inc(st_ready, 1)
                    if t < 0:
                        continue
                    act.wait_ge(ys_ready, 4 * n + t + 2)
                    act.activation(YQ4[:, t, :], YS[:, t, :], ACT.Square).then_inc(yq_ready, 1)
                act.wait_ge(gss_done, n + 1)
                act.activation(RS, bank[3][:, 256:512], ACT.Sqrt, scale=1.0 / 512, bias=C["eps5"]).then_inc(gsd_ready, 1)

        def ssm_vector(v, l):
            L = LV[l]
            w = L["ssm_w"].rearrange("p (t k) -> p t k", k=4)
            bias = L["ssm_b"].unsqueeze(2)
            dskip = L["ssm_d"].unsqueeze(2)
            gain = L["ssm_g"].unsqueeze(2)

            def conv(o, x, t):
                return causal_conv(v, o, PRJ[:, x, :], lambda k: w[:, t, k:k + 1], bias[:, t, :])

            with v.Fori(0, SSM_GROUPS) as g:
                n = 2 * l + g
                v.drain()
                conv(BC[:, 0, :], XBC0 + 8 + g, 8 + g).then_inc(bc_conv, 1)
                conv(BC[:, 1, :], XBC0 + 10 + g, 10 + g).then_inc(bc_conv, 1)
                v.wait_ge(cb_done, n + 1)
                v.tensor_tensor(CBM, view(bank[2][:, 0:2 * P], 2), wide(C["causal"], 1, 2), ALU.mult)
                v.tensor_copy(BT, bank[3][:, 0:P]).then_inc(cb_ready, 1)
                cols4 = COLS.rearrange("p a (n h) -> p a n h", h=2)

                def decayed(t):
                    par = t % 2
                    v.wait_ge(ex_ready, 4 * n + t + 1)
                    seg = SEG[:, par].rearrange("p (h c) l -> p h c l", h=2)
                    v.tensor_tensor(seg, seg, wide(CBM, 1, 2), ALU.mult)
                    v.tensor_tensor(EX1[:, par], EX1[:, par], wide(BC[:, 1, P:2 * P], 1, 2), ALU.mult).then_inc(m_ready, 1)

                def inputs(t):
                    m, par, tile = 4 * n + t, t % 2, 4 * g + t
                    v.wait_ge(xt_done, m + 1)
                    v.tensor_tensor(XDT[:, :, par, :].rearrange("p c (h d) -> p c h d", h=2),
                                    bank[4][:, 0:2 * P].rearrange("p (c h d) -> p c h d", c=2, h=2),
                                    wide(cols4[:, 0:2, tile, :], 3, 64), ALU.mult)
                    v.drain()
                    v.tensor_tensor(view(XDS, 2), view(XDT[:, 0, par, :], 2), wide(cols4[:, 4, tile, :], 2, 64),
                                    ALU.mult).then_inc(xdt_ready, 1)
                    v.wait_ge(bcast_done, m + 1)
                    for hh in range(2):
                        for c in range(2):
                            v.tensor_scalar(SEG[:, par, 2 * hh + c, :], bank[5][:, (2 * hh + c) * P:(2 * hh + c + 1) * P],
                                                cols4[:, 2 + c, tile, hh:hh + 1], 0.0, ALU.subtract, ALU.min)
                    v.drain().then_inc(seg_ready, 1)

                conv(CV, XBC0 + 4 * g, 4 * g).then_inc(x_conv, 1)
                inputs(0)
                for t in range(4):
                    if t < 3:
                        tile = 4 * g + t + 1
                        conv(CV, XBC0 + tile, tile).then_inc(x_conv, 1)
                    decayed(t)
                    if t < 3:
                        inputs(t + 1)
                    tile = 4 * g + t
                    v.wait_ge(y_done, 4 * n + t + 1)
                    v.scalar_tensor_tensor(YS[:, t, :], XS[:, t % 2, :], dskip[:, tile, :], bank[7][:, 0:T], ALU.mult, ALU.add)
                    v.drain()
                    v.tensor_tensor(YS[:, t, :], YS[:, t, :], PRJ[:, Z0 + tile, :], ALU.mult).then_inc(ys_ready, 1)
                v.wait_ge(gsd_ready, n + 1)
                v.reciprocal(RS, RS)
                v.drain()
                for t in range(4):
                    v.scalar_tensor_tensor(MIX[:, 4 + 4 * g + t, :], YS[:, t, :], gain[:, 4 * g + t, :], RS,
                                           ALU.mult, ALU.mult)
            v.drain()

        def window_tensor(pe, l):
            pe.wait_ge(prj_all, l + 1)
            for c in range(2):
                mm = pe.transpose(bank[2][:, c * P:(c + 1) * P], PRJ[:, V0, c * P:(c + 1) * P], ident)
            mm.then_inc(vtk_mm, 1)

            def scores(m0):
                m, par = 4 * l + m0, m0 % 2
                pe.wait_ge(qs_ready, m + 1)
                if m0:
                    pe.wait_ge(sw_max, 2 * m)
                for hh in range(2):
                    q = slice(hh * 64, hh * 64 + 64)
                    for b in range(2):
                        mm = pe.matmul(bank[4 + hh][:, b * T:(b + 1) * T], QS[q, par, b * P:(b + 1) * P], PRJ[q, K0, :],
                                       start=True, stop=True)
                    mm.then_inc(sw_done, 1)

            scores(0)
            for m0 in range(4):
                m, par = 4 * l + m0, m0 % 2
                if m0 < 3:
                    scores(m0 + 1)
                for hh in range(2):
                    pe.wait_ge(sw_p, 2 * m + hh + 1)
                    for k, src in enumerate((0, T, T + P)):
                        mm = pe.transpose(bank[6 + hh][:, k * P:(k + 1) * P], SM[par][:, hh, src:src + P], ident)
                    mm.then_inc(sw_t, 1)
                pe.wait_ge(vtk_ready, l + 1)
                pe.wait_ge(sw_out, m + 1)
                for hh in range(2):
                    q = slice(hh * 64, hh * 64 + 64)
                    pe.wait_ge(sw_tc, 2 * m + hh + 1)
                    pe.matmul(bank[3][q, 0:P], VTK[:, 0, q], PT3[:, hh, 0:P], start=True, stop=True)
                    pe.matmul(bank[3][q, P:2 * P], VTK[:, 0, q], PT3[:, hh, P:2 * P], start=True, stop=False)
                    mm = pe.matmul(bank[3][q, P:2 * P], VTK[:, 1, q], PT3[:, hh, 2 * P:3 * P], start=False, stop=True)
                mm.then_inc(sw_pv, 1)

        def window_scalar(act, l):
            act.wait_ge(lru_done, l + 1)
            act.wait_ge(vtk_mm, l + 1)
            act.activation(VTK, view(bank[2][:, 0:2 * P], 2), ACT.Copy).then_inc(vtk_ready, 1)
            act.activation(QS[:, 0, :], PRJ[:, Q0, :], ACT.Copy).then_inc(qs_ready, 1)
            for m0 in range(4):
                m, par = 4 * l + m0, m0 % 2
                if m0 < 3:
                    act.activation(QS[:, 1 - par, :], PRJ[:, Q0 + m0 + 1, :], ACT.Copy).then_inc(qs_ready, 1)
                sm, st = SM[par], ST[par]
                for hh in range(2):
                    act.wait_ge(sw_max, 2 * m + hh + 1)
                    for b in range(2):
                        act.activation(sm[:, hh, b * T:(b + 1) * T], sm[:, hh, b * T:(b + 1) * T], ACT.Exp,
                                       bias=st[:, 1, 2 * hh + b:2 * hh + b + 1], accum_out=st[:, 2, 2 * hh + b:2 * hh + b + 1])
                    act.activation(st[:, 3, 2 * hh:2 * hh + 2], st[:, 3, 2 * hh:2 * hh + 2], ACT.Exp).then_inc(sw_exp, 1)
                for hh in range(2):
                    act.wait_ge(sw_t, 2 * m + hh + 1)
                    act.activation(PT3[:, hh, :], bank[6 + hh][:, 0:3 * P], ACT.Copy).then_inc(sw_tc, 1)

        def window_vector(v, l):
            sinks = LV[l]["sinks"].rearrange("p (m h) -> p m h", h=2)
            v.drain().then_inc(lru_done, 1)

            def maxima(m0):
                sm, st = SM[m0 % 2], ST[m0 % 2]
                for hh in range(2):
                    c = slice(2 * hh, 2 * hh + 2)
                    v.wait_ge(sw_done, 2 * (4 * l + m0) + hh + 1)
                    v.scalar_tensor_tensor(sm[:, hh, :], bank[4 + hh][:, :], HALF_SCALE, WD["amask"], ALU.mult, ALU.add)
                    v.drain()
                    v.reduce_max(st[:, 0, c], view(sm[:, hh, :], 2), AX_X)
                    v.drain()
                    v.tensor_scalar(st[:, 1, c], st[:, 0, c], sinks[:, m0, hh:hh + 1], -1.0, ALU.max, ALU.mult)
                    v.drain()
                    v.tensor_scalar(st[:, 3, c], st[:, 1, c], sinks[:, m0, hh:hh + 1], None, ALU.add).then_inc(sw_max, 1)

            maxima(0)
            for m0 in range(4):
                m, sm, st = 4 * l + m0, SM[m0 % 2], ST[m0 % 2]
                for hh in range(2):
                    c = slice(2 * hh, 2 * hh + 2)
                    v.wait_ge(sw_exp, 2 * m + hh + 1)
                    v.tensor_tensor(st[:, 2, c], st[:, 2, c], st[:, 3, c], ALU.add)
                    v.drain()
                    v.reciprocal(st[:, 4, c], st[:, 2, c])
                    v.drain()
                    v.tensor_tensor(view(sm[:, hh, :], 2), view(sm[:, hh, :], 2), wide(st[:, 4, c], 2, T),
                                    ALU.mult).then_inc(sw_p, 1)
                if m0 < 3:
                    maxima(m0 + 1)
                v.wait_ge(sw_pv, m + 1)
                v.tensor_copy(MIX[:, 12 + m0, :], bank[3][:, 0:T]).then_inc(sw_out, 1)
            v.drain().then_inc(mix_ready, 1)

        def residual_vector(v, l):
            def add(i, j):
                n = i * RING + j
                b, _ = bank_of(f"out{l}", i, j)
                wait_product(v, f"out{l}", i, j)
                v.scalar_tensor_tensor(tmp[:, n, :], h[:, n, :], ALPHA, bank[b][:, 0:T], ALU.mult,
                                       ALU.add).then_inc(bank_free[b], 1)

            ahead(v, 8, lo_chunk(v, f"out{l}"), add, started=True)

        q8_ready, sc_done, sc_in = sem("q8_ready"), sem("sc_done"), sem("sc_in")
        gate_in, gate_exp = sem("gate_in"), sem("gate_exp")
        ijg_ready, ijt_done, pair_ready = sem("ijg_ready"), sem("ijt_done"), sem("pair_ready")
        hot = sem("hot")
        g_done = sem("g_done")
        g_in = sem("g_in")
        acc_zero = sem("acc_zero")
        u_done = sem("u_done")
        gp_ready = sem("gp_ready")
        G4 = G.rearrange("p j (n t) -> p n t j", t=4)
        GROUPS = T // 4

        def peer_units(e, name, unit, begin=None, middle=None):
            def step(i, j, more):
                n = UNITS * j + 2
                if more:
                    unit(i, j + 1, 0, unit_of(name, i, n), 2)
                if middle:
                    middle(i, j)
                if more:
                    unit(i, j + 1, 1, unit_of(name, i, n + 1), 3)
                    n += 2
                unit(i, j, 2, unit_of(name, i, n), n % UNITS)
                unit(i, j, 3, unit_of(name, i, n + 1), (n + 1) % UNITS)

            for q in range(2):
                unit(0, 0, q, unit_of(name, 0, q), q)
            if begin:
                begin()
            with e.Fori(0, BLOCKS // RING - 1) as i:
                for j in range(RING):
                    step(i, j, True)
            for j in range(RING):
                step(BLOCKS // RING - 1, j, j < RING - 1)

        def peer_tensor(pe, l):
            name = f"peer{l}"
            product3(pe, f"wq{l}", 4, h_hi, h_lo2, T, KT)
            pe.wait_ge(q8_ready, l + 1)
            for f in range(8):
                tt, hp = f // 4, f % 4
                if f >= 4:
                    pe.wait_ge(sc_in, 8 * l + f - 3)
                for a in range(2):
                    mm = pe.matmul(bank[2 + f % 4][:, a * 256:(a + 1) * 256], Q8[:, 2 * hp + a, tt * P:(tt + 1) * P],
                                   WD["keys"], start=True, stop=True)
                mm.then_inc(sc_done, 1)
            pe.wait_ge(ijg_ready, l + 1)
            for tt in range(2):
                for q in range(3):
                    mm = pe.transpose(bank[2 + tt][:, q * P:(q + 1) * P], IJG[:, q, tt * P:(tt + 1) * P], ident)
                mm.then_inc(ijt_done, 1)
            with pe.Fori(0, GROUPS // 2) as i:
                for half in range(2):
                    x = GROUPS * l + 2 * i + half
                    pe.wait_ge(hot, x + 1)
                    pe.wait_ge(g_in, x + 1)
                    for s in range(4):
                        mm = pe.matmul(bank[4 + half][:, s * P:(s + 1) * P], OHA[:, 4 * half + s, :],
                                       OHB[:, 4 * half + s, :], start=True, stop=True)
                    mm.then_inc(g_done, 1)

            def tensor_unit(i, j, q, n, buf):
                if q == 0:
                    b, use = bank_of(name, i, j)
                    pe.wait_ge(bank_free[b], use + 1)
                if q == 2:
                    pe.wait_ge(gp_ready, BLOCKS * l + RING * i + j + 3)
                    if j == 0:
                        pe.wait_ge(acc_zero, l + 1)
                pe.wait_ge(split_lo, n + 1)
                for m in range(4):
                    w = slice(m * P, (m + 1) * P)
                    w_hi, w_lo = SPLIT[:, buf, 0, w], SPLIT[:, buf, 1, w]
                    if q < 2:
                        k = 4 * q + m
                        mm = mm3(pe, bank[bank_of(name, i, j)[0]][:, 0:T], w_hi, w_lo, h_hi[:, k, :], h_lo2[:, k, :],
                                 k == 0, k == KT - 1)
                    else:
                        d = 4 * (q - 2) + m
                        mm = mm3(pe, bank[4 + d // 2][:, (d % 2) * T:(d % 2 + 1) * T], w_hi, w_lo, GPR[:, j % 2, 0, :],
                                 GPR[:, j % 2, 1, :], False, True, skip_group_check=True)
                mm.then_inc(unit_used, 1)

            peer_units(pe, name, tensor_unit)

        def peer_scalar(act, l):
            name = f"peer{l}"

            def drain_q(i, j):
                b, _ = bank_of(f"wq{l}", i, j)
                wait_product(act, f"wq{l}", i, j)
                act.activation(pairs(Q8)[:, j, :], bank[b][:, :], ACT.Copy).then_inc(bank_free[b], 1)

            ahead(act, 4, hi_chunk(act, f"wq{l}"), drain_q)
            act.drain().then_inc(q8_ready, 1)
            for f in range(8):
                act.wait_ge(sc_done, 8 * l + f + 1)
                act.activation(SC[:, 4 * f:4 * f + 4, :], view(bank[2 + f % 4][:, :], 4), ACT.Copy).then_inc(sc_in, 1)
            if l + 1 < DEPTH:
                act.dma_start(wide_t[:], A["wide"][l + 1]).then_inc(wide_in, 16)
            act.wait_ge(gate_in, l + 1)
            act.activation(IJG[:, 0, :], IJG[:, 0, :], ACT.Exp).then_inc(gate_exp, 1)
            for tt in range(2):
                act.wait_ge(ijt_done, 2 * l + tt + 1)
                a = act.activation(PAIR[:, :, tt * P:(tt + 1) * P], view(bank[2 + tt][:, 0:3 * P], 3), ACT.Copy)
            a.then_inc(pair_ready, 1)
            with act.Fori(0, GROUPS // 2) as i:
                for half in range(2):
                    act.wait_ge(g_done, GROUPS * l + 2 * i + half + 3)
                    act.activation(G4[:, 2 * i + half], view(bank[4 + half][:, :], 4), ACT.Copy).then_inc(g_in, 1)

            def gelu(i, j):
                b, _ = bank_of(name, i, j)
                act.wait_ge(unit_used, unit_of(name, i, UNITS * j) + UNITS)
                act.wait_ge(gp_ready, BLOCKS * l + RING * i + j + 2)
                act.activation(GA, bank[b][:, 0:T], ACT.Gelu).then_inc(bank_free[b], 1)

            peer_units(act, name, lambda *a: hi_quarter(act, name, *a),
                       begin=lambda: act.wait_ge(unit_used, unit_of(name, 0, 2) + UNITS), middle=gelu)

        def top16(v, width):
            for a in range(TOP):
                v.max(V16[:, a, 0:8], WK[:, a, 0, 0:width])
            v.drain()
            for a in range(TOP):
                v.max_index(I16[:, a, 0:8], V16[:, a, 0:8], WK[:, a, 0, 0:width])
                v.match_replace(WK[:, a, 1, 0:width], V16[:, a, 0:8], WK[:, a, 0, 0:width], -3.0e38)
            v.drain()
            for a in range(TOP):
                v.max(V16[:, a, 8:16], WK[:, a, 1, 0:width])
            v.drain()
            for a in range(TOP):
                v.max_index(I16[:, a, 8:16], V16[:, a, 8:16], WK[:, a, 1, 0:width])
            v.drain()

        def peer_vector(v, l):
            name = f"peer{l}"
            by_turn = lambda ap: ap.rearrange("p (n a) k -> p n a k", a=TOP)
            work = lo_chunk(v, f"wq{l}")
            for j in range(4):
                work(0, j)
            v.wait_ge(sc_in, 8 * (l + 1))
            with v.Fori(0, 2 * ROWS // TOP) as i:
                v.tensor_copy(WK[:, :, 0, 0:NKEYS], by_turn(SC)[:, i])
                v.drain()
                top16(v, NKEYS)
                v.tensor_copy(by_turn(TV)[:, i], V16)
                v.tensor_copy(by_turn(TIU)[:, i], I16)
            v.drain()
            tv4 = TV.rearrange("p (n a m) k -> p n a m k", a=TOP, m=2)
            with v.Fori(0, NR // TOP) as i:
                for a in range(TOP):
                    v.tensor_tensor(view(WK[:, a, 0, :], TOPK), wide(tv4[:, i, a, 0, :], 2, TOPK),
                                    wide(tv4[:, i, a, 1, :], 1, TOPK), ALU.add)
                v.drain()
                top16(v, TOPK * TOPK)
                v.tensor_copy(by_turn(BV)[:, i], V16)
                v.tensor_copy(by_turn(BPU)[:, i], I16)
            v.drain()
            g0 = view(IJG[:, 0, :], NR)
            v.tensor_tensor(g0, BV, wide(BV[:, :, 0], 2, TOPK), ALU.subtract).then_inc(gate_in, 1)
            bp = BPU.rearrange("p a b -> p (a b)")
            v.tensor_scalar(PAU[:, 0, :], bp, 4, None, ALU.logical_shift_right)
            v.tensor_scalar(PAU[:, 1, :], bp, 15, None, ALU.bitwise_and)
            v.tensor_copy(TIF, TIU)
            v.drain()
            v.tensor_copy(PAF, PAU)
            tif = TIF.rearrange("p (n m) k -> p n m k", m=2)
            eq, eq2 = EQ.rearrange("p n (k a) -> p (n k) a", a=TOPK), EQ2.rearrange("p n (k a) -> p (n k) a", a=TOPK)
            for m in range(2):
                v.drain()
                v.tensor_tensor(eq, wide(PAF[:, m, :], 2, TOPK), wide(iota[:, 0:TOPK], 1, NR * TOPK), ALU.is_equal)
                v.drain()
                v.tensor_tensor(EQ2.rearrange("p n (k a) -> p n k a", a=TOPK), EQ.rearrange("p n (k a) -> p n k a", a=TOPK),
                                wide(tif[:, :, m, :], 2, TOPK), ALU.mult)
                v.drain()
                v.reduce_sum(IJG[:, 1 + m, :], eq2, AX_X)
            v.wait_ge(gate_exp, l + 1)
            v.reduce_sum(MXS[:, 0, :], g0, AX_X)
            v.drain()
            v.reciprocal(MXS[:, 1, :], MXS[:, 0, :])
            v.drain()
            v.tensor_tensor(g0, g0, wide(MXS[:, 1, :], 2, TOPK), ALU.mult)
            v.drain().then_inc(ijg_ready, 1)
            v.wait_ge(pair_ready, l + 1)
            pair = PAIR.rearrange("p q (n t) -> p q n t", t=8).unsqueeze(4)
            with v.Fori(0, GROUPS // 2) as i:
                for half in range(2):
                    v.wait_ge(g_done, GROUPS * l + 2 * i + half + 1)
                    for s in range(4):
                        t = 4 * half + s
                        v.tensor_scalar(OHA[:, t, :], iota, pair[:, 1, i, t, :], pair[:, 0, i, t, :],
                                        ALU.is_equal, ALU.mult)
                        a = v.tensor_scalar(OHB[:, t, :], iota, pair[:, 2, i, t, :], None, ALU.is_equal)
                    a.then_inc(hot, 1)
            v.wait_ge(g_in, GROUPS * (l + 1) + 2)
            for b in range(4, 8):
                a = v.memset(bank[b][:, :], 0.0)
            a.then_inc(acc_zero, 1)

            def gate(i, j):
                b, use = bank_of(name, i, j)
                v.wait_ge(bank_free[b], use + 2)
                v.wait_ge(unit_used, unit_of(name, i, UNITS * j - 2) + UNITS)
                g_hi, g_lo = GPR[:, j % 2, 0, :], GPR[:, j % 2, 1, :]
                v.tensor_tensor(GA, GA, G[:, i * RING + j, :], ALU.mult)
                v.drain()
                v.tensor_copy(g_hi, GA)
                v.drain()
                v.tensor_tensor(g_lo, GA, g_hi.bitcast(F32), ALU.subtract).then_inc(gp_ready, 1)

            peer_units(v, name, lambda i, j, q, n, buf: lo_quarter(v, name, i, j, q, n, buf, q == 3), middle=gate)
            v.wait_ge(unit_used, unit_of(name, 0, UNITS * BLOCKS) + UNITS)
            for b in range(4):
                v.scalar_tensor_tensor(pairs(tmp)[:, b, :], pairs(h_hi)[:, b, :].bitcast(F32), ALPHA, bank[4 + b][:, :],
                                       ALU.mult, ALU.add)
            v.drain()
            for b in range(4):
                v.scalar_tensor_tensor(pairs(tmp)[:, b, :], pairs(h_lo2)[:, b, :].bitcast(F32), ALPHA,
                                       pairs(tmp)[:, b, :], ALU.mult, ALU.add)

        block = ctx.enter_context(nc.Block())

        SETUP = 16 * 6

        @block.sync
        def _(sp):
            for dst, src in ((const_t[:], A["const"]), (vec_t, A["vec"]), (lay_t[0][:], A["lay"][0]),
                             (lay_t[1][:], A["lay"][1]), (hyc_t, A["hyc"]), (X, A["xin"])):
                sp.dma_start(dst, src).then_inc(setup_in, 16)
            sp.dma_start(wide_t[:], A["wide"][0]).then_inc(wide_in, 16)
            stream(sp, "ada", A["w_ada"], 24)
            hyena_sync(sp, A["w_hy"], A["decay"], A["w4"])
            stream(sp, "hy_out", A["w_hyout"], 8)
            stream(sp, "kv", A["w_kv"], 4)
            stream(sp, "q", A["w_q"], 8)
            stream(sp, "z", A["w_z"], 8)
            stream(sp, "at_out", A["w_atout"], 8)
            for l in range(DEPTH):
                stream(sp, f"proj{l}", A[f"w_proj{l}"], 17)
                stream(sp, f"out{l}", A[f"w_out{l}"], 8)
                stream(sp, f"wq{l}", A[f"w_wq{l}"], 4)
                stream(sp, f"peer{l}", A[f"w_peer{l}"], BLOCKS)
            sp.wait_ge(h_new, 2 * DEPTH + 1)
            sp.dma_start(out, h).then_inc(stored, 16)
            sp.wait_ge(stored, 16)

        @block.gpsimd
        def _(pool):
            pool.wait_ge(h_ready, 4)
            pool.dma_start(rope_t, A["rope"]).then_inc(rope_in, 16)

        @block.scalar
        def _(act):
            ada_scalar(act)
            filter_scalar(act)
            sums_scalar(act, 0)
            rms_scalar(act, 0)
            hyena_scalar(act)
            act.wait_ge(yg_done, CT + 1)
            parts_scalar(act, YG, YG_HI)
            hi_rest(act, "hy_out")
            sums_scalar(act, 1)
            rms_scalar(act, 1)
            kv_scalar(act)
            gather(act, "q", pairs(QR), ACT.Copy, 8, started=True)
            hi_chunk(act, "z")(0, 0)
            prep_scalar(act)
            gather(act, "z", pairs(ZG), ACT.Silu, 8, started=True)
            heads_scalar(act)
            hi_chunk(act, "at_out")(0, 0)
            act.wait_ge(og_done, HEADS + 2)
            parts_scalar(act, OG, OG_HI)
            hi_rest(act, "at_out")
            norm_scalar(act, 0, PRJ[:, 0:8, :])
            for l in range(DEPTH):
                proj_scalar(act, l)
                lru_scalar(act, l)
                rows_scalar(act, l)
                ssm_scalar(act, l)
                window_scalar(act, l)
                hi_chunk(act, f"out{l}")(0, 0)
                act.wait_ge(mix_ready, l + 1)
                parts_scalar(act, MIX, MIX_HI)
                hi_rest(act, f"out{l}")
                norm_scalar(act, 2 * l + 1, tmp)
                peer_scalar(act, l)
                norm_scalar(act, 2 * l + 2, tmp)

        @block.vector
        def _(v):
            filter_vector(v)
            ada_vector(v)
            rms_vector(v, 0)
            hyena_vector(v)
            parts_vector(v, YG, YG_HI, YG_LO, 0)
            add_gated(v, "hy_out", 0, 2)
            sums_vector(v, 1)
            rms_vector(v, 1)
            prep_vector(v)
            heads_vector(v)
            lo_chunk(v, "at_out")(0, 0)
            parts_vector(v, OG, OG_HI, OG_LO, UNITS)
            add_gated(v, "at_out", 1, 1)
            norm_vector(v, 0, X[:, :, 0:T], PRJ[:, 0:8, :], V1["emb_g"], V1["emb_b"], h, (h_hi, h_lo1))
            v.sem_inc(ys_ready, 1)
            v.sem_inc(sw_out, 1)
            v.sem_inc(gp_ready, 2)
            for l in range(DEPTH):
                lru_vector(v, l)
                rows_vector(v, l)
                ssm_vector(v, l)
                window_vector(v, l)
                lo_chunk(v, f"out{l}")(0, 0)
                parts_vector(v, MIX, MIX_HI, MIX_LO, (2 + l) * UNITS)
                residual_vector(v, l)
                norm_vector(v, 2 * l + 1, tmp, tmp, LV[l]["ln1_g"], LV[l]["ln1_b"], h, (h_hi, h_lo2))
                peer_vector(v, l)
                norm_vector(v, 2 * l + 2, tmp, tmp, LV[l]["ln2_g"], LV[l]["ln2_b"], h,
                            (h_hi, h_lo1) if l < DEPTH - 1 else None)

        @block.tensor
        def _(pe):
            for s in chunk_done:
                pe.sem_inc(s, 1)
            for s in bank_free:
                pe.sem_inc(s, 1)
            pe.sem_inc(unit_used, UNITS)
            filter_tensor(pe)
            sums_tensor(pe, 0)
            ada_tensor(pe)
            pe.wait_ge(h_ready, 2)
            hyena_tensor(pe)
            product3(pe, "hy_out", 8, YG_HI, YG_LO, T2, 16, parts=0)
            sums_tensor(pe, 1)
            pe.wait_ge(h_ready, 4)
            kv_tensor(pe)
            product3(pe, "q", 8, H1_HI[:, :, 0:T], H1_LO[:, :, 0:T], T, KT)
            prep_tensor(pe)
            product3(pe, "z", 8, H1_HI[:, :, 0:T], H1_LO[:, :, 0:T], T, KT)
            turn_tensor(pe)
            heads_tensor(pe)
            product3(pe, "at_out", 8, OG_HI, OG_LO, T, 16, parts=UNITS)
            norm_tensor(pe, 0, X)
            pe.sem_inc(rg_act, 2)
            pe.sem_inc(g_done, 2)
            pe.sem_inc(g_in, 2)
            for l in range(DEPTH):
                proj_tensor(pe, l)
                lru_tensor(pe, l)
                rows_tensor(pe, l)
                ssm_tensor(pe, l)
                window_tensor(pe, l)
                product3(pe, f"out{l}", 8, MIX_HI, MIX_LO, T, 16, parts=(2 + l) * UNITS)
                norm_tensor(pe, 2 * l + 1, tmp)
                peer_tensor(pe, l)
                norm_tensor(pe, 2 * l + 2, tmp)


def tiles(w, order, kt):
    k, n = w.shape
    t = w.reshape(kt, P, n // P, P).transpose(2, 1, 0, 3)[list(order)].reshape(len(order), P, kt * P)
    per = CHUNK // (kt * P)
    return np.ascontiguousarray(t.reshape(-1, per, P, kt * P).transpose(0, 2, 1, 3).reshape(-1, P, CHUNK))


def cols(v):
    return np.asarray(v).reshape(-1, P).T


def rows_to(a, rows=P):
    a = np.asarray(a)
    return np.concatenate([a, np.zeros((rows - a.shape[0],) + a.shape[1:], a.dtype)], 0) if a.shape[0] < rows else a


def constants():
    f = np.float32
    s = np.arange(P)
    q, k = np.arange(P)[:, None], np.arange(T)[None, :]
    block0 = (k <= q)
    block1 = np.where(k < P, k > q, k - P <= q)
    amask = np.where(np.stack([block0, block1], 1), 0.0, -1e30).astype(f)
    const = np.concatenate([np.eye(P), np.ones((P, P)), np.tile(s, (P, 1)), (s[:, None] <= s[None, :]),
                            np.full((P, 1), 1e-6), np.full((P, 1), 1e-5)], 1).astype(f)
    t, fr = np.arange(T)[:, None], np.arange(T)[None, :]
    ang = 2 * np.pi * ((t * fr) % T2) / T2
    alt = (-1.0) ** np.arange(T)
    re, sn = np.cos(ang), -np.sin(ang)
    im = sn.copy()
    im[:, 0] = alt
    rex = re[:, 0:P].copy()
    rex[:, 0] = alt
    ire = np.cos(ang).T * (2.0 / T2)
    ire[0] /= 2
    iim = -np.sin(ang).T * (2.0 / T2)
    iim[0] = alt / T2
    split = lambda m: m.reshape(2, P, -1).transpose(1, 0, 2).reshape(P, -1)
    lin = np.linspace(0.0, 1.0, T, dtype=f)[:, None]
    wv = (f(2 * np.pi) * np.arange(T, dtype=f)[:, None] / f(T)).astype(f)
    bands = np.linspace(1e-4, 15, 16, dtype=f)[None, :]
    arg = (bands * wv).astype(f)
    z = np.concatenate([lin, np.cos(arg), -np.sin(arg)], 1).astype(f).T
    hyc = np.concatenate([split(re), split(im), split(sn), split(rex), split(ire), split(iim), rows_to(z)], 1).astype(f)
    lo, hi = np.log(1e-2) / 1.5, np.log(1e-2) / 0.3
    deltas = np.abs(np.linspace(lo, hi, E_HY, dtype=f))
    dec = np.exp(-lin * deltas[None, :]).astype(f)
    back = dec.copy()
    back[0] = 0
    d = np.stack([dec, back], 1).reshape(2, P, 2, CT, P).transpose(3, 1, 0, 2, 4).reshape(CT, P, 512)
    inv = (1.0 / (10000.0 ** (np.arange(0, 64, 2, dtype=f) / f(64)))).astype(f)
    row, col = (np.arange(T) // 64).astype(f), (np.arange(T) % 64).astype(f)
    angle = np.concatenate([row[:, None] * inv, row[:, None] * inv, col[:, None] * inv, col[:, None] * inv], 1)
    rot = np.zeros((P, P))
    for base in (0, 64):
        for c in range(32):
            rot[base + c + 32, base + c] = -1
            rot[base + c, base + c + 32] = 1
    rope = np.concatenate([np.cos(angle.astype(f)).T, np.sin(angle.astype(f)).T, rot], 1).astype(f)
    return const, amask.reshape(P, -1), hyc, np.ascontiguousarray(d.astype(f)), rope


def layout(a):
    f = np.float32
    one = lambda v: rows_to(np.asarray(v).reshape(-1, 1))
    const, amask, hyc, decay, rope = constants()
    x = np.concatenate([a["x"][0].T.reshape(KT, P, T), a["ctx"][0].T.reshape(KT, P, T)], 2).transpose(1, 0, 2)
    inner = CT
    conv_w = a["hy_conv_w"][0].reshape(3, 3, CT, P)[:, [1, 2, 0]]
    conv_b = a["hy_conv_b"][0].reshape(3, CT, P)[[1, 2, 0]]
    vec = np.concatenate([
        np.stack([cols(a["c"][0]), cols(a["c_ctx"])], 2).reshape(P, 16),
        np.concatenate([cols(a["norm_g"][l]) for l in range(2)], 1),
        np.concatenate([cols(a["ada_b"][l]) for l in range(2)], 1),
        conv_w.transpose(3, 2, 1, 0).reshape(P, 144), conv_b.transpose(2, 1, 0).reshape(P, 48),
        cols(a["hy_d"][0]), one(a["at_q_g"][0]), one(a["at_k_g"][0]),
        one(a["hy_fb1"][0]), one(a["hy_fb2"][0]), one(a["hy_fb3"][0]), one(a["hy_freq"][0]),
        cols(a["emb_ln_g_2"]), cols(a["emb_ln_b_2"]),
        rows_to(a["hy_fw1"][0]), rows_to(a["hy_fw2"][0]), rows_to(a["hy_fw3"][0])], 1)
    lay, wide = [], []
    for l in range(DEPTH):
        wax = np.zeros((2, LRU_T, P, P), f)
        for m, name in enumerate(("rg_wa_2", "rg_wx_2")):
            for b in range(8):
                o = 64 * (b % 2)
                wax[m, b // 2, o:o + 64, o:o + 64] = a[name][l, b]
        keys = np.zeros((P, 256), f)
        keys[0:64, 0:P] = a["peer_keys_2"][l, 0].T
        keys[64:P, P:] = a["peer_keys_2"][l, 1].T
        lay.append(np.concatenate([
            a["rg_conv_w_2"][l].reshape(4, LRU_T, P).transpose(2, 1, 0).reshape(P, 16), cols(a["rg_conv_b_2"][l]),
            cols(a["rg_ba_2"][l]), cols(a["rg_bx_2"][l]), cols(a["rg_lambda_2"][l]),
            a["ssm_conv_w_2"][l].reshape(4, XBC_T, P).transpose(2, 1, 0).reshape(P, 48), cols(a["ssm_conv_b_2"][l]),
            one(a["ssm_dt_bias_2"][l]), one(a["ssm_a_log_2"][l]), cols(np.repeat(a["ssm_d_2"][l], 64)),
            cols(a["ssm_norm_g_2"][l]), cols(a["ln1_g_2"][l]), cols(a["ln1_b_2"][l]), cols(a["ln2_g_2"][l]),
            cols(a["ln2_b_2"][l]), np.tile(a["attn_sinks_2"][l][[0, 4, 1, 5, 2, 6, 3, 7]][None], (P, 1))], 1))
        wide.append(np.concatenate([
            a["w_in_2"][l][:, 3584:3600].reshape(KT, P, 16).transpose(1, 0, 2).reshape(P, 128), keys,
            wax.transpose(2, 0, 1, 3).reshape(P, 1024), amask], 1))
    hy = [t for c in range(CT) for t in (CT + c, 2 * CT + c, c, 3 * CT + c)]
    w4 = a["hy_fw4"][0].reshape(64, 2, CT, P).transpose(2, 0, 1, 3).reshape(CT, 64, 256)
    at = a["at_w_in"][0]
    arrays = {
        "const": const, "vec": vec, "lay": np.stack(lay), "wide": np.stack(wide), "hyc": hyc, "decay": decay, "rope": rope, "w4": w4, "xin": x,
        "w_ada": a["ada_w"].reshape(2, KT, P, 12, 256).transpose(0, 3, 2, 1, 4).reshape(24, P, CHUNK),
        "w_hy": tiles(a["hy_w_in"][0], hy, KT), "w_hyout": tiles(a["hy_w_out"][0], range(8), 16),
        "w_kv": tiles(at, [t for g in range(4) for t in (16 + g, 20 + g)], KT),
        "w_q": tiles(at, range(16), KT), "w_z": tiles(at, range(24, 40), KT),
        "w_atout": tiles(a["at_w_out"][0], range(8), 16),
    }
    for l in range(DEPTH):
        w = a["w_in_2"][l]
        heads = [hd for m in range(4) for hd in (m, m + 4)]
        wq = w[:, 3600:4112].reshape(D, 8, 64)[:, heads].reshape(D, 512)
        wcat = np.concatenate([w[:, 0:512], w[:, 2048:3584], wq, w[:, 4112:4368], w[:, 512:2048]], 1)
        arrays[f"w_proj{l}"] = tiles(wcat, range(34), KT)
        wo = a["w_out_2"][l]
        wo = np.concatenate([wo[0:1536], wo[1536:].reshape(8, 64, D)[heads].reshape(512, D)], 0)
        arrays[f"w_out{l}"] = tiles(wo, range(8), 16)
        arrays[f"w_wq{l}"] = tiles(a["peer_wq_2"][l], range(8), KT)
        u = a["peer_u_2"][l].reshape(P, BLOCKS, KT, P).transpose(1, 3, 2, 0).reshape(BLOCKS, P, D)
        v = a["peer_v_2"][l].reshape(P, BLOCKS, D).transpose(1, 0, 2)
        arrays[f"w_peer{l}"] = np.concatenate([u, v], 2)
    return {k: np.ascontiguousarray(v) for k, v in arrays.items()}


def kernel(**inputs):
    import concourse.bacc as bacc
    from concourse.bass_utils import run_bass_kernel_spmd

    arrays = layout({k: np.asarray(v) for k, v in inputs.items()})
    nc = bacc.Bacc("TRN2", target_bir_lowering=False, num_devices=1)
    handles = {k: nc.dram_tensor(f"in_{k}", v.shape, F32, kind="ExternalInput").ap() for k, v in arrays.items()}
    out = nc.dram_tensor("out_h", (P, KT, T), F32, kind="ExternalOutput").ap()
    program(nc, handles, out)
    r = run_bass_kernel_spmd(nc, [{f"in_{k}": v for k, v in arrays.items()}], core_ids=[0])
    return r.results[0]["out_h"].transpose(2, 1, 0).reshape(1, T, D)
```
